# Optimizing a Trainium2 kernel written in Bass

```python
import math
import jax
import jax.numpy as jnp
from jax import lax
import numpy as np
import jax, jax.numpy as jnp

D_MODEL = 1024
BATCH = 1
SEQ = 512
DEPTH = 1

ATTN_HEADS = 8
KV_HEADS = 2
HEAD_DIM = 64
Q_PER_KV = ATTN_HEADS // KV_HEADS
ATTN_WIDTH = ATTN_HEADS * HEAD_DIM
KV_WIDTH = KV_HEADS * HEAD_DIM
SSM_WIDTH = D_MODEL - ATTN_WIDTH
SSM_GROUP = 16
SSM_GROUPS = SSM_WIDTH // SSM_GROUP
SSM_STATE = 64
CMP_BLOCK = 32
CMP_STRIDE = 16
CMP_HIDDEN = 256
SEL_BLOCK = 64
SEL_TOPN = 16
WINDOW = 512
Q_BLOCK = 128
FORCE_SCORE = 1.0e4
ROPE_THETA = 10000.0
FFN_DIM = 2816
CONV_WIDTH = 3
NORM_EPS = 1e-6
IN_WIDTH = ATTN_WIDTH + 6 * KV_WIDTH + 3 * ATTN_HEADS + SSM_WIDTH


def rmsnorm(x, g):
    xf = x.astype(jnp.float32)
    y = xf * lax.rsqrt(jnp.mean(xf * xf, axis=-1, keepdims=True) + NORM_EPS)
    return (y * g.astype(jnp.float32)).astype(x.dtype)

def rope(x, pos):
    half = HEAD_DIM // 2
    inv = jnp.power(ROPE_THETA, -jnp.arange(half, dtype=jnp.float32) * 2.0 / HEAD_DIM)
    ang = pos.astype(jnp.float32)[:, None] * inv[None, :]
    cos = jnp.cos(ang)[None, :, None, :]
    sin = jnp.sin(ang)[None, :, None, :]
    xf = x.astype(jnp.float32)
    x1, x2 = xf[..., :half], xf[..., half:]
    return jnp.concatenate([x1 * cos - x2 * sin, x1 * sin + x2 * cos], axis=-1).astype(x.dtype)

def masked_softmax(s, mask):
    s = jnp.where(mask, s.astype(jnp.float32), -jnp.inf)
    m = jnp.max(s, axis=-1, keepdims=True)
    m = jnp.where(jnp.isfinite(m), m, 0.0)
    e = jnp.where(mask, jnp.exp(s - m), 0.0)
    return e / jnp.maximum(jnp.sum(e, axis=-1, keepdims=True), 1e-30)

def compress_blocks(kv, pe, w1, w2):
    b, l = kv.shape[0], kv.shape[1]
    n_cmp = (l - CMP_BLOCK) // CMP_STRIDE + 1
    idx = jnp.arange(n_cmp)[:, None] * CMP_STRIDE + jnp.arange(CMP_BLOCK)[None, :]
    blocks = kv[:, idx] + pe[None, None, :, None, :]
    flat = blocks.transpose(0, 1, 3, 2, 4).reshape(b, n_cmp, KV_HEADS, CMP_BLOCK * HEAD_DIM)
    out = jax.nn.gelu(flat @ w1) @ w2
    return out.transpose(0, 2, 1, 3)

def nsa_attention(q, k_c, v_c, k_s, v_s, k_w, v_w, gates, pe_k, pe_v, w_ck1, w_ck2, w_cv1, w_cv2):
    b, l = q.shape[0], q.shape[1]
    pos = jnp.arange(l)
    q = rope(q, pos)
    k_c = rope(k_c, pos)
    k_s = rope(k_s, pos)
    k_w = rope(k_w, pos)
    kc = compress_blocks(k_c, pe_k, w_ck1, w_ck2)
    vc = compress_blocks(v_c, pe_v, w_cv1, w_cv2)
    n_cmp = kc.shape[2]
    c_start = jnp.arange(n_cmp) * CMP_STRIDE
    c_end = c_start + CMP_BLOCK - 1
    n_sel = l // SEL_BLOCK
    top_n = min(SEL_TOPN, n_sel)
    s_start = jnp.arange(n_sel) * SEL_BLOCK
    overlap = jnp.clip(
        jnp.minimum(c_start[:, None] + CMP_BLOCK, s_start[None, :] + SEL_BLOCK)
        - jnp.maximum(c_start[:, None], s_start[None, :]), 0, None).astype(jnp.float32) / CMP_BLOCK
    ks_blk = k_s.reshape(b, n_sel, SEL_BLOCK, KV_HEADS, HEAD_DIM).transpose(0, 3, 1, 2, 4)
    vs_blk = v_s.reshape(b, n_sel, SEL_BLOCK, KV_HEADS, HEAD_DIM).transpose(0, 3, 1, 2, 4)
    pad = ((0, 0), (WINDOW, 0), (0, 0), (0, 0))
    kw_pad = jnp.pad(k_w, pad).transpose(0, 2, 1, 3)
    vw_pad = jnp.pad(v_w, pad).transpose(0, 2, 1, 3)
    n_blk = l // Q_BLOCK
    q_blk = q.reshape(b, n_blk, Q_BLOCK, KV_HEADS, Q_PER_KV, HEAD_DIM).transpose(1, 0, 3, 4, 2, 5)
    scale = HEAD_DIM ** -0.5
    b_idx = jnp.arange(b)[:, None, None, None]
    h_idx = jnp.arange(KV_HEADS)[None, :, None, None]
    sel_ids = jnp.arange(n_sel)
    win_off = jnp.arange(WINDOW + Q_BLOCK) - WINDOW
    sub = jnp.arange(SEL_BLOCK)

    def attend_block(args):
        qi, i = args
        t = i * Q_BLOCK + jnp.arange(Q_BLOCK)
        s_c = jnp.einsum('bhgqd,bhnd->bhgqn', qi, kc) * scale
        p_c = masked_softmax(s_c, c_end[None, :] <= t[:, None])
        o_c = jnp.einsum('bhgqn,bhnd->bhgqd', p_c.astype(vc.dtype), vc)
        imp = jnp.einsum('bhgqn,ns->bhqs', p_c, overlap)
        cur = (t // SEL_BLOCK)[:, None]
        forced = (sel_ids == 0) | (sel_ids == cur) | (sel_ids == cur - 1)
        score = jnp.where(sel_ids > cur, -jnp.inf, jnp.where(forced, FORCE_SCORE, imp))
        top_s, top_i = lax.top_k(score, top_n)
        k_g = ks_blk[b_idx, h_idx, top_i].reshape(b, KV_HEADS, Q_BLOCK, top_n * SEL_BLOCK, HEAD_DIM)
        v_g = vs_blk[b_idx, h_idx, top_i].reshape(b, KV_HEADS, Q_BLOCK, top_n * SEL_BLOCK, HEAD_DIM)
        key_pos = (top_i[..., None] * SEL_BLOCK + sub).reshape(b, KV_HEADS, Q_BLOCK, top_n * SEL_BLOCK)
        valid = jnp.repeat(jnp.isfinite(top_s), SEL_BLOCK, axis=-1) & (key_pos <= t[:, None])
        s_s = jnp.einsum('bhgqd,bhqkd->bhgqk', qi, k_g) * scale
        p_s = masked_softmax(s_s, valid[:, :, None])
        o_s = jnp.einsum('bhgqk,bhqkd->bhgqd', p_s.astype(v_g.dtype), v_g)
        k_wi = lax.dynamic_slice_in_dim(kw_pad, i * Q_BLOCK, WINDOW + Q_BLOCK, axis=2)
        v_wi = lax.dynamic_slice_in_dim(vw_pad, i * Q_BLOCK, WINDOW + Q_BLOCK, axis=2)
        w_pos = i * Q_BLOCK + win_off
        m_w = (w_pos[None, :] <= t[:, None]) & (w_pos[None, :] > t[:, None] - WINDOW) & (w_pos[None, :] >= 0)
        s_w = jnp.einsum('bhgqd,bhkd->bhgqk', qi, k_wi) * scale
        p_w = masked_softmax(s_w, m_w)
        o_w = jnp.einsum('bhgqk,bhkd->bhgqd', p_w.astype(v_wi.dtype), v_wi)
        return o_c, o_s, o_w

    o_c, o_s, o_w = lax.map(attend_block, (q_blk, jnp.arange(n_blk)))

    def unblock(o):
        return o.transpose(1, 0, 4, 2, 3, 5).reshape(b, l, ATTN_HEADS, HEAD_DIM)

    out = (gates[..., 0:1] * unblock(o_c) + gates[..., 1:2] * unblock(o_s)
           + gates[..., 2:3] * unblock(o_w))
    return out.reshape(b, l, ATTN_WIDTH)

def s5_mixer(u, lam_re, lam_im, log_step, b_re, b_im, c_re, c_im, d_skip, w_glu, b_glu):
    b, l, _ = u.shape
    uf = u.astype(jnp.float32).reshape(b, l, SSM_GROUPS, SSM_GROUP)
    step = jnp.exp(log_step.astype(jnp.float32))[:, None]
    lr = lam_re.astype(jnp.float32)
    li = lam_im.astype(jnp.float32)
    mag = jnp.exp(lr * step)
    a_re = mag * jnp.cos(li * step)
    a_im = mag * jnp.sin(li * step)
    den = lr * lr + li * li
    n_re = a_re - 1.0
    f_re = (n_re * lr + a_im * li) / den
    f_im = (a_im * lr - n_re * li) / den
    br = b_re.astype(jnp.float32)
    bi = b_im.astype(jnp.float32)
    bb_re = f_re[..., None] * br - f_im[..., None] * bi
    bb_im = f_re[..., None] * bi + f_im[..., None] * br
    bu_re = jnp.einsum('blgc,gpc->blgp', uf, bb_re)
    bu_im = jnp.einsum('blgc,gpc->blgp', uf, bb_im)
    a_re_t = jnp.broadcast_to(a_re, bu_re.shape)
    a_im_t = jnp.broadcast_to(a_im, bu_re.shape)

    def combine(e1, e2):
        a1r, a1i, b1r, b1i = e1
        a2r, a2i, b2r, b2i = e2
        return (a2r * a1r - a2i * a1i, a2r * a1i + a2i * a1r,
                a2r * b1r - a2i * b1i + b2r, a2r * b1i + a2i * b1r + b2i)

    _, _, x_re, x_im = lax.associative_scan(combine, (a_re_t, a_im_t, bu_re, bu_im), axis=1)
    y = (jnp.einsum('blgp,gcp->blgc', x_re, c_re.astype(jnp.float32))
         - jnp.einsum('blgp,gcp->blgc', x_im, c_im.astype(jnp.float32))
         + d_skip.astype(jnp.float32) * uf)
    y = jax.nn.gelu(y.reshape(b, l, SSM_WIDTH))
    y = y * jax.nn.sigmoid(y @ w_glu.astype(jnp.float32) + b_glu.astype(jnp.float32))
    return y.astype(u.dtype)

def causal_dwconv(u, w, bias):
    ch = u.shape[-1]
    y = lax.conv_general_dilated(u, w[:, None, :].astype(u.dtype), window_strides=(1,),
                                 padding=[(CONV_WIDTH - 1, 0)],
                                 dimension_numbers=('NWC', 'WIO', 'NWC'),
                                 feature_group_count=ch)
    return y + bias

def split_heads(t, n_heads):
    return t.reshape(t.shape[0], t.shape[1], n_heads, HEAD_DIM)

def first_inputs(seed: int = 0) -> dict:
    key = jax.random.key(seed)
    ks = jax.random.split(key, 32)
    f32 = jnp.float32

    def nrm(k, shape, s):
        return jax.random.normal(k, shape, f32) * s

    D, F, NL = D_MODEL, FFN_DIM, DEPTH
    G, P, C = SSM_GROUPS, SSM_STATE, SSM_GROUP
    return {
        "x": nrm(ks[0], (BATCH, SEQ, D), 1.0),
        "c": nrm(ks[1], (BATCH, D), 1.0),
        "norm1_g": 1.0 + nrm(ks[2], (NL, D), 0.02),
        "norm2_g": 1.0 + nrm(ks[3], (NL, D), 0.02),
        "normf_g": 1.0 + nrm(ks[4], (D,), 0.02),
        "w_ada": nrm(ks[5], (NL, D, 6 * D), D ** -0.5),
        "b_ada": nrm(ks[6], (NL, 6 * D), 0.01),
        "w_in": nrm(ks[7], (NL, D, IN_WIDTH), D ** -0.5),
        "pe_k": nrm(ks[8], (NL, CMP_BLOCK, HEAD_DIM), 0.02),
        "pe_v": nrm(ks[9], (NL, CMP_BLOCK, HEAD_DIM), 0.02),
        "w_ck1": nrm(ks[10], (NL, CMP_BLOCK * HEAD_DIM, CMP_HIDDEN), (CMP_BLOCK * HEAD_DIM) ** -0.5),
        "w_ck2": nrm(ks[11], (NL, CMP_HIDDEN, HEAD_DIM), CMP_HIDDEN ** -0.5),
        "w_cv1": nrm(ks[12], (NL, CMP_BLOCK * HEAD_DIM, CMP_HIDDEN), (CMP_BLOCK * HEAD_DIM) ** -0.5),
        "w_cv2": nrm(ks[13], (NL, CMP_HIDDEN, HEAD_DIM), CMP_HIDDEN ** -0.5),
        "lam_re": -0.5 + nrm(ks[14], (NL, G, P), 0.01),
        "lam_im": math.pi * jnp.arange(P, dtype=f32) + nrm(ks[15], (NL, G, P), 0.01),
        "log_step": jax.random.uniform(ks[16], (NL, G), f32, math.log(1e-3), math.log(1e-1)),
        "b_re": nrm(ks[17], (NL, G, P, C), (2 * C) ** -0.5),
        "b_im": nrm(ks[18], (NL, G, P, C), (2 * C) ** -0.5),
        "c_re": nrm(ks[19], (NL, G, C, P), P ** -0.5),
        "c_im": nrm(ks[20], (NL, G, C, P), P ** -0.5),
        "d_skip": nrm(ks[21], (NL, G, C), 1.0),
        "w_glu": nrm(ks[22], (NL, SSM_WIDTH, SSM_WIDTH), SSM_WIDTH ** -0.5),
        "b_glu": nrm(ks[23], (NL, SSM_WIDTH), 0.01),
        "attn_norm_g": 1.0 + nrm(ks[24], (NL, ATTN_WIDTH), 0.02),
        "ssm_norm_g": 1.0 + nrm(ks[25], (NL, SSM_WIDTH), 0.02),
        "w_o": nrm(ks[26], (NL, D, D), D ** -0.5),
        "w_up": nrm(ks[27], (NL, D, 2 * F), D ** -0.5),
        "conv_w": nrm(ks[28], (NL, CONV_WIDTH, 2 * F), CONV_WIDTH ** -0.5),
        "conv_b": nrm(ks[29], (NL, 2 * F), 0.01),
        "w_down": nrm(ks[30], (NL, F, D), F ** -0.5),
    }

def first_block(x, c, norm1_g, norm2_g, normf_g, w_ada, b_ada, w_in, pe_k, pe_v, w_ck1, w_ck2,
              w_cv1, w_cv2, lam_re, lam_im, log_step, b_re, b_im, c_re, c_im, d_skip, w_glu,
              b_glu, attn_norm_g, ssm_norm_g, w_o, w_up, conv_w, conv_b, w_down):
    b, l, _ = x.shape
    sizes = [ATTN_WIDTH] + [KV_WIDTH] * 6 + [3 * ATTN_HEADS]
    cuts = [int(v) for v in np.cumsum(sizes)]
    for li in range(DEPTH):
        mod = (jax.nn.silu(c) @ w_ada[li] + b_ada[li])[:, None, :]
        sh1, sc1, gt1, sh2, sc2, gt2 = jnp.split(mod, 6, axis=-1)
        h = rmsnorm(x, norm1_g[li]) * (1.0 + sc1) + sh1
        z = h @ w_in[li]
        zq, zkc, zvc, zks, zvs, zkw, zvw, zg, zs = jnp.split(z, cuts, axis=-1)
        gates = jax.nn.sigmoid(zg.reshape(b, l, ATTN_HEADS, 3))
        o_attn = nsa_attention(split_heads(zq, ATTN_HEADS), split_heads(zkc, KV_HEADS),
                               split_heads(zvc, KV_HEADS), split_heads(zks, KV_HEADS),
                               split_heads(zvs, KV_HEADS), split_heads(zkw, KV_HEADS),
                               split_heads(zvw, KV_HEADS), gates, pe_k[li], pe_v[li],
                               w_ck1[li], w_ck2[li], w_cv1[li], w_cv2[li])
        y_ssm = s5_mixer(zs, lam_re[li], lam_im[li], log_step[li], b_re[li], b_im[li],
                         c_re[li], c_im[li], d_skip[li], w_glu[li], b_glu[li])
        mix = jnp.concatenate([rmsnorm(o_attn, attn_norm_g[li]), rmsnorm(y_ssm, ssm_norm_g[li])], axis=-1)
        x = x + gt1 * (mix @ w_o[li])
        h = rmsnorm(x, norm2_g[li]) * (1.0 + sc2) + sh2
        u = causal_dwconv(h @ w_up[li], conv_w[li], conv_b[li])
        a, v = jnp.split(u, 2, axis=-1)
        x = x + gt2 * ((jax.nn.silu(a) * v) @ w_down[li])
    return rmsnorm(x, normf_g)


_first_inputs = first_inputs


def first_inputs(seed=0):
    import zlib

    import numpy as np

    out = dict(_first_inputs(seed))
    spreads = {}
    factors = {'norm1_g': 5.08,
     'norm2_g': 4.992,
     'normf_g': 2.884,
     'b_ada': 3.462,
     'pe_k': 8.0,
     'pe_v': 8.0,
     'lam_re': 8.0,
     'b_glu': 8.0,
     'attn_norm_g': 7.477,
     'ssm_norm_g': 7.226,
     'conv_b': 8.0}
    for name, (base, spread) in spreads.items():
        noise = np.random.default_rng([zlib.crc32(name.encode()), seed]).standard_normal(out[name].shape)
        drawn = base * np.exp(spread * noise) if base else spread * noise
        out[name] = jnp.asarray(drawn.astype(out[name].dtype))
    for name, factor in factors.items():
        out[name] = (out[name] * factor).astype(out[name].dtype)
    return out


_narrow_inputs = first_inputs


def first_inputs(seed=0):
    out = dict(_narrow_inputs(seed))
    wider = {'normf_g': 3.27,
     'pe_v': 5.74,
     'lam_re': 12.0,
     'b_glu': 4.26,
     'attn_norm_g': 3.36,
     'ssm_norm_g': 3.33,
     'conv_b': 3.36}
    for name, times in wider.items():
        mean = out[name].mean()
        out[name] = (mean + times * (out[name] - mean)).astype(out[name].dtype)
    return out


DEPTH_2 = 2

N_MIXERS = 2
CONV_EXPAND = 2
CONV_WIDTH_2 = D_MODEL * CONV_EXPAND
CONV_K = 3
HEADS_PER_GROUP = D_MODEL // HEAD_DIM
DILATED_GROUPS = ((128, 1), (512, 4), (2048, 16))
N_GROUPS = len(DILATED_GROUPS)
ATTN_WIDTH_2 = HEADS_PER_GROUP * HEAD_DIM
QKV_COLS = N_GROUPS * 3 * ATTN_WIDTH_2
BLOCK = 128
N_BUCKETS = 32
MAX_DISTANCE = 2048
EPS = 1e-6
N_CONV_LAYERS = (DEPTH_2 + 1) // 2
N_ATTN_LAYERS = DEPTH_2 // 2


def rms_norm(x, g):
    xf = x.astype(jnp.float32)
    y = xf * lax.rsqrt(jnp.mean(xf * xf, axis=-1, keepdims=True) + EPS)
    return (y * g.astype(jnp.float32)).astype(x.dtype)

def t5_bucket(dist):
    max_exact = N_BUCKETS // 2
    d = jnp.maximum(dist, 1).astype(jnp.float32)
    large = max_exact + (jnp.log(d / max_exact) / math.log(MAX_DISTANCE / max_exact)
                         * (N_BUCKETS - max_exact)).astype(jnp.int32)
    large = jnp.minimum(large, N_BUCKETS - 1)
    return jnp.where(dist < max_exact, dist, large)

def short_conv_mixer(h, w_in, w_conv, w_out):
    S = h.shape[1]
    proj = h @ w_in
    b_gate, c_gate, u, z = jnp.split(proj, 4, axis=-1)
    v = c_gate * u
    vp = jnp.pad(v, ((0, 0), (CONV_K - 1, 0), (0, 0)))
    conv = sum(w_conv[k] * vp[:, k:k + S] for k in range(CONV_K))
    y = b_gate * conv * jax.nn.silu(z)
    return y @ w_out

def dilated_group_attention(q, k, v, bias_tab, window, dilation):
    B, S, H, Dh = q.shape
    L = S // dilation
    nb = -(-L // BLOCK)
    Lp = nb * BLOCK
    span = window // dilation

    def to_sub(t):
        t = t.reshape(B, L, dilation, H, Dh).transpose(0, 2, 3, 1, 4)
        t = jnp.pad(t, ((0, 0), (0, 0), (0, 0), (0, Lp - L), (0, 0)))
        return t.reshape(B, dilation, H, nb, BLOCK, Dh)

    def band(t):
        prev = jnp.pad(t, ((0, 0), (0, 0), (0, 0), (1, 0), (0, 0), (0, 0)))[:, :, :, :-1]
        return jnp.concatenate([prev, t], axis=4)

    qs = to_sub(q)
    kb = band(to_sub(k))
    vb = band(to_sub(v))
    logits = jnp.einsum('brhnqd,brhnkd->brhnqk', qs, kb).astype(jnp.float32) * (HEAD_DIM ** -0.5)

    a = jnp.arange(BLOCK)[:, None]
    kk = jnp.arange(2 * BLOCK)[None, :]
    step = BLOCK + a - kk
    blk = jnp.arange(nb)[:, None, None]
    key_pos = (blk - 1) * BLOCK + kk[None]
    valid = (step >= 0) & (step <= span) & (key_pos >= 0)
    bucket = t5_bucket(jnp.clip(step, 0, span) * dilation)
    bias = bias_tab.astype(jnp.float32)[bucket].transpose(2, 0, 1)[:, None]

    logits = jnp.where(valid, logits + bias, -jnp.inf)
    lse = jax.nn.logsumexp(logits, axis=-1)
    probs = jnp.exp(logits - lse[..., None])
    out = jnp.einsum('brhnqk,brhnkd->brhnqd', probs.astype(v.dtype), vb)

    out = out.reshape(B, dilation, H, Lp, Dh)[:, :, :, :L]
    out = out.transpose(0, 3, 1, 2, 4).reshape(B, S, H, Dh)
    lse = lse.reshape(B, dilation, H, Lp)[:, :, :, :L]
    lse = lse.transpose(0, 3, 1, 2).reshape(B, S, H)
    return out, lse

def dilated_attention_mixer(h, w_in, q_gain, k_gain, w_out, rel_bias):
    B, S, _ = h.shape
    proj = h @ w_in
    qkv = proj[..., :QKV_COLS].reshape(B, S, N_GROUPS, 3, HEADS_PER_GROUP, HEAD_DIM)
    z = proj[..., QKV_COLS:]
    outs, lses = [], []
    for g, (window, dilation) in enumerate(DILATED_GROUPS):
        q = rms_norm(qkv[:, :, g, 0], q_gain[g])
        k = rms_norm(qkv[:, :, g, 1], k_gain[g])
        bias_g = rel_bias[:, g * HEADS_PER_GROUP:(g + 1) * HEADS_PER_GROUP]
        o, l = dilated_group_attention(q, k, qkv[:, :, g, 2], bias_g, window, dilation)
        outs.append(o)
        lses.append(l)
    alpha = jax.nn.softmax(jnp.stack(lses, axis=0), axis=0)
    o = jnp.sum(alpha[..., None] * jnp.stack(outs, axis=0).astype(jnp.float32), axis=0)
    y = o.reshape(B, S, ATTN_WIDTH_2).astype(h.dtype) * jax.nn.silu(z)
    return y @ w_out

def second_inputs(seed: int = 0) -> dict:
    key = jax.random.key(seed)
    ks = jax.random.split(key, 12)
    f32 = jnp.float32
    nc, na = N_CONV_LAYERS, N_ATTN_LAYERS
    x = jax.random.normal(ks[0], (BATCH, SEQ, D_MODEL), f32)
    conv_norm = 1.0 + 0.1 * jax.random.normal(ks[1], (nc, D_MODEL), f32)
    conv_w_in = jax.random.normal(ks[2], (nc, D_MODEL, 4 * CONV_WIDTH_2), f32) * D_MODEL ** -0.5
    conv_w = jax.random.normal(ks[3], (nc, CONV_K, CONV_WIDTH_2), f32) * CONV_K ** -0.5
    conv_w_out = jax.random.normal(ks[4], (nc, CONV_WIDTH_2, D_MODEL), f32) * CONV_WIDTH_2 ** -0.5
    attn_norm = 1.0 + 0.1 * jax.random.normal(ks[5], (na, D_MODEL), f32)
    attn_w_in = jax.random.normal(ks[6], (na, D_MODEL, QKV_COLS + ATTN_WIDTH_2), f32) * D_MODEL ** -0.5
    attn_q_gain = 1.0 + 0.1 * jax.random.normal(ks[7], (na, N_GROUPS, HEAD_DIM), f32)
    attn_k_gain = 1.0 + 0.1 * jax.random.normal(ks[8], (na, N_GROUPS, HEAD_DIM), f32)
    attn_w_out = jax.random.normal(ks[9], (na, ATTN_WIDTH_2, D_MODEL), f32) * ATTN_WIDTH_2 ** -0.5
    rel_bias = 0.5 * jax.random.normal(ks[10], (N_BUCKETS, N_GROUPS * HEADS_PER_GROUP), f32)
    return {"x": x, "conv_norm": conv_norm, "conv_w_in": conv_w_in, "conv_w": conv_w,
            "conv_w_out": conv_w_out, "attn_norm": attn_norm, "attn_w_in": attn_w_in,
            "attn_q_gain": attn_q_gain, "attn_k_gain": attn_k_gain, "attn_w_out": attn_w_out,
            "rel_bias": rel_bias}

def second_block(x, conv_norm, conv_w_in, conv_w, conv_w_out, attn_norm, attn_w_in,
              attn_q_gain, attn_k_gain, attn_w_out, rel_bias):
    for i in range(DEPTH_2):
        j = i // N_MIXERS
        if i % N_MIXERS == 0:
            h = rms_norm(x, conv_norm[j])
            x = x + short_conv_mixer(h, conv_w_in[j], conv_w[j], conv_w_out[j])
        else:
            h = rms_norm(x, attn_norm[j])
            x = x + dilated_attention_mixer(h, attn_w_in[j], attn_q_gain[j], attn_k_gain[j],
                                            attn_w_out[j], rel_bias)
    return x


def setup_inputs(seed=0):
    out = dict(first_inputs(seed))
    for name, value in second_inputs(seed + 1).items():
        if name != "x":
            out[name + "_2"] = value
    return out


def reference(
    x, c, norm1_g, norm2_g, normf_g, w_ada, b_ada, w_in, pe_k, pe_v, w_ck1, w_ck2, w_cv1, w_cv2,
    lam_re, lam_im, log_step, b_re, b_im, c_re, c_im, d_skip, w_glu, b_glu, attn_norm_g,
    ssm_norm_g, w_o, w_up, conv_w, conv_b, w_down, conv_norm_2, conv_w_in_2, conv_w_2,
    conv_w_out_2, attn_norm_2, attn_w_in_2, attn_q_gain_2, attn_k_gain_2, attn_w_out_2,
    rel_bias_2,
):
    x = first_block(
        x, c, norm1_g, norm2_g, normf_g, w_ada, b_ada, w_in, pe_k, pe_v, w_ck1, w_ck2, w_cv1,
        w_cv2, lam_re, lam_im, log_step, b_re, b_im, c_re, c_im, d_skip, w_glu, b_glu,
        attn_norm_g, ssm_norm_g, w_o, w_up, conv_w, conv_b, w_down,
    )
    return second_block(
        x, conv_norm_2, conv_w_in_2, conv_w_2, conv_w_out_2, attn_norm_2, attn_w_in_2,
        attn_q_gain_2, attn_k_gain_2, attn_w_out_2, rel_bias_2,
    )


_drawn_inputs = setup_inputs


def setup_inputs(seed=0):
    import zlib

    import numpy as np

    out = dict(_drawn_inputs(seed))
    spreads = {}
    factors = {'lam_re': 6.098,
     'attn_norm_2': 7.107,
     'attn_q_gain_2': 8.0,
     'attn_k_gain_2': 8.0,
     'rel_bias_2': 4.01}
    for name, (base, spread) in spreads.items():
        noise = np.random.default_rng([zlib.crc32(name.encode()), seed]).standard_normal(out[name].shape)
        drawn = base * np.exp(spread * noise) if base else spread * noise
        out[name] = jnp.asarray(drawn.astype(out[name].dtype))
    for name, factor in factors.items():
        out[name] = (out[name] * factor).astype(out[name].dtype)
    return out
```

```python
from contextlib import ExitStack

import numpy as np

import concourse.bass as bass
from concourse import mybir

P = 128
D = 1024
L = 512
KD = D // P
TT = L // P
HD = 64
NEG = -1.0e30
NCMP = (L - 32) // 16 + 1
FT = 2816 // P
CT = 2048 // P
NPAIR = 8
CH = 2048

T_ZS, T_KC, T_VC, T_Q, T_KS, T_VS, T_KW, T_VW, T_ZG = 0, 4, 5, 6, 10, 11, 12, 13, 14

N_IN, N_GLU, N_O, N_UP, N_DOWN, N_CIN, N_COUT, N_AIN, N_AOUT, N_ALL = 0, 8, 9, 13, 35, 51, 83, 91, 131, 135
PAIR_STEPS = 6 + 1 + 2 + 4 + 4
NB_DOWN = FT // 2

O_IN, O_GLU, O_O, O_UP, O_DOWN, O_CIN, O_COUT, O_AIN, O_AOUT = 0, 16, 20, 28, 72, 80, 144, 152, 232

F32 = mybir.dt.float32
F32R = mybir.dt.float32r
ACT = mybir.ActivationFunctionType
ALU = mybir.AluOpType
AX = mybir.AxisListType
PI = float(np.pi)

GROUPS = ((128, 1), (512, 4), (2048, 16))
VLEN = (384, 256, 64)
VOFF = (0, 384, 640)
VTOT = 704


class Count:

    def __init__(self, sem):
        self.sem, self.n, self.turns = sem, 0, 0

    def inc(self, ins):
        ins.then_inc(self.sem, 1)
        self.n += 1

    def wait(self, eng):
        eng.wait_ge(self.sem, self.n + self.turns)

    def loop(self, i, per):
        self.turns, self.per, self.start = i * per, per, self.n

    def leave(self, trips):
        assert self.n == self.start + self.per, (self.n - self.start, self.per)
        self.turns, self.n = 0, self.start + self.per * trips


def done_after(n, r=0):
    if n < 7:
        return 2 * n + 2 + 2 * r
    if n < N_O:
        return 15 if n == 7 else 19
    if n < N_DOWN:
        return 21 + 2 * (n - N_O + r)
    if n < N_CIN:
        return O_DOWN + (n - N_DOWN) // 2 + r // 2
    if n < N_COUT:
        return O_CIN + 1 + 2 * (n - N_CIN + r)
    if n < N_AIN:
        return O_COUT + n - N_COUT + r
    return O_AIN + 1 + 2 * (n - N_AIN + r)


def emptied(t, half=0):
    return t // 2 - (1 if t % 2 and t > 15 else 0) + half


def unit_slots(u):
    if u < 2:
        return [(0, u, i, 2 * i if i else 1, 2 if i else 1) for i in range(TT)]
    return [(u - 1, h, i, 4 * h + i, 1) for h in range(2) for i in range(TT)]


def build(nc, A, out):
    es = ExitStack()
    with es:
        def sem(name):
            return es.enter_context(nc.semaphore(name))

        def sb(scope, name, shape, dt=F32):
            return scope.enter_context(nc.sbuf_tensor(name, shape, dt))

        bank = [es.enter_context(nc.psum_tensor(f"bank{i}", [P, 512], F32)) for i in range(8)]

        x = sb(es, "x", [P, KD, L])
        raw = sb(es, "raw", [P, 2, CH])
        w_hi = sb(es, "w_hi", [P, 2, CH], F32R)
        w_lo = sb(es, "w_lo", [P, 2, CH], F32R)
        sq = sb(es, "sq", [P, 2, L])
        hf = sb(es, "hf", [P, 2, L])
        std = sb(es, "std", [P, L])
        ones = sb(es, "ones", [P, P])
        ident = sb(es, "ident", [P, P])
        cols = sb(es, "cols", [P, 64])
        eps = cols[:, 0:1]
        gains = sb(es, "gains", [P, 56])
        mod = sb(es, "mod", [P, 48])
        b_ada = sb(es, "b_ada", [P, 48])
        conv_wb = sb(es, "conv_wb", [P, 4, 2 * FT])
        conv2_w = sb(es, "conv2_w", [P, 3, CT])
        qk_gain = sb(es, "qk_gain", [P, 6])

        early = ExitStack()
        s_sb = sb(early, "s_sb", [P, 1088])
        pt_s = sb(early, "pt_s", [P, 512])
        pt_w = sb(early, "pt_w", [P, 512])
        pt_c = sb(early, "pt_c", [P, P])
        hid = sb(early, "hid", [P, 2, 2, 62])
        kc_t = sb(early, "kc_t", [P, 62])
        vc_t = sb(early, "vc_t", [P, 2, HD])
        gates = sb(early, "gates", [P, TT, 24])
        early.close()
        h_hi = sb(es, "h_hi", [P, KD, L], F32R)
        h_lo = sb(es, "h_lo", [P, KD, L], F32R)

        sa = ExitStack()
        z = sb(sa, "z", [P, 15, L])
        r32 = sb(sa, "r32", [P, 2, KD * P])
        e_tab = sb(sa, "e_tab", [P, 2, 2, L])
        pool_t = sb(sa, "pool_t", [P, L])
        over = ExitStack()
        y_hi = sb(over, "y_hi", [P, 4, L], F32R)
        y_lo = sb(over, "y_lo", [P, 4, L], F32R)
        over.close()
        pq = sb(sa, "pq", [P, 8, L])
        scr8 = sb(sa, "scr8", [P, 2048])
        v_tok = sb(sa, "v_tok", [P, 2, TT, P])
        b_s5 = sb(sa, "b_s5", [P, 2, 4, P])
        c_s5 = sb(sa, "c_s5", [P, 3, 16, 32])
        b_tab = sb(sa, "b_tab", [P, 2, 16, 32])
        a_tab = sb(sa, "a_tab", [P, 2, 16, 16])
        s5c = sb(sa, "s5c", [P, 21, 16])
        mask = sb(sa, "mask", [P, 512])
        cmask = sb(sa, "cmask", [P, TT, NCMP])
        pe_t = sb(sa, "pe_t", [P, 2, 32])
        w_c2 = sb(sa, "w_c2", [P, 2, P])
        w_v2 = sb(sa, "w_v2", [P, 2, HD])
        small = sb(sa, "small", [P, 64])
        cs = sb(sa, "cs", [P, 2, KD])
        sa.close()

        onehot = z[0:32, 0:2].rearrange("p a b -> p (a b)")[:, 0:VTOT]
        vmask = z[0:16, 2:4].rearrange("p a b -> p (a b)")[:, 0:VTOT]
        vec = z[0:16, 6:8].rearrange("p a b -> p (a b)")[:, 0:VTOT]
        tabs = z[0:32, 4, 0:48]

        sf = ExitStack()
        act_hi = sb(sf, "act_hi", [P, FT, L], F32R)
        act_lo = sb(sf, "act_lo", [P, FT, L], F32R)
        up_av = sb(sf, "up_av", [P, 2, L])
        cv_av = sb(sf, "cv_av", [P, 2, L])
        sf.close()

        sc_ = ExitStack()
        yc_hi = sb(sc_, "yc_hi", [P, CT, L], F32R)
        yc_lo = sb(sc_, "yc_lo", [P, CT, L], F32R)
        cg = sb(sc_, "cg", [P, L])
        cu = sb(sc_, "cu", [P, L + 2])
        cacc = sb(sc_, "cacc", [P, L])
        csil = sb(sc_, "csil", [P, L])
        sc_.close()

        sd = ExitStack()
        qk = sb(sd, "qk", [P, 2, 6, L])
        vv = sb(sd, "vv", [P, 2, 3 * TT, 3, HD])
        zg = sb(sd, "zg", [P, 2, L])
        bias = sb(sd, "bias", [P, 2, 512])
        rawd = sb(sd, "rawd", [P, 2, L])
        rden = sb(sd, "rden", [P, L])
        sd_sb = sb(sd, "sd_sb", [P, 4, 1024])
        yatt = sb(sd, "yatt", [P, NPAIR, L])
        perm_f = sb(sd, "perm_f", [P, 2, 4, P])
        perm_b = sb(sd, "perm_b", [P, 2, 4, P])
        head_ones = sb(sd, "head_ones", [P, P])[:, :]
        sd.close()

        cw = conv_wb[:, :, :].rearrange("p a b -> p (a b)")
        spread = cw[:, 0:64].rearrange("p (g r i h) -> p g r i h", g=2, r=4, i=4)
        stat = cw[:, 64:88].rearrange("p (g i h) -> p g i h", g=3, i=4)
        mnat = cw[:, 88:96].rearrange("p (i h) -> p i h", i=4)
        mperm = cw[:, 96:112].rearrange("p (g r h) -> p g r h", g=2, r=4)
        pmask = cw[:, 112:120].rearrange("p (g i) -> p g i", g=2)
        stdd = (std[:, :], hf[:, 1])

        vec_dram = nc.dram_tensor("bias_vectors", (16, VTOT), F32, kind="Internal")
        bias_dram = nc.dram_tensor("bias_tiles", (16, P, 512), F32, kind="Internal")

        vec_in, vec_done, vec_ready, vec_out = sem("vec_in"), sem("vec_done"), sem("vec_ready"), sem("vec_out")
        bias_made, bias_in = sem("bias_made"), sem("bias_in")
        perm_in = sem("perm_in")
        dve_held = sem("dve_held")
        half_used = sem("half_used")
        conv_done, silu_done, af_ready, ah_ready = sem("conv_done"), sem("silu_done"), sem("af_ready"), sem("ah_ready")
        al_ready = sem("al_ready")
        xf_ready = sem("xf_ready")
        cu_zero = sem("cu_zero")
        yc_ready, ych_ready, ycl_ready = sem("yc_ready"), sem("ych_ready"), sem("ycl_ready")
        d_sq, d_sum, d_std, d_qk = sem("d_sq"), sem("d_sum"), sem("d_std"), sem("d_qk")
        d_scores, d_max, d_spread, d_natural, d_min, d_back, d_mperm = (
            sem("d_scores"), sem("d_max"), sem("d_spread"), sem("d_natural"), sem("d_min"), sem("d_back"),
            sem("d_mperm"))
        d_exp, d_turned, d_pt, d_pv = sem("d_exp"), sem("d_turned"), sem("d_pt"), sem("d_pv")
        d_vturned, d_vset, d_y, d_ones = sem("d_vturned"), sem("d_vset"), sem("d_y"), sem("d_ones")
        raw_in = [sem("raw_in0"), sem("raw_in1")]
        hi_done, lo_done = sem("hi_done"), sem("lo_done")
        r32_in = [sem("r32_in0"), sem("r32_in1")]
        r32_used = sem("r32_used")
        x_in, c_in_s = sem("x_in"), sem("c_in_s")
        gains_in, s5_in, attn_in = sem("gains_in"), sem("s5_in"), sem("attn_in")
        ones_in = sem("ones_in")
        eps_set = sem("eps_set")
        cs_ready = sem("cs_ready")
        sq_ready, sq_used, sums_done = sem("sq_ready"), sem("sq_used"), sem("sums_done")
        std_ready, rstd_ready = sem("std_ready"), sem("rstd_ready")
        mod_done, mod_ready = sem("mod_done"), sem("mod_ready")
        hf_ready, hh_ready, hl_ready = sem("hf_ready"), sem("hh_ready"), sem("hl_ready")
        proj_done = sem("proj_done")
        evac = [sem("evac0"), sem("evac1")]
        prep_done, prep_taken = sem("prep_done"), [sem("prep_taken0"), sem("prep_taken1")]
        dve_step, act_step, pool_step = sem("dve_step"), sem("act_step"), sem("pool_step")
        s5_act, s5_need, s5_tabs = sem("s5_act"), sem("s5_need"), sem("s5_tabs")
        e_ready, bu_done, bu_taken = sem("e_ready"), sem("bu_done"), sem("bu_taken")
        back_done, cmul_done, y_ready, yg_ready = sem("back_done"), sem("cmul_done"), sem("y_ready"), sem("yg_ready")
        yh_ready, yl_ready, glu_ready, mixed = sem("yh_ready"), sem("yl_ready"), sem("glu_ready"), sem("mixed")
        roped, blocks_ready, hid_ready = sem("roped"), sem("blocks_ready"), sem("hid_ready")
        gates_ready = sem("gates_ready")
        scores_done, max_ready, exp_done = sem("scores_done"), sem("max_ready"), sem("exp_done")
        turned, turned_c, pt_dve, pt_act, pv_done, combined = (
            sem("turned"), sem("turned_c"), sem("pt_dve"), sem("pt_act"), sem("pv_done"), sem("combined"))
        osq, ostd, onorm, oturned = sem("osq"), sem("ostd"), sem("onorm"), sem("oturned")
        otaken = sem("otaken")
        out_sent = sem("out_sent")

        G = {n: gains[:, 8 * i:8 * i + 8] for i, n in enumerate(("n1", "n2", "nf", "conv", "attn2", "mix"))}
        BGLU, DSKIP = gains[:, 48:52], gains[:, 52:56]
        GS1, GS2 = cols[:, 8:16], cols[:, 16:24]
        SH1, SC1, GT1, SH2, SC2, GT2 = (mod[:, 8 * i:8 * i + 8] for i in range(6))
        (LR, LI, STEP, MAG, TH, TK, SIN, COS, ARE, AIM, DEN, NRE, FRE, FIM, T0, T1, PC, PS, PC2, PS2,
         TC) = (s5c[:, i] for i in range(21))

        B_SUM, B_MISC, B_PREP = 2, 3, (2, 7)
        B_BU, B_Y = (4, 5), 6
        MODC = bank[B_MISC][:, 0:48]
        SC = bank[B_MISC][:, 48:48 + NCMP]
        TC31 = bank[B_MISC][0:NCMP, 128:256]
        PV = bank[B_MISC][:, 256:448]

        o_tok = scr8[:, :].rearrange("p (t f) -> p t f", t=TT)
        rope_cs = pq[:, 0:2]
        ropem = pq[:, 2:4].rearrange("p a b -> p (a b)")[:, 0:5 * P].rearrange("p (m f) -> p m f", m=5)
        cosT, sinT = rope_cs[:, 0], rope_cs[:, 1]
        s5t = scr8[:, 0:768].rearrange("p (a b c) -> p a b c", a=3, b=16)
        c_in = scr8[:, 768:1280].rearrange("p (a b c) -> p a b c", a=2, b=16)
        blk = scr8[:, 0:1984].rearrange("p (v k n) -> p v k n", v=2, k=16)

        def products(pe, b, wh, wl, xh, xl, nk, first=True, last=True, k0=0, ready=None):
            for n in range(nk):
                k = (k0 + n) % nk
                if ready is not None:
                    pe.wait_ge(hl_ready, ready + n + 1)
                pe.matmul(bank[b][:, :], wh(k), xh(k), start=first and n == 0, stop=False)
                pe.matmul(bank[b][:, :], wh(k), xl(k), start=False, stop=False)
                mm = pe.matmul(bank[b][:, :], wl(k), xh(k), start=False, stop=last and n == nk - 1)
            return mm

        def hblock(s, nk, m):
            return (lambda k: w_hi[:, s, (m * nk + k) * P:(m * nk + k + 1) * P],
                    lambda k: w_lo[:, s, (m * nk + k) * P:(m * nk + k + 1) * P])

        hx = (lambda k: h_hi[:, k], lambda k: h_lo[:, k])

        NORMS = {"n1": (0, 0, 0), "ssm": (8, 1, 8), "n2": (12, 2, 16), "nf": (20, 3, None), "conv": (28, 4, 24),
                 "attn2": (36, 5, 32)}

        block = es.enter_context(nc.Block())

        @block.sync
        def _(sp):
            sp.dma_start(cs[:, 0], A["c"]).then_inc(c_in_s, 16)

            def load32(r, s=None, i=None):
                if r >= 2:
                    sp.wait_ge(r32_used, r - 1)
                sp.dma_start(r32[:, r % 2], A["w32"][r]).then_inc(r32_in[r % 2], 16)

            def load(n):
                if n >= 2:
                    sp.wait_ge(lo_done, n - 1)
                sp.dma_start(raw[:, n % 2], A["w_a"][n]).then_inc(raw_in[n % 2], 16)

            load32(0)
            load32(1)
            sp.dma_start(ones[:, :], A["ones"]).then_inc(ones_in, 16)
            sp.dma_start(x[:, :, :], A["x"]).then_inc(x_in, 16)
            sp.dma_start(onehot, A["onehot"]).then_inc(vec_in, 16)
            sp.dma_start(vmask, A["vmask"]).then_inc(vec_in, 16)
            sp.dma_start(tabs, A["tabs"]).then_inc(vec_in, 16)
            sp.dma_start(gains[:, :], A["gains"]).then_inc(gains_in, 16)
            sp.dma_start(b_ada[:, :], A["b_ada"]).then_inc(gains_in, 16)
            for r in range(2, 16):
                load32(r)
                if r == 8:
                    load(0)
                if r == 10:
                    load(1)
            sp.dma_start(s5c[:, 0:3], A["s5c"]).then_inc(s5_in, 16)
            sp.dma_start(b_s5[:, :, :, :], A["b_s5"]).then_inc(s5_in, 16)
            sp.dma_start(c_in[:, :, :, :], A["c_s5"]).then_inc(s5_in, 16)
            sp.wait_ge(vec_ready, 2)
            sp.dma_start(vec_dram.ap(), vec).then_inc(vec_out, 16)
            for dst, name in ((ident[:, :], "ident"), (ropem[:, :, :], "ropem"), (rope_cs[:, :, :], "rope_cs"),
                              (mask[:, :], "mask"), (cmask[:, :, :], "cmask"), (pe_t[:, :, :], "pe_t"),
                              (w_c2[:, :, :], "w_c2"), (w_v2[:, :, :], "w_v2"),
                              (conv_wb[:, :, :], "conv_wb"), (conv2_w[:, :, :], "conv2_w"),
                              (qk_gain[:, :], "qk_gain")):
                sp.dma_start(dst, A[name]).then_inc(attn_in, 16)
            for n in range(2, 8):
                load(n)
            load32(16)
            load32(17)
            load(8)
            load(9)
            for r in range(18, 56):
                load32(r)
            sp.dma_start(bias_dram.ap()[:, :, 384:512].rearrange("h a k -> a h k"),
                         bass.AP(A["neg"].tensor, 0, [[P, P], [0, 16], [1, P]])).then_inc(vec_out, 16)
            sp.wait_ge(vec_out, 32)
            for off, c0, w in ((127, 0, 256), (VOFF[1] + 127, 256, 128)):
                sp.dma_start(bias_dram.ap()[:, :, c0:c0 + w],
                             bass.AP(vec_dram, off, [[VTOT, 16], [-1, P], [1, w]])).then_inc(bias_made, 16)
            for j in range(4):
                sp.dma_start(bias_dram.ap()[:, 32 * j:32 * j + 32, 384 + 32 * j:416 + 32 * j],
                             bass.AP(vec_dram, VOFF[2] + 31, [[VTOT, 16], [-1, 32], [1, 32]])).then_inc(bias_made, 16)
            for n in range(10, N_UP):
                load(n)

            def load_in(n, i, src, w=CH):
                sp.wait_ge(lo_done, 2 * i + (n - 1))
                sp.dma_start(raw[:, n % 2, 0:w], src).then_inc(raw_in[n % 2], 16)

            with sp.Fori(0, (N_DOWN - N_UP) // 2) as i:
                for j in range(2):
                    load_in(N_UP + j, i, A["w_a"][bass.ds(2 * i + (N_UP + j), 1)].rearrange("a p k -> (a p) k"))
            with sp.Fori(0, (N_CIN - N_DOWN) // 2) as i:
                for j in range(2):
                    load_in(N_DOWN + j, i, A["w_d"][bass.ds(2 * i + j, 1)].rearrange("a p k -> (a p) k"),
                            NB_DOWN * P)
            with sp.Fori(0, (N_AIN - N_CIN) // 2) as i:
                for j in range(2):
                    load_in(N_CIN + j, i, A["w_b"][bass.ds(2 * i + j, 1)].rearrange("a p k -> (a p) k"))
            sp.wait_ge(proj_done, done_after(N_AIN - 1))
            for dst, name in ((perm_f[:, :, :, :], "perm_f"), (perm_b[:, :, :, :], "perm_b"),
                              (pmask, "pmask"), (head_ones, "head_ones")):
                sp.dma_start(dst, A[name]).then_inc(perm_in, 16)
            sp.wait_ge(bias_made, 16 * 6)

            def load_bias(c, r):
                if c:
                    sp.wait_ge(d_max, 4 * r + 4 * c)
                sp.dma_start(bias[:, :, :], bias_dram.ap()[bass.ds(2 * r + 2 * c, 2)].rearrange("h a k -> a h k"))\
                  .then_inc(bias_in, 16)

            load_bias(0, 0)
            for n in range(N_AIN, N_AIN + 5):
                load_in(n, 0, A["w_b"][n - N_CIN])
            with sp.Fori(0, 3) as i:
                for j in range(10):
                    n = N_AIN + 5 + j
                    sp.wait_ge(lo_done, 10 * i + (n - 1))
                    sp.dma_start(raw[:, n % 2], A["w_b"][bass.ds(10 * i + (n - N_CIN), 1)].rearrange("a p k -> (a p) k"))\
                      .then_inc(raw_in[n % 2], 16)
                    if j % 5 == 3:
                        load_bias(1 + j // 5, 2 * i)
            for n in range(N_AIN + 35, N_ALL):
                load_in(n, 0, A["w_b"][n - N_CIN])
                if n == N_AIN + 38:
                    load_bias(7, 0)
            for k in range(KD):
                sp.wait_ge(evac[k % 2], emptied(O_AOUT + k) + 1)
                sp.dma_start(out[:, k], x[:, k]).then_inc(out_sent, 16)
            sp.wait_ge(out_sent, 16 * KD)

        @block.scalar
        def _(act):
            def hi(n, r=0):
                if n >= N_ALL:
                    return
                act.wait_ge(raw_in[n % 2], 8 * r + 16 * (n // 2 + 1))
                o = n - 2
                if N_DOWN <= o < N_CIN and (o - N_DOWN) % 2 == 0:
                    act.wait_ge(half_used, r // 2 + (o - N_DOWN) // 2 + 1)
                elif o >= 0:
                    act.wait_ge(proj_done, done_after(o, r))
                act.activation(w_hi[:, n % 2], raw[:, n % 2], ACT.Copy).then_inc(hi_done, 1)

            def squares(name, src, nk, ready=None):
                q0 = NORMS[name][0]
                for k in range(nk):
                    if ready:
                        ready(k)
                    if q0 + k >= 2:
                        act.wait_ge(sq_used, q0 + k - 1)
                    act.activation(sq[:, (q0 + k) % 2], src(k), ACT.Square).then_inc(sq_ready, 1)

            def root(name, width):
                m = NORMS[name][1]
                act.activation(cols[:, 24 + m:25 + m], eps, ACT.Sqrt)
                act.wait_ge(sums_done, m + 1)
                if m:
                    act.wait_ge(rstd_ready, m)
                act.activation(std[:, :], bank[B_SUM][:, :], ACT.Sqrt, bias=eps,
                               scale=1.0 / width).then_inc(std_ready, 1)

            def high_h(g, k, shift=None):
                act.wait_ge(hf_ready, g + 1)
                if shift is None:
                    ins = act.activation(h_hi[:, k], hf[:, g % 2], ACT.Copy)
                else:
                    ins = act.activation(h_hi[:, k], hf[:, g % 2], ACT.Identity, bias=shift[:, k:k + 1])
                ins.then_inc(hh_ready, 1)

            def highs(name, shift=None):
                for k in range(KD):
                    high_h(NORMS[name][2] + k, k, shift)

            act.wait_ge(c_in_s, 16)
            act.activation(cs[:, 1], cs[:, 0], ACT.Silu).then_inc(cs_ready, 1)
            act.wait_ge(x_in, 16)
            squares("n1", lambda k: x[:, k], KD)
            act.wait_ge(eps_set, 1)
            root("n1", D)
            hi(0)
            hi(1)
            highs("n1", SH1)
            for t in range(15):
                act.wait_ge(proj_done, t + 1)
                if t == 6:
                    act.wait_ge(vec_out, 16)
                act.activation(z[:, t], bank[t % 2][:, :], ACT.Copy).then_inc(evac[t % 2], 1)
                if t % 2 or t == 14:
                    hi(t // 2 + 2)
                if t == 0:
                    act.wait_ge(s5_in, 48)
                    act.activation(STEP, STEP, ACT.Exp).then_inc(s5_act, 1)
                if t == 1:
                    act.wait_ge(s5_need, 1)
                    act.activation(MAG, T0, ACT.Exp).then_inc(s5_act, 1)
                if t == 3:
                    act.wait_ge(s5_need, 2)
                    act.activation(SIN, TH, ACT.Sin).then_inc(s5_act, 1)
                    act.activation(COS, TC, ACT.Sin).then_inc(s5_act, 1)
            act.wait_ge(prep_done, 4)
            act.activation(gates[:, :, :], bank[7][:, :].rearrange("p (t f) -> p t f", t=TT)[:, :, 0:24],
                           ACT.Sigmoid).then_inc(prep_taken[1], 1)
            for s in range(2):
                act.wait_ge(prep_done, 17 + s)
                act.activation(hid[:, s], bank[B_PREP[s]][:, 0:124].rearrange("p (h n) -> p h n", h=2),
                               ACT.Gelu_apprx_tanh).then_inc(prep_taken[s], 1)

            for u in range(33):
                if u:
                    kw = P * ((u - 1) // 8 + 1)
                    act.wait_ge(turned, u)
                    if u >= 2:
                        act.wait_ge(pv_done, u - 1)
                    act.activation(pt_w[:, 0:kw], bank[7][:, 0:kw], ACT.Copy).then_inc(pt_act, 1)
                    act.wait_ge(turned_c, u)
                    act.activation(pt_c[0:NCMP, :], TC31, ACT.Copy).then_inc(pt_act, 1)
                if u < 32:
                    i = u // 8
                    kw = P * (i + 1)
                    den = small[:, 8 * (u % 2):8 * (u % 2) + 3]
                    nmx = small[:, 8 * (u % 2) + 4:8 * (u % 2) + 7]
                    act.wait_ge(max_ready, 3 * u + 3)
                    if u >= 2:
                        act.wait_ge(combined, u - 1)
                    for b, (c0, w) in enumerate(((1024 + 32 * (u % 2), NCMP), (0, kw), (512, kw))):
                        act.activation(s_sb[:, c0:c0 + w], s_sb[:, c0:c0 + w], ACT.Exp, bias=nmx[:, b:b + 1],
                                       scale=-1.0, accum_out=den[:, b:b + 1]).then_inc(exp_done, 1)
                if u >= 8 and u % 8 == 0:
                    zt = u // 8 - 1
                    act.wait_ge(y_ready, zt + 1)
                    act.activation(z[:, zt], z[:, zt], ACT.Gelu_apprx_tanh).then_inc(yg_ready, 1)
            for m in range(4):
                act.wait_ge(yg_ready, m + 1)
                act.wait_ge(cmul_done, 16)
                act.activation(y_hi[:, m], z[:, m], ACT.Copy).then_inc(yh_ready, 1)
            for i in range(TT):
                act.wait_ge(combined, 8 * i + 8)
                if i:
                    act.wait_ge(osq, i)
                act.activation(sq[:, 0], o_tok[:, i], ACT.Square, accum_out=small[:, 16 + i:17 + i]).then_inc(osq, 1)
            act.wait_ge(osq, 4)
            act.activation(small[:, 20:24], small[:, 16:20], ACT.Sqrt, bias=eps, scale=1.0 / 512).then_inc(ostd, 1)
            for m in range(4):
                t = O_GLU + m
                act.wait_ge(proj_done, t)
                act.activation(pool_t[:, :] if m % 2 else e_tab[:, 0, 0], bank[t % 2][:, :], ACT.Sigmoid,
                               bias=BGLU[:, m:m + 1]).then_inc(evac[t % 2], 1)
                if m >= 0:
                    act.wait_ge(mixed, m + 1)
            hi(10)
            squares("ssm", lambda k: z[:, k], 4)
            root("ssm", 512)
            for m in range(4):
                high_h(8 + m, 4 + m)
            for m in range(4):
                high_h(12 + m, m)
            for n in range(N_O, N_UP):
                act.wait_ge(proj_done, done_after(n))
                hi(n + 2)

            def rehigh(name, ready):
                squares(name, lambda k: x[:, k], KD, ready)
                root(name, D)

            def x_ready(o):
                return lambda k: act.wait_ge(evac[k % 2], emptied(o + k) + 1)

            rehigh("n2", x_ready(O_O))
            highs("n2", SH2)
            with act.Fori(0, FT // 2) as i:
                for j in range(2):
                    n, t = N_UP + j, O_UP + 2 * j
                    for m in range(2):
                        act.wait_ge(proj_done, 4 * i + (t + m))
                        act.activation(up_av[:, m], bank[m][:, :], ACT.Copy).then_inc(evac[m], 1)
                    if j == 0:
                        hi(n + 2, 2 * i)
                    act.wait_ge(conv_done, 4 * i + (2 * j + 1))
                    act.activation(cv_av[:, 0], cv_av[:, 0], ACT.Silu).then_inc(silu_done, 1)
                    if j == 1:
                        hi(n + 2, 2 * i)
                    act.wait_ge(af_ready, 2 * i + (j + 1))
                    act.activation(act_hi[:, bass.ds(2 * i + j, 1)].rearrange("p a l -> p (a l)"), cv_av[:, 0],
                                   ACT.Copy).then_inc(ah_ready, 1)
            with act.Fori(0, 4) as i:
                for j in range(4):
                    n = N_DOWN + j
                    if j % 2:
                        act.wait_ge(proj_done, 2 * i + (O_DOWN + j // 2))
                    else:
                        act.wait_ge(half_used, 2 * i + (j // 2 + 1))
                    hi(n + 2, 4 * i)
            rehigh("nf", x_ready(O_DOWN))
            rehigh("conv", lambda k: act.wait_ge(xf_ready, k + 1))
            highs("conv")
            with act.Fori(0, CT) as i:
                t = O_CIN
                act.wait_ge(proj_done, 4 * i + t)
                act.activation(cg[:, :], bank[0][:, :], ACT.Copy).then_inc(evac[0], 1)
                act.wait_ge(proj_done, 4 * i + (t + 1))
                hi(N_CIN + 2, 2 * i)
                act.wait_ge(proj_done, 4 * i + (t + 3))
                act.activation(csil[:, :], bank[1][:, :], ACT.Silu).then_inc(evac[1], 1)
                hi(N_CIN + 3, 2 * i)
                act.wait_ge(yc_ready, i + 1)
                act.activation(yc_hi[:, bass.ds(i, 1)].rearrange("p a l -> p (a l)"), cacc[:, :],
                               ACT.Copy).then_inc(ych_ready, 1)
            for n in range(N_COUT, N_AIN):
                act.wait_ge(proj_done, done_after(n))
                hi(n + 2)
            rehigh("attn2", x_ready(O_COUT))
            highs("attn2")

            def qk_evac(c, r, e):
                tile, nth = O_AIN + 10 * c + e, 6 * c + e
                act.wait_ge(proj_done, 10 * r + tile)
                if nth >= 2:
                    act.wait_ge(d_qk, 6 * r + (nth - 1))
                act.activation(rawd[:, e % 2], bank[e % 2][:, :], ACT.Copy).then_inc(evac[e % 2], 1)
                act.wait_ge(evac[e % 2], 5 * r + (emptied(tile) + 1))
                act.activation(sq[:, e % 2], rawd[:, e % 2], ACT.Square).then_inc(d_sq, 1)

            def qk_root(c, r, e):
                act.wait_ge(d_sum, 6 * r + (6 * c + e + 1))
                act.activation(stdd[e % 2], bank[2][:, :], ACT.Sqrt, bias=eps, scale=1.0 / HD)\
                   .then_inc(d_std, 1)

            def v_evac(c, r, g):
                tile = O_AIN + 10 * c + 6 + g
                act.wait_ge(proj_done, 10 * r + tile)
                if 3 * c + g:
                    act.wait_ge(d_vturned, 3 * r + (3 * c + g))
                d = GROUPS[g][1]
                src, dst = bank[g % 2][:, :], hf[:, 0]
                if d > 1:
                    src = src.rearrange("p (l r) -> p l r", r=d)
                    dst = dst.rearrange("p (r l) -> p l r", r=d)
                act.activation(dst, src, ACT.Copy).then_inc(evac[g % 2], 1)

            def z_evac(c, r):
                act.wait_ge(proj_done, 10 * r + (O_AIN + 10 * c + 9))
                act.activation(zg[:, c % 2], bank[1][:, :], ACT.Silu).then_inc(evac[1], 1)

            def exps(c, r, u):
                act.wait_ge(d_mperm, r + (c + 1))
                slots = unit_slots(u)
                for k, (g, h, i, s0, n) in enumerate(slots):
                    m = mnat[:, i, h:h + 1] if g == 0 else mperm[:, g - 1, i, h:h + 1]
                    v = sd_sb[:, u, P * s0:P * (s0 + n)]
                    ins = act.activation(v, v, ACT.Exp, bias=m, scale=-1.0)
                ins.then_inc(d_exp, 1)

            def pair_act(att, nxt):
                if nxt:
                    c, r = nxt
                    n, rr = N_AIN + 5 * c, 5 * r
                    for e in range(6):
                        qk_evac(c, r, e)
                        if e % 2:
                            hi(n + e // 2 + 2, rr)
                        if e:
                            qk_root(c, r, e - 1)
                    v_evac(c, r, 0)
                    qk_root(c, r, 5)
                for u in range(4):
                    if att:
                        exps(*att, u)
                    if nxt and u < 3:
                        if u < 2:
                            v_evac(c, r, 1 + u)
                        else:
                            z_evac(c, r)
                        if u % 2 == 0:
                            hi(n + 3 + u // 2 + 2, rr)

            pair_act(None, (0, 0))
            with act.Fori(0, 3) as i:
                pair_act((0, 2 * i), (1, 2 * i))
                pair_act((1, 2 * i), (2, 2 * i))
            pair_act((6, 0), (7, 0))
            pair_act((7, 0), None)
            for k in range(KD):
                act.wait_ge(d_y, k + 1)
                act.activation(h_hi[:, k], yatt[:, k], ACT.Copy).then_inc(hh_ready, 1)
            for n in range(N_AOUT, N_ALL):
                act.wait_ge(proj_done, done_after(n))
                hi(n + 2)

        @block.gpsimd
        def _(pool):
            def e_make(t):
                e = e_tab[:, t % 2]
                steps.wait(pool)
                if t == 0:
                    pool.wait_ge(s5_tabs, 1)
                if t >= 2:
                    pool.wait_ge(back_done, 2 * (t - 1))
                sh = [P, 16, 32]

                def a_of(j):
                    return a_tab[:, j, t].unsqueeze(2).broadcast_to(sh)

                def b_of(j):
                    return b_tab[:, j, t].unsqueeze(1).broadcast_to(sh)

                def v(ap):
                    return ap.rearrange("p (a b) -> p a b", a=16)

                for j, (m0, m1, op) in enumerate((((0, 0), (1, 1), ALU.subtract), ((1, 0), (0, 1), ALU.add))):
                    pool.tensor_tensor(v(e[:, j]), a_of(m0[0]), b_of(m0[1]), ALU.mult)
                    steps.inc(pool.tensor_tensor(v(pool_t[:, :]), a_of(m1[0]), b_of(m1[1]), ALU.mult))
                    steps.wait(pool)
                    ins = pool.tensor_tensor(e[:, j], e[:, j], pool_t[:, :], op)
                    if j:
                        ins.then_inc(e_ready, 1)
                    else:
                        steps.inc(ins)
                        steps.wait(pool)
                pool.wait_ge(e_ready, t + 1)

            def lo(n, r=0):
                pool.wait_ge(hi_done, r + (n + 1))
                pool.tensor_tensor(w_lo[:, n % 2], raw[:, n % 2], w_hi[:, n % 2].bitcast(F32),
                                   ALU.subtract).then_inc(lo_done, 1)

            steps = Count(pool_step)
            pool.memset(eps, 1.0e-6).then_inc(eps_set, 1)
            for n in range(8):
                lo(n)
            e_make(0)
            e_make(1)
            for t in range(2, 16):
                e_make(t)
            lo(8)
            with pool.Fori(0, (N_ALL - 9) // 2) as i:
                for j in range(2):
                    lo(9 + j, 2 * i)

        @block.vector
        def _(dve):
            steps = Count(dve_step)

            def step(ins):
                steps.inc(ins)
                steps.wait(dve)

            def tt(o, a, b, op):
                step(dve.tensor_tensor(o, a, b, op))

            def rstd(m):
                dve.wait_ge(std_ready, m + 1)
                dve.reciprocal(std[:, :], std[:, :]).then_inc(rstd_ready, 1)
                dve.wait_ge(rstd_ready, m + 1)

            def normed(g, src, gain):
                if g >= 2:
                    dve.wait_ge(hl_ready, g - 1)
                o = hf[:, g % 2]
                dve.scalar_tensor_tensor(o, src, gain, std[:, :], ALU.mult, ALU.mult).then_inc(hf_ready, 1)

            def low_h(g, k, shift=None):
                dve.wait_ge(hh_ready, g + 1)
                if shift is None:
                    ins = dve.tensor_tensor(h_lo[:, k], hf[:, g % 2], h_hi[:, k].bitcast(F32), ALU.subtract)
                else:
                    ins = dve.scalar_tensor_tensor(h_lo[:, k], hf[:, g % 2], shift[:, k:k + 1],
                                                   h_hi[:, k].bitcast(F32), ALU.add, ALU.subtract)
                ins.then_inc(hl_ready, 1)

            def mult(o, a, b): tt(o, a, b, ALU.mult)
            def add(o, a, b): tt(o, a, b, ALU.add)
            def sub(o, a, b): tt(o, a, b, ALU.subtract)

            def renorm(name, gain, shift=None):
                q, m, g0 = NORMS[name]
                rstd(m)
                for k in range(KD):
                    normed(g0 + k, x[:, k], gain[:, k:k + 1])
                    if k:
                        low_h(g0 + k - 1, k - 1, shift)
                low_h(g0 + KD - 1, KD - 1, shift)

            dve.wait_ge(vec_in, 48)
            dve.wait_ge(vec_done, 1)
            dve.tensor_tensor(vec[:, 0:384], bank[4][0:16, 0:384], vmask[:, 0:384], ALU.add).then_inc(vec_ready, 1)
            dve.tensor_tensor(vec[:, 384:704], bank[5][0:16, 0:320], vmask[:, 384:704], ALU.add).then_inc(vec_ready, 1)
            dve.wait_ge(gains_in, 32)
            dve.wait_ge(mod_done, 16)
            step(dve.tensor_tensor(mod[:, 0:16], MODC[:, 0:16], b_ada[:, 0:16], ALU.add))
            step(dve.scalar_tensor_tensor(GS1, SC1, 1.0, G["n1"], ALU.add, ALU.mult))
            renorm("n1", GS1, SH1)
            dve.memset(s5t[:, 0], 0.0)
            dve.memset(c_s5[:, :, :, :], 0.0)
            dve.wait_ge(s5_act, 1)
            dve.wait_ge(s5_in, 48)
            dve.tensor_tensor(T0, LR, STEP, ALU.mult).then_inc(s5_need, 1)
            mult(TH, LI, STEP)
            step(dve.tensor_scalar(TK, TH, 1.0 / (2 * PI), 12582912.0, ALU.mult, ALU.add))
            step(dve.tensor_scalar(TK, TK, 12582912.0, None, ALU.subtract))
            step(dve.scalar_tensor_tensor(TH, TK, -6.28125, TH, ALU.mult, ALU.add))
            step(dve.scalar_tensor_tensor(TH, TK, -(2 * PI - 6.28125), TH, ALU.mult, ALU.add))
            step(dve.tensor_scalar(TH, TH, 3.1415925, -3.1415925, ALU.min, ALU.max))
            step(dve.tensor_scalar(TC, TH, PI / 2, None, ALU.is_gt))
            step(dve.scalar_tensor_tensor(TC, TC, -2 * PI, TH, ALU.mult, ALU.add))
            step(dve.tensor_scalar(TC, TC, PI / 2, None, ALU.add))
            dve.tensor_scalar(TC, TC, 3.1415925, -3.1415925, ALU.min, ALU.max).then_inc(s5_need, 1)
            dve.wait_ge(s5_act, 4)
            mult(ARE, MAG, COS)
            mult(AIM, MAG, SIN)
            mult(T0, LR, LR)
            mult(T1, LI, LI)
            add(DEN, T0, T1)
            step(dve.reciprocal(DEN, DEN))
            step(dve.tensor_scalar(NRE, ARE, -1.0, None, ALU.add))
            mult(T0, NRE, LR)
            mult(T1, AIM, LI)
            add(T0, T0, T1)
            mult(FRE, T0, DEN)
            mult(T0, AIM, LR)
            mult(T1, NRE, LI)
            sub(T0, T0, T1)
            mult(FIM, T0, DEN)
            fre, fim = (f.unsqueeze(2).broadcast_to([P, 16, 16]) for f in (FRE, FIM))
            mult(s5t[:, 0], c_in[:, 0], fre)
            mult(s5t[:, 1], c_in[:, 1], fim)
            sub(s5t[:, 0], s5t[:, 0], s5t[:, 1])
            mult(s5t[:, 1], c_in[:, 0], fim)
            mult(s5t[:, 2], c_in[:, 1], fre)
            add(s5t[:, 1], s5t[:, 1], s5t[:, 2])
            for g in range(2):
                r = slice(64 * g, 64 * g + 64)
                cc = slice(16 * g, 16 * g + 16)
                dve.tensor_copy(c_s5[r, 0, :, cc], s5t[r, 0])
                dve.tensor_scalar(c_s5[r, 1, :, cc], s5t[r, 0], -1.0, None, ALU.mult)
                step(dve.tensor_scalar(c_s5[r, 2, :, cc], s5t[r, 1], -1.0, None, ALU.mult))

            def square_power():
                mult(PC2, PC, PC)
                mult(T0, PS, PS)
                mult(PS2, PC, PS)
                sub(PC, PC2, T0)
                step(dve.tensor_scalar(PS, PS2, 2.0, None, ALU.mult))

            def grow(tab, count):
                dve.memset(tab[:, 0, :, 0:1], 1.0)
                step(dve.memset(tab[:, 1, :, 0:1], 0.0))
                m = 1
                while m < count:
                    pc, ps = (f.unsqueeze(2).broadcast_to([P, 16, m]) for f in (PC, PS))
                    oc, os_ = tab[:, 0, :, 0:m], tab[:, 1, :, 0:m]
                    nc_, ns = tab[:, 0, :, m:2 * m], tab[:, 1, :, m:2 * m]
                    tmp = s5t[:, 0, :, 0:m]
                    mult(nc_, oc, pc)
                    mult(tmp, os_, ps)
                    sub(nc_, nc_, tmp)
                    mult(ns, oc, ps)
                    mult(tmp, os_, pc)
                    add(ns, ns, tmp)
                    square_power()
                    m *= 2

            step(dve.tensor_copy(PC, COS))
            step(dve.tensor_copy(PS, SIN))
            grow(b_tab, 32)
            grow(a_tab, 16)
            dve.sem_inc(s5_tabs, 1)

            def rope(s_rot, s_dup, src, dst):
                dve.wait_ge(prep_done, max(s_rot, s_dup) + 1)
                ins = dve.tensor_tensor(hf[:, 0], bank[B_PREP[s_rot % 2]][:, :], sinT, ALU.mult)
                ins.then_inc(prep_taken[s_rot % 2], 1)
                if s_dup:
                    dve.tensor_tensor(dst, bank[B_PREP[1]][:, :], cosT, ALU.mult).then_inc(prep_taken[1], 1)
                    dve.wait_ge(prep_taken[1], s_dup // 2 + 1)
                else:
                    step(dve.tensor_tensor(dst, src, cosT, ALU.mult))
                dve.wait_ge(prep_taken[s_rot % 2], s_rot // 2 + 1)
                dve.tensor_tensor(dst, dst, hf[:, 0], ALU.add).then_inc(roped, 1)

            dve.wait_ge(attn_in, 16 * 11)
            dve.wait_ge(hh_ready, 8)
            dve.wait_ge(hl_ready, 8)
            dve.wait_ge(evac[0], 3)
            rope(0, 0, z[:, T_KC], z[:, T_KC])
            dve.wait_ge(roped, 1)
            dve.wait_ge(evac[1], 3)
            for v, src in enumerate((z[:, T_KC], z[:, T_VC])):
                for j2 in range(2):
                    for hh in range(2):
                        for c in range(2):
                            r = slice(64 * hh, 64 * hh + 64)
                            tok = src[r].rearrange("p (n j) -> p j n", j=16)[:, j2:16:2, c:c + NCMP]
                            pe_j = pe_t[r, v, 16 * c + j2:16 * c + 16:2].unsqueeze(2).broadcast_to([64, 8, NCMP])
                            dve.tensor_tensor(blk[64 * j2:64 * j2 + 64, v, 8 * c:8 * c + 8, 31 * hh:31 * hh + 31],
                                              tok, pe_j, ALU.add).then_inc(blocks_ready, 1)
            for s in (1, 2):
                dve.wait_ge(prep_done, s + 1)
                dve.tensor_copy(v_tok[:, s - 1], bank[B_PREP[s % 2]][:, :].rearrange("p (t f) -> p t f", t=TT))\
                   .then_inc(prep_taken[s % 2], 1)
            for j in range(4):
                dve.wait_ge(roped, j + 1)
                rope(4 + j, 0, z[:, T_Q + j], z[:, T_Q + j])
            for j, dst in enumerate((T_VS, T_VW, T_KC, T_VC)):
                dve.wait_ge(roped, 5 + j)
                dve.wait_ge(blocks_ready, 16)
                rope(8 + 2 * j, 9 + 2 * j, None, z[:, dst])
            dve.wait_ge(prep_done, 19)
            dve.tensor_copy(kc_t[:, :], bank[2][:, 0:62]).then_inc(prep_taken[0], 1)
            dve.wait_ge(prep_done, 20)
            dve.tensor_copy(vc_t[0:NCMP, :, :], bank[7][0:NCMP, 0:128].rearrange("p (h f) -> p h f", h=2))\
               .then_inc(prep_taken[1], 1)

            fw, zz, qq = pq[:, 0:4], None, pq[:, 4:8]

            def s5_forward(t):
                e = e_tab[:, t % 2]
                dve.wait_ge(e_ready, t + 1)
                dve.wait_ge(bu_done, t + 1)
                for j in range(2):
                    src = bank[B_BU[j]][:, :].unsqueeze(1).broadcast_to([P, 2, L])
                    dve.tensor_tensor(fw[:, 2 * j:2 * j + 2], e, src, ALU.mult).then_inc(bu_taken, 1)
                dve.wait_ge(bu_taken, 2 * t + 2)
                steps.inc(dve.tensor_tensor(fw[:, 0], fw[:, 0], fw[:, 3], ALU.add))
                step(dve.tensor_tensor(fw[:, 2], fw[:, 2], fw[:, 1], ALU.subtract))
                mag = MAG[:, t:t + 1].broadcast_to([P, L])
                for j in (0, 2):
                    steps.inc(dve.tensor_tensor_scan(fw[:, j + 1], mag, fw[:, j], 0.0, ALU.mult, ALU.add))
                steps.wait(dve)

            def s5_back(t):
                e = e_tab[:, t % 2]
                if t:
                    dve.wait_ge(cmul_done, t)
                for j in range(2):
                    src = fw[:, 2 * j + 1].unsqueeze(1).broadcast_to([P, 2, L])
                    dve.tensor_tensor(qq[:, 2 * j:2 * j + 2], e, src, ALU.mult).then_inc(back_done, 1)

            def y_make(zt):
                dve.wait_ge(cmul_done, 4 * zt + 4)
                dve.scalar_tensor_tensor(z[:, zt], z[:, zt], DSKIP[:, zt:zt + 1], bank[B_Y][:, :],
                                         ALU.mult, ALU.add).then_inc(y_ready, 1)

            coef = small[:, 32:35]
            for u in range(33):
                if u:
                    h, i = (u - 1) % 8, (u - 1) // 8
                    kw = P * (i + 1)
                    den = small[:, 8 * ((u - 1) % 2):8 * ((u - 1) % 2) + 3]
                    dve.wait_ge(turned, u)
                    if u >= 2:
                        dve.wait_ge(pv_done, u - 1)
                    dve.tensor_copy(pt_s[:, 0:kw], bank[2][:, 0:kw]).then_inc(pt_dve, 1)
                if u < 32:
                    i = u // 8
                    kw = P * (i + 1)
                    nmx = small[:, 8 * (u % 2) + 4:8 * (u % 2) + 7]
                    dve.wait_ge(scores_done, u + 1)
                    for b, (src, m, c0, w) in enumerate((
                            (SC, cmask[:, i], 1024 + 32 * (u % 2), NCMP),
                            (bank[0][:, 0:kw], mask[:, 384 - P * i:512], 0, kw),
                            (bank[1][:, 0:kw], mask[:, 384 - P * i:512], 512, kw))):
                        dve.tensor_tensor_reduce(s_sb[:, c0:c0 + w], src, m, -HD ** -0.5, 1.0e28,
                                                 ALU.add, ALU.min, nmx[:, b:b + 1]).then_inc(max_ready, 1)
                if u:
                    h, i = (u - 1) % 8, (u - 1) // 8
                    dve.wait_ge(exp_done, 3 * u)
                    step(dve.tensor_scalar(den, den, 1.0e-30, None, ALU.max))
                    step(dve.reciprocal(den, den))
                    step(dve.tensor_tensor(coef, den, gates[:, i, 3 * h:3 * h + 3], ALU.mult))
                    o = o_tok[:, i, HD * h:HD * h + HD]
                    dve.wait_ge(pv_done, u)
                    step(dve.tensor_scalar(o, PV[:, 0:64], coef[:, 0:1], None, ALU.mult))
                    step(dve.scalar_tensor_tensor(o, PV[:, 64:128], coef[:, 1:2], o, ALU.mult, ALU.add))
                    dve.scalar_tensor_tensor(o, PV[:, 128:192], coef[:, 2:3], o, ALU.mult, ALU.add)\
                       .then_inc(combined, 1)
                if u % 8 == 0 and u:
                    y_make(u // 8 - 1)
                if u < 32:
                    if u % 2 == 0:
                        s5_forward(u // 2)
                    else:
                        s5_back(u // 2)
            dve.wait_ge(mod_done, 48)
            step(dve.tensor_tensor(mod[:, 16:48], MODC[:, 16:48], b_ada[:, 16:48], ALU.add))
            step(dve.scalar_tensor_tensor(GS2, SC2, 1.0, G["n2"], ALU.add, ALU.mult))
            for m in range(4):
                dve.wait_ge(yh_ready, m + 1)
                dve.tensor_tensor(y_lo[:, m], z[:, m], y_hi[:, m].bitcast(F32), ALU.subtract).then_inc(yl_ready, 1)
            dve.wait_ge(ostd, 1)
            step(dve.reciprocal(small[:, 24:28], small[:, 20:24]))
            dve.wait_ge(combined, 32)
            for i in range(TT):
                dve.tensor_scalar(o_tok[:, i], o_tok[:, i], small[:, 24 + i:25 + i], None, ALU.mult)\
                   .then_inc(onorm, 1)
            for m in range(4):
                t = O_GLU + m
                dve.wait_ge(evac[t % 2], t // 2 + (0 if t % 2 else 1))
                dve.tensor_tensor(z[:, m], z[:, m], pool_t[:, :] if m % 2 else e_tab[:, 0, 0], ALU.mult)\
                   .then_inc(mixed, 1)
            dve.wait_ge(mixed, 4)
            rstd(1)
            for m in range(4):
                normed(8 + m, z[:, m], G["mix"][:, 4 + m:5 + m])
                if m:
                    low_h(7 + m, 3 + m)
            low_h(11, 7)
            for m in range(4):
                g = 12 + m
                dve.wait_ge(oturned, m + 1)
                dve.wait_ge(hl_ready, g - 1)
                dve.tensor_scalar(hf[:, g % 2], bank[4 + m][:, :], G["mix"][:, m:m + 1], None, ALU.mult)\
                   .then_inc(hf_ready, 1)
                if m:
                    low_h(g - 1, m - 1)
            low_h(15, 3)
            for m in range(KD):
                t = O_O + m
                dve.wait_ge(proj_done, t)
                dve.scalar_tensor_tensor(x[:, m], bank[t % 2][:, :], GT1[:, m:m + 1], x[:, m], ALU.mult,
                                         ALU.add).then_inc(evac[t % 2], 1)

            renorm("n2", GS2, SH2)
            with dve.Fori(0, FT // 2) as i:
                steps.loop(i, 8)
                for j in range(2):
                    for m in range(2):
                        c = 2 * i + (j + FT * m)

                        def wb(k):
                            return conv_wb[:, k, bass.ds(c, 1)]

                        u, o = up_av[:, m], cv_av[:, m]
                        dve.wait_ge(evac[m], 2 * i + (emptied(O_UP + 2 * j + m) + 1))
                        step(dve.tensor_scalar(o, u, wb(2), wb(3), ALU.mult, ALU.add))
                        step(dve.scalar_tensor_tensor(o[:, 1:], u[:, 0:L - 1], wb(1), o[:, 1:], ALU.mult, ALU.add))
                        dve.scalar_tensor_tensor(o[:, 2:], u[:, 0:L - 2], wb(0), o[:, 2:], ALU.mult, ALU.add)\
                           .then_inc(conv_done, 1)
                    dve.wait_ge(silu_done, 2 * i + (j + 1))
                    dve.wait_ge(conv_done, 4 * i + (2 * j + 2))
                    dve.tensor_tensor(cv_av[:, 0], cv_av[:, 0], cv_av[:, 1], ALU.mult).then_inc(af_ready, 1)
                    dve.wait_ge(ah_ready, 2 * i + (j + 1))
                    at = bass.ds(2 * i + j, 1)
                    dve.tensor_tensor(act_lo[:, at].rearrange("p a l -> p (a l)"), cv_av[:, 0],
                                      act_hi[:, at].rearrange("p a l -> p (a l)").bitcast(F32),
                                      ALU.subtract).then_inc(al_ready, 1)
                    dve.wait_ge(al_ready, 2 * i + (j + 1))
            steps.leave(FT // 2)
            with dve.Fori(0, 4) as i:
                for j in range(2):
                    at = x[:, bass.ds(2 * i + j, 1)].rearrange("p a l -> p (a l)")
                    dve.wait_ge(proj_done, 2 * i + (O_DOWN + j))
                    dve.scalar_tensor_tensor(at, bank[j][:, :], mod[:, bass.ds(2 * i + (40 + j), 1)], at, ALU.mult,
                                             ALU.add).then_inc(evac[j], 1)
            for m in range(2):
                dve.wait_ge(evac[m], emptied(O_DOWN + 6 + m) + 1)
            rstd(3)
            for k in range(KD):
                dve.scalar_tensor_tensor(x[:, k], x[:, k], G["nf"][:, k:k + 1], std[:, :], ALU.mult, ALU.mult)\
                   .then_inc(xf_ready, 1)
            step(dve.memset(cu[:, 0:2], 0.0))
            dve.wait_ge(xf_ready, KD)
            renorm("conv", G["conv"])
            with dve.Fori(0, CT) as i:
                steps.loop(i, 4)

                def tap(k):
                    return conv2_w[:, k, bass.ds(i, 1)]

                t = O_CIN
                dve.wait_ge(proj_done, 4 * i + (t + 1))
                dve.wait_ge(evac[0], 2 * i + (emptied(t) + 1))
                dve.tensor_tensor(cu[:, 2:], cg[:, :], bank[1][:, :], ALU.mult).then_inc(evac[1], 1)
                dve.wait_ge(evac[1], 2 * i + (emptied(t + 1) + 1))
                step(dve.tensor_scalar(cacc[:, :], cu[:, 2:], tap(2), None, ALU.mult))
                step(dve.scalar_tensor_tensor(cacc[:, :], cu[:, 1:L + 1], tap(1), cacc[:, :], ALU.mult, ALU.add))
                step(dve.scalar_tensor_tensor(cacc[:, :], cu[:, 0:L], tap(0), cacc[:, :], ALU.mult, ALU.add))
                dve.wait_ge(proj_done, 4 * i + (t + 2))
                dve.tensor_tensor(cacc[:, :], cacc[:, :], bank[0][:, :], ALU.mult).then_inc(evac[0], 1)
                dve.wait_ge(evac[0], 2 * i + (emptied(t + 2) + 1))
                dve.wait_ge(evac[1], 2 * i + (emptied(t + 3) + 1))
                dve.tensor_tensor(cacc[:, :], cacc[:, :], csil[:, :], ALU.mult).then_inc(yc_ready, 1)
                dve.wait_ge(ych_ready, i + 1)
                at = bass.ds(i, 1)
                step(dve.tensor_tensor(yc_lo[:, at].rearrange("p a l -> p (a l)"), cacc[:, :],
                                       yc_hi[:, at].rearrange("p a l -> p (a l)").bitcast(F32), ALU.subtract))
            steps.leave(CT)
            dve.sem_inc(ycl_ready, 1)
            with dve.Fori(0, 4) as i:
                for j in range(2):
                    at = x[:, bass.ds(2 * i + j, 1)].rearrange("p a l -> p (a l)")
                    dve.wait_ge(proj_done, 2 * i + (O_COUT + j))
                    dve.tensor_tensor(at, bank[j][:, :], at, ALU.add).then_inc(evac[j], 1)
            for m in range(2):
                dve.wait_ge(evac[m], emptied(O_COUT + 6 + m) + 1)
            renorm("attn2", G["attn2"])

            for c in range(2):
                dve.memset(vv[:, c, :, 1], 1.0).then_inc(d_ones, 1)
            for g in range(3):
                step(dve.tensor_scalar(qk_gain[:, 2 * g:2 * g + 1], qk_gain[:, 2 * g:2 * g + 1], HD ** -0.5, None,
                                       ALU.mult))
            dve.wait_ge(perm_in, 64)

            def qk_make(c, r, e):
                nth = 6 * c + e
                d = GROUPS[e // 2][1]
                dst, a, b = qk[:, c % 2, e], rawd[:, e % 2], stdd[e % 2]
                dve.wait_ge(d_std, 6 * r + (nth + 1))
                step(dve.reciprocal(b, b))
                if d > 1:
                    dst = dst.rearrange("p (r l) -> p l r", r=d)
                    a = a.rearrange("p (l r) -> p l r", r=d)
                    b = b.rearrange("p (l r) -> p l r", r=d)
                dve.scalar_tensor_tensor(dst, a, qk_gain[:, e:e + 1], b, ALU.mult, ALU.mult).then_inc(d_qk, 1)

            def v_make(c, r, g):
                dve.wait_ge(d_vturned, 3 * r + (3 * c + g + 1))
                dve.tensor_copy(vv[:, c % 2, TT * g:TT * g + TT, 0:3:2],
                                bank[3][:, :].rearrange("p (i h f) -> p i h f", i=TT, h=2)).then_inc(d_vset, 1)

            def scores_in(c, r, u):
                dve.wait_ge(d_scores, 4 * r + (4 * c + u + 1))
                if u == 0:
                    dve.wait_ge(bias_in, 16 * r + 16 * (c + 1))
                dve.sem_inc(dve_held, 1)
                for g, h, i, s0, n in unit_slots(u):
                    src = bank[4 + s0 // 4][:, P * (s0 % 4):P * (s0 % 4 + n)]
                    b1 = (256, 384, 512)[g]
                    ins = dve.tensor_tensor_reduce(sd_sb[:, u, P * s0:P * (s0 + n)], src,
                                                   bias[:, h, b1 - P * n:b1], -1.0, 3.0e38, ALU.add, ALU.min,
                                                   stat[:, g, i, h:h + 1])
                ins.then_inc(d_max, 1)

            def spread_stats(c, r):
                dve.wait_ge(d_max, 4 * r + (4 * c + 4))
                for g in range(2):
                    a = stat[:, g + 1].unsqueeze(2).broadcast_to([P, 4, 4, 2])
                    m = pmask[:, g].unsqueeze(1).unsqueeze(3).broadcast_to([P, 4, 4, 2])
                    dve.tensor_tensor(spread[:, g], a, m, ALU.mult).then_inc(d_spread, 1)

            def least(c, r):
                dve.wait_ge(d_natural, r + (c + 1))
                nat = bank[3][:, 0:16].rearrange("p (g i h) -> p g i h", g=2, i=4)
                step(dve.tensor_tensor(mnat, stat[:, 0], nat[:, 0], ALU.min))
                dve.tensor_tensor(mnat, mnat, nat[:, 1], ALU.min).then_inc(d_min, 1)

            def least_back(c, r):
                dve.wait_ge(d_back, r + (c + 1))
                for g in range(2):
                    a = bank[3][:, 64 + 32 * g:96 + 32 * g].rearrange("p (r i h) -> p r i h", r=4, i=4)
                    m = pmask[:, g].unsqueeze(1).unsqueeze(3).broadcast_to([P, 4, 4, 2])
                    step(dve.tensor_tensor(spread[:, g], a, m, ALU.mult))
                dve.tensor_reduce(cw[:, 96:112].rearrange("p (a h) -> p a h", h=2),
                                  cw[:, 0:64].rearrange("p (a i h) -> p a h i", i=4, h=2),
                                  AX.X, ALU.add).then_inc(d_mperm, 1)

            def pt_copy(c, r, u):
                dve.wait_ge(d_turned, 4 * r + (4 * c + u + 1))
                lo_ = P if u < 2 else 0
                steps.inc(dve.tensor_copy(sd_sb[:, u, lo_:512], bank[4][:, lo_:512]))
                steps.wait(dve)
                dve.tensor_copy(sd_sb[:, u, 512:1024], bank[5][:, :]).then_inc(d_pt, 1)

            def finish(c, r):
                dve.wait_ge(d_pv, 4 * r + (4 * c + 4))
                y = yatt[:, bass.ds(r + c, 1)].rearrange("p a l -> p (a l)")
                for h in range(2):
                    o = y[64 * h:64 * h + 64, :]
                    rows, other = slice(64 * h, 64 * h + 64), slice(64 - 64 * h, 128 - 64 * h)
                    step(dve.reciprocal(rden[rows, :], bank[6 + h][other, :]))
                    step(dve.tensor_tensor(o, bank[6 + h][rows, :], rden[rows, :], ALU.mult))
                dve.tensor_tensor(y, y, zg[:, c % 2], ALU.mult).then_inc(d_y, 1)

            def pair_dve(att, nxt):
                if att:
                    scores_in(*att, 0)
                for u in range(4):
                    if att and u:
                        scores_in(*att, u)
                    if nxt and u:
                        qk_make(*nxt, u - 1)
                if att:
                    spread_stats(*att)
                    least(*att)
                if nxt:
                    qk_make(*nxt, 3)
                if att:
                    least_back(*att)
                if nxt:
                    qk_make(*nxt, 4)
                    qk_make(*nxt, 5)
                for u in range(4):
                    if att:
                        pt_copy(*att, u)
                    if nxt and u < 3:
                        v_make(*nxt, u)
                if att:
                    finish(*att)

            pair_dve(None, (0, 0))
            with dve.Fori(0, 3) as i:
                steps.loop(i, 2 * PAIR_STEPS)
                pair_dve((0, 2 * i), (1, 2 * i))
                pair_dve((1, 2 * i), (2, 2 * i))
            steps.leave(3)
            pair_dve((6, 0), (7, 0))
            pair_dve((7, 0), None)
            for k in range(KD):
                dve.wait_ge(hh_ready, 40 + k + 1)
                dve.tensor_tensor(h_lo[:, k], yatt[:, k], h_hi[:, k].bitcast(F32), ALU.subtract)\
                   .then_inc(hl_ready, 1)
            for k in range(KD):
                dve.wait_ge(proj_done, O_AOUT + k)
                dve.tensor_tensor(x[:, k], bank[k % 2][:, :], x[:, k], ALU.add).then_inc(evac[k % 2], 1)

        @block.tensor
        def _(pe):
            def sums(name, nk, b=B_SUM):
                q0, m, _ = NORMS[name]
                for k in range(nk):
                    pe.wait_ge(sq_ready, q0 + k + 1)
                    mm = pe.matmul(bank[b][:, :], ones[:, :], sq[:, (q0 + k) % 2], start=k == 0, stop=k == nk - 1)
                    mm.then_inc(sq_used, 1)
                pe.wait_ge(sq_used, q0 + nk)
                pe.sem_inc(sums_done, 1)

            def ada(r, j):
                pe.wait_ge(r32_in[r % 2], 16 * (r // 2 + 1))
                for k in range(KD):
                    mm = pe.matmul(MODC[:, j:j + 1], r32[:, r % 2, k * P:(k + 1) * P], cs[:, 1, k:k + 1],
                                   start=k == 0, stop=k == KD - 1, skip_group_check=True)
                mm.then_inc(r32_used, 1)

            def mod_count(n):
                pe.wait_ge(r32_used, n)
                pe.sem_inc(mod_done, 16)

            def bank_free(t, d=0):
                n = t // 2 - (1 if t > 15 and t % 2 else 0)
                if n > 0:
                    pe.wait_ge(evac[t % 2], n)

            pe.wait_ge(ones_in, 16)
            pe.wait_ge(vec_in, 48)
            pe.matmul(bank[4][0:16, 0:384], tabs[:, 0:16], onehot[:, 0:384], start=True, stop=True)
            pe.matmul(bank[5][0:16, 0:256], tabs[:, 16:32], onehot[:, 384:640], start=True, stop=True)
            pe.matmul(bank[5][0:16, 256:320], tabs[:, 32:48], onehot[:, 640:704], start=True, stop=True)\
              .then_inc(vec_done, 1)
            pe.wait_ge(cs_ready, 1)
            for r in range(16):
                if r == 8:
                    sums("n1", KD)
                ada(r, r)
            mod_count(16)
            for t in range(15):
                n, m = t // 2, t % 2
                if m == 0:
                    pe.wait_ge(lo_done, n + 1)
                bank_free(t)
                mm = products(pe, t % 2, *hblock(n % 2, KD, m), *hx, KD, ready=None if t else 0)
                mm.then_inc(proj_done, 1)

            def prep(s, body):
                if s >= 2:
                    pe.wait_ge(prep_taken[s % 2], s // 2)
                body(bank[B_PREP[s % 2]]).then_inc(prep_done, 1)

            def turn4(dst, src):
                for i in range(TT):
                    mm = pe.transpose(dst[:, i * P:(i + 1) * P], src[:, i * P:(i + 1) * P], ident[:, :])
                return mm

            def once(m, src):
                return lambda b: pe.matmul(b[:, :], ropem[:, m], src, start=True, stop=True)

            pe.wait_ge(attn_in, 16 * 11)
            pe.wait_ge(std_ready, 1)
            pe.wait_ge(evac[0], 8)
            pe.wait_ge(evac[1], 7)
            prep(0, once(0, z[:, T_KC]))
            prep(1, lambda b: turn4(b, z[:, T_VS]))
            prep(2, lambda b: turn4(b, z[:, T_VW]))
            prep(3, lambda b: turn4(b, z[:, T_ZG]))
            for j in range(4):
                prep(4 + j, once(0, z[:, T_Q + j]))
            for j in range(4):
                src = z[:, T_KS if j < 2 else T_KW]
                prep(8 + 2 * j, once(3 + j % 2, src))
                prep(9 + 2 * j, once(1 + j % 2, src))

            def hidden(v):
                def body(b):
                    for c in range(2):
                        for hh in range(2):
                            r = 16 + 4 * v + 2 * c + hh
                            pe.wait_ge(r32_in[r % 2], 16 * (r // 2 + 1))
                            for k in range(8):
                                mm = pe.matmul(b[:, 62 * hh:62 * hh + 62], r32[:, r % 2, k * P:(k + 1) * P],
                                               blk[:, v, 8 * c + k], start=c == 0 and hh == 0 and k == 0,
                                               stop=c == 1 and k == 7, skip_group_check=True)
                            if (c, hh) != (1, 1):
                                mm.then_inc(r32_used, 1)
                    return mm
                return body

            pe.wait_ge(blocks_ready, 16)
            for v in range(2):
                prep(16 + v, hidden(v))
                pe.wait_ge(prep_done, 17 + v)
                pe.sem_inc(r32_used, 1)

            def kc_body(b):
                for k in range(2):
                    mm = pe.matmul(b[:, 0:62], w_c2[:, k], hid[:, 0, k], start=k == 0, stop=k == 1)
                return mm

            def vc_body(b):
                for hh in range(2):
                    for k in range(2):
                        mm = pe.matmul(b[0:NCMP, 64 * hh:64 * hh + 64], hid[:, 1, k, 31 * hh:31 * hh + 31], w_v2[:, k],
                                       start=k == 0, stop=k == 1)
                return mm

            prep(18, kc_body)
            prep(19, vc_body)
            pe.wait_ge(prep_taken[0], 10)
            pe.wait_ge(prep_taken[1], 10)
            pe.wait_ge(roped, 9)

            ks_of, kw_of = (T_VS, T_VW), (T_KC, T_VC)

            def scores(u):
                h, i = u % 8, u // 8
                r = slice(64 * (h % 2), 64 * (h % 2) + 64)
                kv, w = h // 4, P * (i + 1)
                q = z[r, T_Q + h // 2, i * P:(i + 1) * P]
                if u:
                    pe.wait_ge(max_ready, 3 * u)
                pe.matmul(bank[0][:, 0:w], q, z[r, ks_of[kv], 0:w], start=True, stop=True)
                pe.matmul(bank[1][:, 0:w], q, z[r, kw_of[kv], 0:w], start=True, stop=True)
                if u >= 2:
                    pe.wait_ge(combined, u - 1)
                ada(24 + u, 16 + u)
                pe.matmul(SC, q, kc_t[r, 31 * kv:31 * kv + 31], start=True, stop=True,
                          skip_group_check=True).then_inc(scores_done, 1)

            def turn(u):
                i = u // 8
                pe.wait_ge(exp_done, 3 * u + 3)
                if u:
                    pe.wait_ge(pt_dve, u)
                    pe.wait_ge(pt_act, 2 * u)
                for j in range(i + 1):
                    pe.transpose(bank[2][:, j * P:(j + 1) * P], s_sb[:, j * P:(j + 1) * P], ident[:, :])
                    mm = pe.transpose(bank[7][:, j * P:(j + 1) * P], s_sb[:, 512 + j * P:640 + j * P], ident[:, :])
                mm.then_inc(turned, 1)

            def turn_c(u):
                if u < 31:
                    pe.wait_ge(max_ready, 3 * u + 4)
                else:
                    pe.wait_ge(combined, u)
                pe.transpose(TC31, s_sb[:, 1024 + 32 * (u % 2):1024 + 32 * (u % 2) + NCMP], ident[:, :])\
                  .then_inc(turned_c, 1)

            def values(u):
                h, i = u % 8, u // 8
                kv = slice(64 * (h // 4), 64 * (h // 4) + 64)
                pe.wait_ge(pt_dve, u + 1)
                pe.wait_ge(pt_act, 2 * u + 2)
                if u:
                    pe.wait_ge(combined, u)
                pe.matmul(PV[:, 0:64], pt_c[0:NCMP, :], vc_t[0:NCMP, h // 4], start=True, stop=True,
                          skip_group_check=True)
                for b, pt in enumerate((pt_s, pt_w)):
                    for j in range(i + 1):
                        mm = pe.matmul(PV[:, 64 + 64 * b:128 + 64 * b], pt[:, j * P:(j + 1) * P], v_tok[:, b, j, kv],
                                       start=j == 0, stop=j == i, skip_group_check=True)
                mm.then_inc(pv_done, 1)

            def s5_b(t):
                zt, j = t // 4, t % 4
                r = slice(32 * j, 32 * j + 32)
                if t:
                    pe.wait_ge(bu_taken, 2 * t)
                for c in range(2):
                    mm = pe.matmul(bank[B_BU[c]][:, :], b_s5[r, c, zt], z[r, zt], start=True, stop=True)
                mm.then_inc(bu_done, 1)

            def s5_c(t):
                zt, j = t // 4, t % 4
                pe.wait_ge(back_done, 2 * t + 2)
                if j == 0 and zt:
                    pe.wait_ge(y_ready, zt)
                for n, (part, p) in enumerate(((0, 0), (2, 1), (2, 2), (1, 3))):
                    mm = pe.matmul(bank[B_Y][32 * j:32 * j + 32, :], c_s5[:, part, t], pq[:, 4 + p],
                                   start=n == 0, stop=n == 3, skip_group_check=True)
                mm.then_inc(cmul_done, 1)

            s5_b(0)
            for u in range(33):
                if u:
                    turn(u - 1)
                if u < 32:
                    scores(u)
                if u:
                    turn_c(u - 1)
                    values(u - 1)
                if u % 2 == 0 and u:
                    s5_c(u // 2 - 1)
                if u % 2 and u // 2 + 1 < 16:
                    s5_b(u // 2 + 1)
            mod_count(56)
            pe.sem_inc(mod_done, 16)

            pe.wait_ge(lo_done, N_GLU + 1)
            pe.wait_ge(yl_ready, 4)
            for m in range(4):
                bank_free(O_GLU + m)
                mm = products(pe, m % 2, *hblock(N_GLU % 2, 4, m), lambda k: y_hi[:, k], lambda k: y_lo[:, k], 4)
                mm.then_inc(proj_done, 1)
            pe.wait_ge(onorm, 4)
            pe.wait_ge(y_ready, 4)
            for m in range(4):
                for i in range(TT):
                    mm = pe.transpose(bank[4 + m][:, i * P:(i + 1) * P], o_tok[:, i, m * P:(m + 1) * P], ident[:, :])
                mm.then_inc(oturned, 1)
            sums("ssm", 4)
            for m in range(KD):
                n = N_O + m // 2
                if m % 2 == 0:
                    pe.wait_ge(lo_done, n + 1)
                bank_free(O_O + m)
                mm = products(pe, m % 2, *hblock(n % 2, KD, m % 2), *hx, KD, k0=4, ready=None if m else 8)
                mm.then_inc(proj_done, 1)

            sums("n2", KD)
            with pe.Fori(0, FT // 2) as i:
                for j in range(2):
                    pe.wait_ge(lo_done, 2 * i + (N_UP + j + 1))
                    for m in range(2):
                        pe.wait_ge(evac[m], 2 * i + emptied(O_UP + 2 * j + m))
                        products(pe, m, *hblock((N_UP + j) % 2, KD, m), *hx, KD,
                                 ready=None if j or m else 16).then_inc(proj_done, 1)
            pe.wait_ge(al_ready, FT)
            with pe.Fori(0, 4) as i:
                for j in range(2):
                    for half in range(2):
                        n = N_DOWN + 2 * j + half
                        pe.wait_ge(lo_done, 4 * i + (n + 1))
                        if half == 0:
                            pe.wait_ge(evac[j], i + emptied(O_DOWN + j))
                        k0 = NB_DOWN * half
                        mm = products(pe, j, *hblock(n % 2, NB_DOWN, 0), lambda k: act_hi[:, k0 + k],
                                      lambda k: act_lo[:, k0 + k], NB_DOWN, half == 0, half == 1)
                        mm.then_inc(half_used if half == 0 else proj_done, 1)
            sums("nf", KD)
            sums("conv", KD)
            with pe.Fori(0, CT) as i:
                for j in range(2):
                    pe.wait_ge(lo_done, 2 * i + (N_CIN + j + 1))
                    for m in range(2):
                        pe.wait_ge(evac[m], 2 * i + emptied(O_CIN + 2 * j + m))
                        products(pe, m, *hblock((N_CIN + j) % 2, KD, m), *hx, KD,
                                 ready=None if j or m else 24).then_inc(proj_done, 1)
            pe.wait_ge(ycl_ready, 1)
            with pe.Fori(0, 4) as i:
                for j in range(2):
                    n = N_COUT + j
                    pe.wait_ge(lo_done, 2 * i + (n + 1))
                    pe.wait_ge(evac[j], i + emptied(O_COUT + j))
                    products(pe, j, *hblock(n % 2, CT, 0), lambda k: yc_hi[:, k], lambda k: yc_lo[:, k], CT)\
                        .then_inc(proj_done, 1)
            sums("attn2", KD)
            pe.wait_ge(hl_ready, 40)
            pe.wait_ge(perm_in, 64)
            pe.wait_ge(d_ones, 2)

            def project(c, r, e):
                n, t = N_AIN + 5 * c + e // 2, O_AIN + 10 * c + e
                if e % 2 == 0:
                    pe.wait_ge(lo_done, 5 * r + (n + 1))
                pe.wait_ge(evac[e % 2], 5 * r + emptied(t))
                products(pe, e % 2, *hblock(n % 2, KD, e % 2), *hx, KD).then_inc(proj_done, 1)

            def head_sums(c, r, e):
                nth = 6 * c + e
                pe.wait_ge(d_sq, 6 * r + (nth + 1))
                if nth:
                    pe.wait_ge(d_std, 6 * r + nth)
                pe.matmul(bank[2][:, :], head_ones, sq[:, e % 2], start=True, stop=True).then_inc(d_sum, 1)

            def pair_scores(c, r, u):
                if u:
                    pe.wait_ge(d_max, 4 * r + (4 * c + u))
                for g, h, i, s0, n in unit_slots(u):
                    rows = slice(64 * h, 64 * h + 64)
                    q, k = qk[rows, c % 2, 2 * g], qk[rows, c % 2, 2 * g + 1]
                    k1 = P * (i + 1)
                    mm = pe.matmul(bank[4 + s0 // 4][:, P * (s0 % 4):P * (s0 % 4 + n)], q[:, P * i:P * i + P],
                                   k[:, k1 - P * n:k1], start=True, stop=True)
                mm.then_inc(d_scores, 1)

            def to_natural(c, r):
                pe.wait_ge(d_spread, 2 * r + (2 * c + 2))
                pe.wait_ge(d_vset, 3 * r + (3 * c + 3))
                for g in range(2):
                    for j in range(4):
                        mm = pe.matmul(bank[3][:, 8 * g:8 * g + 8], perm_f[:, g, j],
                                       cw[:, 32 * g + 8 * j:32 * g + 8 * j + 8], start=j == 0, stop=j == 3)
                mm.then_inc(d_natural, 1)

            def to_groups(c, r):
                pe.wait_ge(d_min, r + (c + 1))
                for g in range(2):
                    for j in range(4):
                        mm = pe.matmul(bank[3][:, 64 + 32 * g + 8 * j:72 + 32 * g + 8 * j], perm_b[:, g, j],
                                       cw[:, 88:96], start=True, stop=True)
                mm.then_inc(d_back, 1)

            def pair_turn(c, r, u):
                pe.wait_ge(d_exp, 4 * r + (4 * c + u + 1))
                if u:
                    pe.wait_ge(d_pt, 4 * r + (4 * c + u))
                for g, h, i, s0, n in unit_slots(u):
                    for s_ in range(s0, s0 + n):
                        mm = pe.transpose(bank[4 + s_ // 4][:, P * (s_ % 4):P * (s_ % 4) + P],
                                          sd_sb[:, u, P * s_:P * s_ + P], ident[:, :])
                mm.then_inc(d_turned, 1)

            def pair_values(c, r, u):
                pe.wait_ge(d_pt, 4 * r + (4 * c + u + 1))
                if u == 0:
                    pe.wait_ge(d_vset, 3 * r + (3 * c + 3))
                for g, h, i, s0, n in unit_slots(u):
                    acc = bank[6 + h][:, :]
                    if g == 0:
                        o = acc[:, P * i:P * i + P]
                    elif g == 1:
                        o = acc.rearrange("p (l r) -> p r l", r=4)[:, i]
                    else:
                        o = acc.rearrange("p (l r) -> p r l", r=16)[:, 4 * i:4 * i + 4]
                    for s_ in range(s0, s0 + n):
                        tile = i if s_ == s0 + n - 1 else i - 1
                        v = vv[:, c % 2, TT * g + tile, h:h + 2].rearrange("p a f -> p (a f)")
                        mm = pe.matmul(o, v, sd_sb[:, u, P * s_:P * s_ + P], start=g == 0 and i == 0,
                                       stop=g == 2 and i == 3, skip_group_check=True)
                mm.then_inc(d_pv, 1)

            def turn_v(c, r, g):
                pe.wait_ge(evac[g % 2], 5 * r + (emptied(O_AIN + 10 * c + 6 + g) + 1))
                if 3 * c + g:
                    pe.wait_ge(d_vset, 3 * r + (3 * c + g))
                if g == 0 and c:
                    pe.wait_ge(d_mperm, r + c)
                for i in range(TT):
                    mm = pe.transpose(bank[3][:, P * i:P * i + P], hf[:, 0, P * i:P * i + P], ident[:, :])
                mm.then_inc(d_vturned, 1)

            def pair_pe(att, nxt):
                for e in range(10):
                    if att and e < 4:
                        pair_scores(*att, e)
                    if att and e >= 8:
                        pair_turn(*att, e - 8)
                        turn_v(*nxt, e - 8) if nxt and e == 8 else None
                        if e == 9:
                            pair_values(*att, 0)
                            if nxt:
                                turn_v(*nxt, 1)
                    elif nxt and e >= 8:
                        turn_v(*nxt, e - 8)
                    if nxt:
                        project(*nxt, e)
                        if 1 <= e <= 6:
                            head_sums(*nxt, e - 1)
                    if att and e == 3:
                        to_natural(*att)
                    if att and e == 4:
                        to_groups(*att)
                if att:
                    pair_turn(*att, 2)
                    pair_values(*att, 1)
                if nxt:
                    turn_v(*nxt, 2)
                if att:
                    pair_turn(*att, 3)
                    pair_values(*att, 2)
                    pair_values(*att, 3)

            pair_pe(None, (0, 0))
            with pe.Fori(0, 3) as i:
                pair_pe((0, 2 * i), (1, 2 * i))
                pair_pe((1, 2 * i), (2, 2 * i))
            pair_pe((6, 0), (7, 0))
            pair_pe((7, 0), None)
            for k in range(KD):
                n = N_AOUT + k // 2
                if k % 2 == 0:
                    pe.wait_ge(lo_done, n + 1)
                pe.wait_ge(evac[k % 2], emptied(O_AOUT + k))
                if k == 0:
                    pe.wait_ge(hl_ready, 48)
                products(pe, k % 2, *hblock(n % 2, KD, k % 2), *hx, KD).then_inc(proj_done, 1)


def row_tiles(w):
    k, n = w.shape
    return w.reshape(k // P, P, n).transpose(1, 0, 2)


def chunks(w, cols_per):
    k, n = w.shape
    c = n // cols_per
    v = w.reshape(k // P, P, c, cols_per // P, P)
    return v.transpose(2, 1, 3, 0, 4).reshape(c, P, -1)


def col(v):
    return v.reshape(-1, P).T


def constants():
    c = {"ones": np.ones((P, P), np.float32), "ident": np.eye(P, dtype=np.float32)}
    rot = np.zeros((P, P), np.float32)
    for h in (0, 64):
        for j in range(32):
            rot[h + j, h + 32 + j] = -1.0
            rot[h + 32 + j, h + j] = 1.0
    dup = [np.zeros((P, P), np.float32) for _ in range(2)]
    for kv in range(2):
        for p in range(P):
            dup[kv][p, 64 * kv + p % 64] = 1.0
    c["ropem"] = np.stack([m.T for m in (rot, dup[0], dup[1], rot @ dup[0], rot @ dup[1])], axis=1)
    inv = np.power(np.float32(10000.0), -np.arange(32, dtype=np.float32) * np.float32(2.0) / np.float32(64))
    ang = np.arange(L, dtype=np.float32)[None, :] * inv.astype(np.float32)[np.arange(P) % 32][:, None]
    c["rope_cs"] = np.stack([np.cos(ang), np.sin(ang)], axis=1).astype(np.float32)
    q = np.arange(P)
    m = np.zeros((P, 512), np.float32)
    m[:, 384:] = np.where(q[None, :] <= q[:, None], 0.0, NEG)
    c["mask"] = m
    t = (np.arange(TT)[None, :] * P + q[:, None])[:, :, None]
    c["cmask"] = np.where(np.arange(NCMP)[None, None, :] * 16 + 31 <= t, 0.0, NEG).astype(np.float32)
    oh, vm = np.zeros((32, VTOT), np.float32), np.full((16, VTOT), NEG, np.float32)
    for g, (window, dil) in enumerate(GROUPS):
        far = 31 if g == 2 else 127 if g == 1 else 128
        zero = (255, 127, 31)[g]
        for s in range(far + 1):
            d = np.int32(s * dil)
            big = 16 + int(np.float32(np.log(np.float32(max(d, 1)) / np.float32(16)))
                           / np.float32(np.log(128.0)) * np.float32(16))
            oh[d if d < 16 else min(big, 31), VOFF[g] + zero - s] = 1.0
            vm[:, VOFF[g] + zero - s] = 0.0
    c["onehot"], c["vmask"] = oh, vm
    c["neg"] = np.full((P, P), NEG, np.float32)
    f = np.zeros((P, 2, 4, P), np.float32)
    pm = np.zeros((P, 2, 4), np.float32)
    for p in range(P):
        for i in range(4):
            for g, token in enumerate((4 * p + i, 16 * (p % 32) + 4 * i + p // 32)):
                f[p, g, i, token % P] = 1.0
                pm[p, g, token // P] = 1.0
    c["perm_f"], c["perm_b"], c["pmask"] = f, f.transpose(3, 1, 2, 0), pm
    c["head_ones"] = np.kron(np.eye(2), np.ones((64, 64))).astype(np.float32)
    return c


def kernel(x, c, norm1_g, norm2_g, normf_g, w_ada, b_ada, w_in, pe_k, pe_v, w_ck1, w_ck2, w_cv1, w_cv2,
           lam_re, lam_im, log_step, b_re, b_im, c_re, c_im, d_skip, w_glu, b_glu, attn_norm_g,
           ssm_norm_g, w_o, w_up, conv_w, conv_b, w_down, conv_norm_2, conv_w_in_2, conv_w_2,
           conv_w_out_2, attn_norm_2, attn_w_in_2, attn_q_gain_2, attn_k_gain_2, attn_w_out_2,
           rel_bias_2):
    import concourse.bacc as bacc
    from concourse.bass_utils import run_bass_kernel_spmd

    a = constants()
    a["x"] = row_tiles(x[0].T)
    a["c"] = col(c[0])
    a["b_ada"] = col(b_ada[0])
    a["gains"] = np.concatenate([col(v) for v in (
        norm1_g[0], norm2_g[0], normf_g, conv_norm_2[0], attn_norm_2[0],
        np.concatenate([attn_norm_g[0], ssm_norm_g[0]]), b_glu[0], d_skip[0].reshape(-1))], axis=1)
    w = w_in[0]
    at = np.cumsum([0, 512, 128, 128, 128, 128, 128, 128, 24, 512])
    q_, kc, vc, ks, vs, kw, vw, zg, zs = (w[:, at[i]:at[i + 1]] for i in range(9))
    w_in_c = np.concatenate([zs, kc, vc, q_, ks, vs, kw, vw, zg, np.zeros((D, 232), np.float32)], axis=1)
    up = w_up[0].reshape(D, 2, FT, P).transpose(0, 2, 1, 3).reshape(D, 2 * FT * P)
    a["w_a"] = np.concatenate([chunks(w_in_c, 256), chunks(w_glu[0], 512), chunks(w_o[0], 256),
                               chunks(up, 256)])
    a["w_d"] = np.concatenate([chunks(w_down[0][h * 1408:(h + 1) * 1408], P)[:, None] for h in range(2)], axis=1)\
        .reshape(16, P, NB_DOWN * P)
    order4 = conv_w_in_2[0].reshape(D, 4, CT, P)[:, [1, 2, 0, 3]].transpose(0, 2, 1, 3).reshape(D, 4 * CT * P)
    wq = attn_w_in_2[0][:, :9216].reshape(D, 3, 3, NPAIR, P)
    wz = attn_w_in_2[0][:, 9216:].reshape(D, NPAIR, P)
    pairs = np.stack([wq[:, 0, 0], wq[:, 0, 1], wq[:, 1, 0], wq[:, 1, 1], wq[:, 2, 0], wq[:, 2, 1],
                      wq[:, 0, 2], wq[:, 1, 2], wq[:, 2, 2], wz], axis=2).reshape(D, NPAIR * 10 * P)
    a["w_b"] = np.concatenate([chunks(order4, 256), chunks(conv_w_out_2[0], P), chunks(pairs, 256),
                               chunks(attn_w_out_2[0], 256)])
    a["tabs"] = rel_bias_2
    ck = [chunks(m[0][1024 * i:1024 * i + 1024], P) for m in (w_ck1, w_cv1) for i in range(2)]
    ada = chunks(w_ada[0], P)
    a["w32"] = np.concatenate([ada[:16]] + ck + [ada[16:]])
    a["pe_t"] = np.stack([np.tile(pe[0].T, (2, 1)) for pe in (pe_k, pe_v)], axis=1)
    a["w_c2"] = row_tiles(np.concatenate([w_ck2[0]] * 2, axis=1))
    a["w_v2"] = row_tiles(w_cv2[0])
    a["s5c"] = np.stack([lam_re[0].reshape(16, P).T, lam_im[0].reshape(16, P).T,
                         np.repeat(log_step[0], 64).reshape(16, P).T], axis=1)
    bs = np.zeros((P, 2, 4, P), np.float32)
    for i, b in enumerate((b_re, b_im)):
        for g in range(32):
            zt, r = g // 8, 16 * (g % 8)
            bs[r:r + 16, i, zt, 64 * (g % 2):64 * (g % 2) + 64] = b[0, g].T
    a["b_s5"] = bs
    a["c_s5"] = np.stack([m[0].transpose(0, 2, 1).reshape(16, P, 16).transpose(1, 0, 2) for m in (c_re, c_im)], axis=1)
    a["conv_wb"] = np.stack([col(conv_w[0, i]) for i in range(3)] + [col(conv_b[0])], axis=1)
    a["conv2_w"] = np.stack([col(conv_w_2[0, i]) for i in range(3)], axis=1)
    a["qk_gain"] = np.stack([np.tile(g[0, i], 2) for i in range(3) for g in (attn_q_gain_2, attn_k_gain_2)], axis=1)

    nc = bacc.Bacc("TRN2", target_bir_lowering=False, num_devices=1)
    arrays, aps = {}, {}
    for name, v in a.items():
        v = np.ascontiguousarray(v)
        arrays["in_" + name] = v
        aps[name] = nc.dram_tensor("in_" + name, v.shape, F32, kind="ExternalInput").ap()
    out = nc.dram_tensor("out_x", (P, KD, L), F32, kind="ExternalOutput").ap()
    build(nc, aps, out)
    r = run_bass_kernel_spmd(nc, [arrays], core_ids=[0]).results[0]["out_x"]
    return np.ascontiguousarray(r.transpose(1, 0, 2).reshape(D, L).T)[None]
```

```python
from contextlib import ExitStack

import numpy as np

import concourse.bass as bass
from concourse import mybir

P = 128
D = 1024
L = 512
KD = D // P
TT = L // P
HD = 64
NEG = -1.0e30
NCMP = (L - 32) // 16 + 1
FT = 2816 // P
CT = 2048 // P
NPAIR = 8
CH = 2048

T_ZS, T_KC, T_VC, T_Q, T_KS, T_VS, T_KW, T_VW, T_ZG = 0, 4, 5, 6, 10, 11, 12, 13, 14

N_IN, N_GLU, N_O, N_UP, N_DOWN, N_CIN, N_COUT, N_AIN, N_AOUT, N_ALL = 0, 8, 9, 13, 35, 51, 83, 91, 131, 135
PAIR_STEPS = 6 + 1 + 2 + 5 + 4
K_EARLY = 6
NB_DOWN = FT // 2

O_IN, O_GLU, O_O, O_UP, O_DOWN, O_CIN, O_COUT, O_AIN, O_AOUT = 0, 16, 20, 28, 72, 80, 144, 152, 232

F32 = mybir.dt.float32
F32R = mybir.dt.float32r
ACT = mybir.ActivationFunctionType
ALU = mybir.AluOpType
AX = mybir.AxisListType
PI = float(np.pi)

GROUPS = ((128, 1), (512, 4), (2048, 16))
VLEN = (384, 256, 64)
VOFF = (0, 384, 640)
VTOT = 704


class Count:

    def __init__(self, sem):
        self.sem, self.n, self.turns = sem, 0, 0

    def inc(self, ins):
        ins.then_inc(self.sem, 1)
        self.n += 1

    def wait(self, eng):
        eng.wait_ge(self.sem, self.n + self.turns)

    def loop(self, i, per):
        self.turns, self.per, self.start = i * per, per, self.n

    def leave(self, trips):
        assert self.n == self.start + self.per, (self.n - self.start, self.per)
        self.turns, self.n = 0, self.start + self.per * trips


def done_after(n, r=0):
    if n < 7:
        return 2 * n + 2 + 2 * r
    if n < N_O:
        return 15 if n == 7 else 19
    if n < N_DOWN:
        return 21 + 2 * (n - N_O + r)
    if n < N_CIN:
        return O_DOWN + (n - N_DOWN) // 2 + r // 2
    if n < N_COUT:
        return O_CIN + 1 + 2 * (n - N_CIN + r)
    if n < N_AIN:
        return O_COUT + n - N_COUT + r
    return O_AIN + 1 + 2 * (n - N_AIN + r)


def emptied(t, half=0):
    return t // 2 - (1 if t % 2 and t > 15 else 0) + half


def unit_slots(u):
    if u < 2:
        return [(0, u, i, 2 * i if i else 1, 2 if i else 1) for i in range(TT)]
    return [(u - 1, h, i, 4 * h + i, 1) for h in range(2) for i in range(TT)]


def build(nc, A, out):
    es = ExitStack()
    with es:
        def sem(name):
            return es.enter_context(nc.semaphore(name))

        def sb(scope, name, shape, dt=F32):
            return scope.enter_context(nc.sbuf_tensor(name, shape, dt))

        bank = [es.enter_context(nc.psum_tensor(f"bank{i}", [P, 512], F32)) for i in range(8)]

        x = sb(es, "x", [P, KD, L])
        raw = sb(es, "raw", [P, 2, CH])
        w_hi = sb(es, "w_hi", [P, 2, CH], F32R)
        w_lo = sb(es, "w_lo", [P, 2, CH], F32R)
        sq = sb(es, "sq", [P, 2, L])
        hf = sb(es, "hf", [P, 2, L])
        std = sb(es, "std", [P, L])
        ones = sb(es, "ones", [P, P])
        ident = sb(es, "ident", [P, P])
        cols = sb(es, "cols", [P, 64])
        eps = cols[:, 0:1]
        gains = sb(es, "gains", [P, 56])
        mod = sb(es, "mod", [P, 48])
        b_ada = sb(es, "b_ada", [P, 48])
        conv_wb = sb(es, "conv_wb", [P, 4, 2 * FT])
        conv2_w = sb(es, "conv2_w", [P, 3, CT])
        qk_gain = sb(es, "qk_gain", [P, 6])

        early = ExitStack()
        s_sb = sb(early, "s_sb", [P, 1088])
        pt_s = sb(early, "pt_s", [P, 512])
        pt_w = sb(early, "pt_w", [P, 512])
        pt_c = sb(early, "pt_c", [P, P])
        hid = sb(early, "hid", [P, 2, 2, 62])
        kc_t = sb(early, "kc_t", [P, 62])
        vc_t = sb(early, "vc_t", [P, 2, HD])
        gates = sb(early, "gates", [P, TT, 24])
        early.close()
        first = ExitStack()
        w_ada = sb(first, "w_ada", [P, 2, 4, D])
        first.close()
        second = ExitStack()
        second.enter_context(nc.sbuf_tensor("beside", [P, KD, L], F32))
        w_cmp = sb(second, "w_cmp", [P, 4, KD * P])
        second.close()
        h_hi = sb(es, "h_hi", [P, KD, L], F32R)
        h_lo = sb(es, "h_lo", [P, KD, L], F32R)

        def w_mlp(r):
            return w_cmp[:, r - 2] if 2 <= r < 6 else r32[:, r % 2]

        sa = ExitStack()
        z = sb(sa, "z", [P, 15, L])
        r32 = sb(sa, "r32", [P, 2, KD * P])
        e_tab = sb(sa, "e_tab", [P, 2, 2, L])
        pool_t = sb(sa, "pool_t", [P, L])
        over = ExitStack()
        y_hi = sb(over, "y_hi", [P, 4, L], F32R)
        y_lo = sb(over, "y_lo", [P, 4, L], F32R)
        over.close()
        pq = sb(sa, "pq", [P, 8, L])
        scr8 = sb(sa, "scr8", [P, 2048])
        v_tok = sb(sa, "v_tok", [P, 2, TT, P])
        b_s5 = sb(sa, "b_s5", [P, 2, 4, P])
        c_s5 = sb(sa, "c_s5", [P, 3, 16, 32])
        b_tab = sb(sa, "b_tab", [P, 2, 16, 32])
        a_tab = sb(sa, "a_tab", [P, 2, 16, 16])
        s5c = sb(sa, "s5c", [P, 21, 16])
        mask = sb(sa, "mask", [P, 512])
        cmask = sb(sa, "cmask", [P, TT, NCMP])
        pe_t = sb(sa, "pe_t", [P, 2, 32])
        w_c2 = sb(sa, "w_c2", [P, 2, P])
        w_v2 = sb(sa, "w_v2", [P, 2, HD])
        small = sb(sa, "small", [P, 64])
        sa.close()

        c_sil = [e_tab[:, 0].rearrange("p a b -> p (a b)"), sq[:, :, :].rearrange("p a b -> p (a b)")]

        onehot = z[0:32, 0:2].rearrange("p a b -> p (a b)")[:, 0:VTOT]
        vmask = z[0:16, 2:4].rearrange("p a b -> p (a b)")[:, 0:VTOT]
        vec = z[0:16, 6:8].rearrange("p a b -> p (a b)")[:, 0:VTOT]
        tabs = z[0:32, 4, 0:48]

        sf = ExitStack()
        act_hi = sb(sf, "act_hi", [P, FT, L], F32R)
        act_lo = sb(sf, "act_lo", [P, FT, L], F32R)
        up_av = sb(sf, "up_av", [P, 2, L])
        cv_av = sb(sf, "cv_av", [P, 2, L])
        sf.close()

        sc_ = ExitStack()
        yc_hi = sb(sc_, "yc_hi", [P, CT, L], F32R)
        yc_lo = sb(sc_, "yc_lo", [P, CT, L], F32R)
        cg = sb(sc_, "cg", [P, L])
        cu = sb(sc_, "cu", [P, L + 2])
        cacc = sb(sc_, "cacc", [P, L])
        csil = sb(sc_, "csil", [P, L])
        sc_.close()

        sd = ExitStack()
        qk = sb(sd, "qk", [P, 2, 6, L])
        vv = sb(sd, "vv", [P, 2, 3 * TT, 3, HD])
        zg = sb(sd, "zg", [P, 2, L])
        bias = sb(sd, "bias", [P, 2, 512])
        rawd = sb(sd, "rawd", [P, 2, L])
        rden = sb(sd, "rden", [P, L])
        sd_sb = sb(sd, "sd_sb", [P, 4, 1024])
        yatt = sb(sd, "yatt", [P, NPAIR, L])
        perm_f = sb(sd, "perm_f", [P, 2, 4, P])
        perm_b = sb(sd, "perm_b", [P, 2, 4, P])
        head_ones = sb(sd, "head_ones", [P, P])[:, :]
        sd.close()

        cw = conv_wb[:, :, :].rearrange("p a b -> p (a b)")
        spread = cw[:, 0:64].rearrange("p (g r i h) -> p g r i h", g=2, r=4, i=4)
        stat = cw[:, 64:88].rearrange("p (g i h) -> p g i h", g=3, i=4)
        mnat = cw[:, 88:96].rearrange("p (i h) -> p i h", i=4)
        mperm = cw[:, 96:112].rearrange("p (g r h) -> p g r h", g=2, r=4)
        pmask = cw[:, 112:120].rearrange("p (g i) -> p g i", g=2)
        stdd = (std[:, :], hf[:, 1])

        vec_dram = nc.dram_tensor("bias_vectors", (16, VTOT), F32, kind="Internal")
        bias_dram = nc.dram_tensor("bias_tiles", (16, P, 512), F32, kind="Internal")

        vec_in, vec_done, vec_ready, vec_out = sem("vec_in"), sem("vec_done"), sem("vec_ready"), sem("vec_out")
        bias_made, bias_in = sem("bias_made"), sem("bias_in")
        perm_in = sem("perm_in")
        dve_held = sem("dve_held")
        half_used = sem("half_used")
        conv_done, silu_done, af_ready, ah_ready = sem("conv_done"), sem("silu_done"), sem("af_ready"), sem("ah_ready")
        al_ready = sem("al_ready")
        xf_ready = sem("xf_ready")
        cu_zero = sem("cu_zero")
        yc_ready, ych_ready, ycl_ready = sem("yc_ready"), sem("ych_ready"), sem("ycl_ready")
        d_sq, d_sum, d_std, d_qk = sem("d_sq"), sem("d_sum"), sem("d_std"), sem("d_qk")
        d_scores, d_max, d_spread, d_natural, d_min, d_back, d_mperm = (
            sem("d_scores"), sem("d_max"), sem("d_spread"), sem("d_natural"), sem("d_min"), sem("d_back"),
            sem("d_mperm"))
        d_exp, d_turned, d_pt, d_pv = sem("d_exp"), sem("d_turned"), sem("d_pt"), sem("d_pv")
        d_vturned, d_vset, d_y, d_ones = sem("d_vturned"), sem("d_vset"), sem("d_y"), sem("d_ones")
        raw_in = [sem("raw_in0"), sem("raw_in1")]
        hi_done, lo_done = sem("hi_done"), sem("lo_done")
        r32_in = [sem("r32_in0"), sem("r32_in1")]
        cmp_in = sem("cmp_in")
        hid_done, hid_taken = sem("hid_done"), sem("hid_taken")
        ada_in = [sem("ada_in0"), sem("ada_in1")]
        r32_used = sem("r32_used")
        x_in, c_in_s = sem("x_in"), sem("c_in_s")
        gains_in, s5_in, attn_in = sem("gains_in"), sem("s5_in"), sem("attn_in")
        ones_in = sem("ones_in")
        eps_set = sem("eps_set")
        cs_ready = sem("cs_ready")
        sq_ready, sq_used, sums_done = sem("sq_ready"), sem("sq_used"), sem("sums_done")
        std_ready, rstd_ready = sem("std_ready"), sem("rstd_ready")
        mod_done = sem("mod_done")
        hf_ready, hh_ready, hl_ready = sem("hf_ready"), sem("hh_ready"), sem("hl_ready")
        proj_done = sem("proj_done")
        evac = [sem("evac0"), sem("evac1")]
        prep_done, prep_taken = sem("prep_done"), [sem("prep_taken0"), sem("prep_taken1")]
        dve_step, act_step, pool_step = sem("dve_step"), sem("act_step"), sem("pool_step")
        s5_act, s5_need, s5_tabs = sem("s5_act"), sem("s5_need"), sem("s5_tabs")
        states = sem("states")
        e_ready, bu_done, bu_taken = sem("e_ready"), sem("bu_done"), sem("bu_taken")
        back_done, cmul_done, y_ready, yg_ready = sem("back_done"), sem("cmul_done"), sem("y_ready"), sem("yg_ready")
        yh_ready, yl_ready, glu_ready, mixed = sem("yh_ready"), sem("yl_ready"), sem("glu_ready"), sem("mixed")
        roped, blocks_ready, hid_ready = sem("roped"), sem("blocks_ready"), sem("hid_ready")
        gates_ready = sem("gates_ready")
        scores_done, max_ready, exp_done = sem("scores_done"), sem("max_ready"), sem("exp_done")
        turned, turned_c, pt_dve, pt_act, pv_done, combined = (
            sem("turned"), sem("turned_c"), sem("pt_dve"), sem("pt_act"), sem("pv_done"), sem("combined"))
        osq, ostd, onorm, oturned = sem("osq"), sem("ostd"), sem("onorm"), sem("oturned")
        otaken = sem("otaken")
        out_sent = sem("out_sent")

        G = {n: gains[:, 8 * i:8 * i + 8] for i, n in enumerate(("n1", "n2", "nf", "conv", "attn2", "mix"))}
        BGLU, DSKIP = gains[:, 48:52], gains[:, 52:56]
        GS1, GS2 = cols[:, 8:16], cols[:, 16:24]
        SH1, SC1, GT1, SH2, SC2, GT2 = (mod[:, 8 * i:8 * i + 8] for i in range(6))
        (LR, LI, STEP, MAG, TH, TK, SIN, COS, ARE, AIM, DEN, NRE, FRE, FIM, T0, T1, PC, PS, PC2, PS2,
         TC) = (s5c[:, i] for i in range(21))

        B_SUM, B_MISC, B_PREP = 2, 3, (2, 7)
        B_BU, B_Y = (4, 5), 6
        SC = bank[B_MISC][:, 48:48 + NCMP]
        TC31 = bank[B_MISC][0:NCMP, 128:256]
        PV = bank[B_MISC][:, 256:448]

        fw, qq = pq[:, 0:4], pq[:, 4:8]
        o_tok = scr8[:, :].rearrange("p (t f) -> p t f", t=TT)
        rope_cs = pq[:, 0:2]
        ropem = pq[:, 2:4].rearrange("p a b -> p (a b)")[:, 0:5 * P].rearrange("p (m f) -> p m f", m=5)
        cosT, sinT = rope_cs[:, 0], rope_cs[:, 1]
        s5t = scr8[:, 0:768].rearrange("p (a b c) -> p a b c", a=3, b=16)
        c_in = scr8[:, 768:1280].rearrange("p (a b c) -> p a b c", a=2, b=16)
        blk = scr8[:, 0:1984].rearrange("p (v k n) -> p v k n", v=2, k=16)

        def products(pe, b, wh, wl, xh, xl, nk, first=True, last=True, ready=None):
            for k in range(nk):
                if ready is not None:
                    pe.wait_ge(hl_ready, ready + k + 1)
                pe.matmul(bank[b][:, :], wh(k), xh(k), start=first and k == 0, stop=False)
                pe.matmul(bank[b][:, :], wh(k), xl(k), start=False, stop=False)
                mm = pe.matmul(bank[b][:, :], wl(k), xh(k), start=False, stop=last and k == nk - 1)
            return mm

        def hblock(s, nk, m):
            return (lambda k: w_hi[:, s, (m * nk + k) * P:(m * nk + k + 1) * P],
                    lambda k: w_lo[:, s, (m * nk + k) * P:(m * nk + k + 1) * P])

        def make_blocks(eng, v, src):
            for j2 in range(2):
                for hh in range(2):
                    for c in range(2):
                        r = slice(64 * hh, 64 * hh + 64)
                        tok = src[r].rearrange("p (n j) -> p j n", j=16)[:, j2:16:2, c:c + NCMP]
                        pe_j = pe_t[r, v, 16 * c + j2:16 * c + 16:2].unsqueeze(2).broadcast_to([64, 8, NCMP])
                        eng.tensor_tensor(blk[64 * j2:64 * j2 + 64, v, 8 * c:8 * c + 8, 31 * hh:31 * hh + 31],
                                          tok, pe_j, ALU.add).then_inc(blocks_ready, 1)

        hx = (lambda k: h_hi[:, k], lambda k: h_lo[:, k])

        NORMS = {"n1": (0, 0, 0), "ssm": (8, 1, 8), "n2": (12, 2, 16), "nf": (20, 3, None), "conv": (28, 4, 24),
                 "attn2": (36, 5, 32)}

        block = es.enter_context(nc.Block())

        @block.sync
        def _(sp):
            sp.dma_start(c_sil[0], bass.AP(A["c"].tensor, 0, [[0, P], [1, D]])).then_inc(c_in_s, 16)

            def load32(r, s=None, i=None):
                if 2 <= r < 4:
                    sp.wait_ge(r32_used, r - 1)
                elif 4 <= r < 6:
                    sp.wait_ge(r32_used, r + 3)
                elif r >= 6:
                    sp.wait_ge(mod_done, r + 11)
                src = A["w32"][r if r < 2 else r + 4] if r < 4 else A["w_ada"][r + 12]
                sp.dma_start(r32[:, r % 2], src).then_inc(r32_in[r % 2], 16)

            def load_ada(g):
                if g >= 2:
                    sp.wait_ge(mod_done, 4 * (g - 1))
                sp.dma_start(w_ada[:, g % 2], A["w_ada"][4 * g:4 * g + 4].rearrange("t p k -> p t k"))\
                  .then_inc(ada_in[g % 2], 16)

            def load(n):
                if n >= 2:
                    sp.wait_ge(lo_done, n - 1)
                sp.dma_start(raw[:, n % 2], A["w_a"][n]).then_inc(raw_in[n % 2], 16)

            load_ada(0)
            load_ada(1)
            sp.dma_start(ones[:, :], A["ones"]).then_inc(ones_in, 16)
            sp.dma_start(x[:, :, :], A["x"]).then_inc(x_in, 16)
            sp.dma_start(onehot, A["onehot"]).then_inc(vec_in, 16)
            sp.dma_start(vmask, A["vmask"]).then_inc(vec_in, 16)
            sp.dma_start(tabs, A["tabs"]).then_inc(vec_in, 16)
            sp.dma_start(gains[:, :], A["gains"]).then_inc(gains_in, 16)
            sp.dma_start(b_ada[:, :], A["b_ada"]).then_inc(gains_in, 16)
            load_ada(2)
            load_ada(3)
            load(0)
            load(1)
            sp.dma_start(s5c[:, 0:3], A["s5c"]).then_inc(s5_in, 16)
            sp.dma_start(b_s5[:, :, :, :], A["b_s5"]).then_inc(s5_in, 16)
            sp.dma_start(c_in[:, :, :, :], A["c_s5"]).then_inc(s5_in, 16)
            sp.wait_ge(vec_ready, 2)
            sp.dma_start(vec_dram.ap(), vec).then_inc(vec_out, 16)
            for dst, name in ((ident[:, :], "ident"), (ropem[:, :, :], "ropem"), (rope_cs[:, :, :], "rope_cs"),
                              (mask[:, :], "mask"), (cmask[:, :, :], "cmask"), (pe_t[:, :, :], "pe_t"),
                              (w_c2[:, :, :], "w_c2"), (w_v2[:, :, :], "w_v2"),
                              (conv_wb[:, :, :], "conv_wb"), (conv2_w[:, :, :], "conv2_w"),
                              (qk_gain[:, :], "qk_gain")):
                sp.dma_start(dst, A[name]).then_inc(attn_in, 16)
            for n in range(2, 8):
                load(n)
            load32(0)
            load32(1)
            load(8)
            sp.wait_ge(proj_done, 15)
            sp.dma_start(w_cmp[:, :, :], A["w32"][2:6].rearrange("t p k -> p t k")).then_inc(cmp_in, 16)
            load(9)
            for r in range(2, 36):
                load32(r)
            sp.dma_start(bias_dram.ap()[:, :, 384:512].rearrange("h a k -> a h k"),
                         bass.AP(A["neg"].tensor, 0, [[P, P], [0, 16], [1, P]])).then_inc(vec_out, 16)
            sp.wait_ge(vec_out, 32)
            for off, c0, w in ((127, 0, 256), (VOFF[1] + 127, 256, 128)):
                sp.dma_start(bias_dram.ap()[:, :, c0:c0 + w],
                             bass.AP(vec_dram, off, [[VTOT, 16], [-1, P], [1, w]])).then_inc(bias_made, 16)
            for j in range(4):
                sp.dma_start(bias_dram.ap()[:, 32 * j:32 * j + 32, 384 + 32 * j:416 + 32 * j],
                             bass.AP(vec_dram, VOFF[2] + 31, [[VTOT, 16], [-1, 32], [1, 32]])).then_inc(bias_made, 16)
            for n in range(10, N_UP):
                load(n)

            def load_in(n, i, src, w=CH):
                sp.wait_ge(lo_done, 2 * i + (n - 1))
                sp.dma_start(raw[:, n % 2, 0:w], src).then_inc(raw_in[n % 2], 16)

            with sp.Fori(0, (N_DOWN - N_UP) // 2) as i:
                for j in range(2):
                    load_in(N_UP + j, i, A["w_a"][bass.ds(2 * i + (N_UP + j), 1)].rearrange("a p k -> (a p) k"))
            with sp.Fori(0, (N_CIN - N_DOWN) // 2) as i:
                for j in range(2):
                    load_in(N_DOWN + j, i, A["w_d"][bass.ds(2 * i + j, 1)].rearrange("a p k -> (a p) k"),
                            NB_DOWN * P)
            with sp.Fori(0, (N_AIN - N_CIN) // 2) as i:
                for j in range(2):
                    load_in(N_CIN + j, i, A["w_b"][bass.ds(2 * i + j, 1)].rearrange("a p k -> (a p) k"))
            load_in(N_AIN, 0, A["w_b"][N_AIN - N_CIN])
            load_in(N_AIN + 1, 0, A["w_b"][N_AIN + 1 - N_CIN])
            sp.wait_ge(proj_done, done_after(N_AIN - 1))
            for dst, name in ((perm_f[:, :, :, :], "perm_f"), (perm_b[:, :, :, :], "perm_b"),
                              (pmask, "pmask"), (head_ones, "head_ones")):
                sp.dma_start(dst, A[name]).then_inc(perm_in, 16)
            sp.wait_ge(bias_made, 16 * 6)

            def load_bias(c, r):
                if c:
                    sp.wait_ge(d_max, 4 * r + 4 * c)
                sp.dma_start(bias[:, :, :], bias_dram.ap()[bass.ds(2 * r + 2 * c, 2)].rearrange("h a k -> a h k"))\
                  .then_inc(bias_in, 16)

            load_bias(0, 0)
            for n in range(N_AIN + 2, N_AIN + 5):
                load_in(n, 0, A["w_b"][n - N_CIN])
            with sp.Fori(0, 3) as i:
                for j in range(10):
                    n = N_AIN + 5 + j
                    sp.wait_ge(lo_done, 10 * i + (n - 1))
                    sp.dma_start(raw[:, n % 2], A["w_b"][bass.ds(10 * i + (n - N_CIN), 1)].rearrange("a p k -> (a p) k"))\
                      .then_inc(raw_in[n % 2], 16)
                    if j % 5 == 3:
                        load_bias(1 + j // 5, 2 * i)
            for n in range(N_AIN + 35, N_ALL):
                load_in(n, 0, A["w_b"][n - N_CIN])
                if n == N_AIN + 38:
                    load_bias(7, 0)
            for k in range(KD):
                sp.wait_ge(evac[k % 2], emptied(O_AOUT + k) + 1)
                sp.dma_start(out[:, k], x[:, k]).then_inc(out_sent, 16)
            sp.wait_ge(out_sent, 16 * KD)

        @block.scalar
        def _(act):
            def hi(n, r=0):
                if n >= N_ALL:
                    return
                act.wait_ge(raw_in[n % 2], 8 * r + 16 * (n // 2 + 1))
                o = n - 2
                if N_DOWN <= o < N_CIN and (o - N_DOWN) % 2 == 0:
                    act.wait_ge(half_used, r // 2 + (o - N_DOWN) // 2 + 1)
                elif o >= 0:
                    act.wait_ge(proj_done, done_after(o, r))
                act.activation(w_hi[:, n % 2], raw[:, n % 2], ACT.Copy).then_inc(hi_done, 1)

            def squares(name, src, nk, ready=None):
                q0, m, _ = NORMS[name]
                act.activation(cols[:, 24 + m:25 + m], eps, ACT.Sqrt)
                for k in range(nk):
                    if ready:
                        ready(k)
                    if q0 + k >= 2:
                        act.wait_ge(sq_used, q0 + k - 1)
                    act.activation(sq[:, (q0 + k) % 2], src(k), ACT.Square).then_inc(sq_ready, 1)

            def root(name, width):
                m = NORMS[name][1]
                act.wait_ge(sums_done, m + 1)
                if m:
                    act.wait_ge(rstd_ready, m)
                act.activation(std[:, :], bank[B_SUM][:, :], ACT.Sqrt, bias=eps,
                               scale=1.0 / width).then_inc(std_ready, 1)

            def high_h(g, k, shift=None):
                act.wait_ge(hf_ready, g + 1)
                if shift is None:
                    ins = act.activation(h_hi[:, k], hf[:, g % 2], ACT.Copy)
                else:
                    ins = act.activation(h_hi[:, k], hf[:, g % 2], ACT.Identity, bias=shift[:, k:k + 1])
                ins.then_inc(hh_ready, 1)

            def highs(name, shift=None):
                for k in range(KD):
                    high_h(NORMS[name][2] + k, k, shift)

            act.wait_ge(c_in_s, 16)
            act.activation(c_sil[0], c_sil[0], ACT.Silu).then_inc(cs_ready, 1)
            act.wait_ge(x_in, 16)
            act.wait_ge(eps_set, 1)
            squares("n1", lambda k: x[:, k], KD)
            root("n1", D)
            act.wait_ge(cs_ready, 1)
            act.activation(c_sil[1], c_sil[0], ACT.Copy).then_inc(cs_ready, 1)
            hi(0)
            hi(1)
            highs("n1", SH1)
            for t in range(15):
                act.wait_ge(proj_done, t + 1)
                if t == 6:
                    act.wait_ge(vec_out, 16)
                act.activation(z[:, t], bank[t % 2][:, :], ACT.Copy).then_inc(evac[t % 2], 1)
                if t % 2:
                    hi(t // 2 + 2)
                if t == 0:
                    act.wait_ge(s5_in, 48)
                    act.activation(STEP, STEP, ACT.Exp).then_inc(s5_act, 1)
                if t == 1:
                    act.wait_ge(s5_need, 1)
                    act.activation(MAG, T0, ACT.Exp).then_inc(s5_act, 1)
                if t == 3:
                    act.wait_ge(s5_need, 2)
                    act.activation(SIN, TH, ACT.Sin).then_inc(s5_act, 1)
                    act.activation(COS, TC, ACT.Sin).then_inc(s5_act, 1)
            for s in (1, 2):
                act.wait_ge(prep_done, s + 1)
                act.activation(v_tok[:, s - 1], bank[B_PREP[s % 2]][:, :].rearrange("p (t f) -> p t f", t=TT), ACT.Copy)\
                   .then_inc(prep_taken[s % 2], 1)
            act.wait_ge(prep_done, 4)
            act.wait_ge(prep_taken[1], 1)
            act.activation(gates[:, :, :], bank[7][:, :].rearrange("p (t f) -> p t f", t=TT)[:, :, 0:24],
                           ACT.Sigmoid).then_inc(prep_taken[1], 1)
            for s in range(2):
                act.wait_ge(hid_done, 1 + s)
                act.activation(hid[:, s], bank[B_BU[s]][:, 0:124].rearrange("p (h n) -> p h n", h=2),
                               ACT.Gelu_apprx_tanh).then_inc(hid_taken, 1)

            for u in range(33):
                if u:
                    kw = P * ((u - 1) // 8 + 1)
                    act.wait_ge(turned, u)
                    if u >= 2:
                        act.wait_ge(pv_done, u - 1)
                    act.activation(pt_w[:, 0:kw], bank[7][:, 0:kw], ACT.Copy).then_inc(pt_act, 1)
                    act.wait_ge(turned_c, u)
                    act.activation(pt_c[0:NCMP, :], TC31, ACT.Copy).then_inc(pt_act, 1)
                if u < 32:
                    i = u // 8
                    kw = P * (i + 1)
                    den = small[:, 8 * (u % 2):8 * (u % 2) + 3]
                    nmx = small[:, 8 * (u % 2) + 4:8 * (u % 2) + 7]
                    act.wait_ge(max_ready, 3 * u + 3)
                    if u >= 2:
                        act.wait_ge(combined, u - 1)
                    for b, (c0, w) in enumerate(((1024 + 32 * (u % 2), NCMP), (0, kw), (512, kw))):
                        act.activation(s_sb[:, c0:c0 + w], s_sb[:, c0:c0 + w], ACT.Exp, bias=nmx[:, b:b + 1],
                                       scale=-1.0, accum_out=den[:, b:b + 1]).then_inc(exp_done, 1)
                if u in (10, 18, 26, 32):
                    zt = (u - 1) // 8 if u == 32 else u // 8 - 1
                    act.wait_ge(y_ready, zt + 1)
                    act.activation(z[:, zt], z[:, zt], ACT.Gelu_apprx_tanh).then_inc(yg_ready, 1)
            act.wait_ge(mod_done, 48)
            act.wait_ge(combined, 32)
            for i in range(TT):
                if i:
                    act.wait_ge(osq, i)
                act.activation(sq[:, 0], o_tok[:, i], ACT.Square, accum_out=small[:, 16 + i:17 + i]).then_inc(osq, 1)
            act.wait_ge(osq, 4)
            act.activation(small[:, 20:24], small[:, 16:20], ACT.Sqrt, bias=eps, scale=1.0 / 512).then_inc(ostd, 1)
            hi(9)
            act.wait_ge(cmul_done, 16)
            for m in range(4):
                act.wait_ge(yg_ready, m + 1)
                act.activation(y_hi[:, m], z[:, m], ACT.Copy).then_inc(yh_ready, 1)
            for m in range(4):
                high_h(8 + m, m)
            for m in range(4):
                t = O_GLU + m
                act.wait_ge(proj_done, t)
                act.activation(pool_t[:, :] if m % 2 else e_tab[:, 0, 0], bank[t % 2][:, :], ACT.Sigmoid,
                               bias=BGLU[:, m:m + 1]).then_inc(evac[t % 2], 1)
                act.wait_ge(mixed, m + 1)
            hi(10)
            squares("ssm", lambda k: z[:, k], 4)
            root("ssm", 512)
            for m in range(4):
                high_h(12 + m, 4 + m)
            for n in range(N_O, N_UP):
                act.wait_ge(proj_done, done_after(n))
                hi(n + 2)

            def rehigh(name, ready):
                squares(name, lambda k: x[:, k], KD, ready)
                root(name, D)

            def x_ready(o):
                return lambda k: act.wait_ge(evac[k % 2], emptied(o + k) + 1)

            rehigh("n2", x_ready(O_O))
            highs("n2", SH2)
            with act.Fori(0, FT // 2) as i:
                for j in range(2):
                    n, t = N_UP + j, O_UP + 2 * j
                    for m in range(2):
                        act.wait_ge(proj_done, 4 * i + (t + m))
                        act.activation(up_av[:, m], bank[m][:, :], ACT.Copy).then_inc(evac[m], 1)
                    if j == 0:
                        hi(n + 2, 2 * i)
                    act.wait_ge(conv_done, 4 * i + (2 * j + 1))
                    act.activation(cv_av[:, 0], cv_av[:, 0], ACT.Silu).then_inc(silu_done, 1)
                    if j == 1:
                        hi(n + 2, 2 * i)
                    act.wait_ge(af_ready, 2 * i + (j + 1))
                    act.activation(act_hi[:, bass.ds(2 * i + j, 1)].rearrange("p a l -> p (a l)"), cv_av[:, 0],
                                   ACT.Copy).then_inc(ah_ready, 1)
            with act.Fori(0, 4) as i:
                for j in range(4):
                    n = N_DOWN + j
                    if j % 2:
                        act.wait_ge(proj_done, 2 * i + (O_DOWN + j // 2))
                    else:
                        act.wait_ge(half_used, 2 * i + (j // 2 + 1))
                    hi(n + 2, 4 * i)
            rehigh("nf", x_ready(O_DOWN))
            rehigh("conv", lambda k: act.wait_ge(xf_ready, k + 1))
            highs("conv")
            with act.Fori(0, CT) as i:
                t = O_CIN
                act.wait_ge(proj_done, 4 * i + t)
                act.activation(cg[:, :], bank[0][:, :], ACT.Copy).then_inc(evac[0], 1)
                act.wait_ge(proj_done, 4 * i + (t + 1))
                hi(N_CIN + 2, 2 * i)
                act.wait_ge(proj_done, 4 * i + (t + 3))
                act.activation(csil[:, :], bank[1][:, :], ACT.Silu).then_inc(evac[1], 1)
                hi(N_CIN + 3, 2 * i)
                act.wait_ge(yc_ready, i + 1)
                act.activation(yc_hi[:, bass.ds(i, 1)].rearrange("p a l -> p (a l)"), cacc[:, :],
                               ACT.Copy).then_inc(ych_ready, 1)
            for n in range(N_COUT, N_AIN):
                act.wait_ge(proj_done, done_after(n))
                hi(n + 2)
            rehigh("attn2", x_ready(O_COUT))
            highs("attn2")

            def qk_evac(c, r, e):
                tile, nth = O_AIN + 10 * c + e, 6 * c + e
                act.wait_ge(proj_done, 10 * r + tile)
                if nth >= 2:
                    act.wait_ge(d_qk, 6 * r + (nth - 1))
                act.activation(rawd[:, e % 2], bank[e % 2][:, :], ACT.Copy).then_inc(evac[e % 2], 1)
                act.wait_ge(evac[e % 2], 5 * r + (emptied(tile) + 1))
                act.activation(sq[:, e % 2], rawd[:, e % 2], ACT.Square).then_inc(d_sq, 1)

            def qk_root(c, r, e):
                act.wait_ge(d_sum, 6 * r + (6 * c + e + 1))
                act.activation(stdd[e % 2], bank[2][:, :], ACT.Sqrt, bias=eps, scale=1.0 / HD)\
                   .then_inc(d_std, 1)

            def v_evac(c, r, g):
                tile = O_AIN + 10 * c + 6 + g
                act.wait_ge(proj_done, 10 * r + tile)
                if 3 * c + g:
                    act.wait_ge(d_vturned, 3 * r + (3 * c + g))
                d = GROUPS[g][1]
                src, dst = bank[g % 2][:, :], hf[:, 0]
                if d > 1:
                    src = src.rearrange("p (l r) -> p l r", r=d)
                    dst = dst.rearrange("p (r l) -> p l r", r=d)
                act.activation(dst, src, ACT.Copy).then_inc(evac[g % 2], 1)

            def z_evac(c, r):
                act.wait_ge(proj_done, 10 * r + (O_AIN + 10 * c + 9))
                act.activation(zg[:, c % 2], bank[1][:, :], ACT.Silu).then_inc(evac[1], 1)

            def exps(c, r, u):
                act.wait_ge(d_mperm, r + (c + 1))
                slots = unit_slots(u)
                for k, (g, h, i, s0, n) in enumerate(slots):
                    m = mnat[:, i, h:h + 1] if g == 0 else mperm[:, g - 1, i, h:h + 1]
                    v = sd_sb[:, u, P * s0:P * (s0 + n)]
                    ins = act.activation(v, v, ACT.Exp, bias=m, scale=-1.0)
                ins.then_inc(d_exp, 1)

            def pair_act(att, nxt):
                if nxt:
                    c, r = nxt
                    n, rr = N_AIN + 5 * c, 5 * r
                    for e in range(6):
                        qk_evac(c, r, e)
                        if e % 2:
                            hi(n + e // 2 + 2, rr)
                        if e:
                            qk_root(c, r, e - 1)
                    v_evac(c, r, 0)
                    qk_root(c, r, 5)
                for u in range(4):
                    if att:
                        exps(*att, u)
                    if nxt and u < 2:
                        v_evac(c, r, 1 + u)
                    if nxt and u == 0:
                        hi(n + 5, rr)
                if nxt:
                    z_evac(c, r)
                    hi(n + 6, rr)

            pair_act(None, (0, 0))
            with act.Fori(0, 3) as i:
                pair_act((0, 2 * i), (1, 2 * i))
                pair_act((1, 2 * i), (2, 2 * i))
            pair_act((6, 0), (7, 0))

            def y_high(k):
                act.wait_ge(d_y, k + 1)
                act.activation(h_hi[:, k], yatt[:, k], ACT.Copy).then_inc(hh_ready, 1)

            for k in range(K_EARLY):
                y_high(k)
            pair_act((7, 0), None)
            for k in range(K_EARLY, KD):
                y_high(k)
            for n in range(N_AOUT, N_ALL):
                act.wait_ge(proj_done, done_after(n))
                hi(n + 2)

        @block.gpsimd
        def _(pool):
            def e_make(t):
                e = e_tab[:, t % 2]
                if t:
                    steps.wait(pool)
                else:
                    pool.wait_ge(blocks_ready, 16)
                    pool.wait_ge(s5_tabs, 1)
                    pool.wait_ge(mod_done, 16)
                    pool.wait_ge(cs_ready, 2)
                if t >= 2:
                    pool.wait_ge(back_done, 2 * (t - 1))
                sh = [P, 16, 32]

                def a_of(j):
                    return a_tab[:, j, t].unsqueeze(2).broadcast_to(sh)

                def b_of(j):
                    return b_tab[:, j, t].unsqueeze(1).broadcast_to(sh)

                def v(ap):
                    return ap.rearrange("p (a b) -> p a b", a=16)

                for j, (m0, m1, op) in enumerate((((0, 0), (1, 1), ALU.subtract), ((1, 0), (0, 1), ALU.add))):
                    pool.tensor_tensor(v(e[:, j]), a_of(m0[0]), b_of(m0[1]), ALU.mult)
                    steps.inc(pool.tensor_tensor(v(pool_t[:, :]), a_of(m1[0]), b_of(m1[1]), ALU.mult))
                    steps.wait(pool)
                    ins = pool.tensor_tensor(e[:, j], e[:, j], pool_t[:, :], op)
                    if j:
                        ins.then_inc(e_ready, 1)
                    else:
                        steps.inc(ins)
                        steps.wait(pool)
                pool.wait_ge(e_ready, t + 1)

            def s5_back(t):
                e = e_tab[:, t % 2]
                pool.wait_ge(states, 2 * t + 2)
                if t:
                    pool.wait_ge(cmul_done, t)
                for j in range(2):
                    src = fw[:, 2 * j + 1].unsqueeze(1).broadcast_to([P, 2, L])
                    pool.tensor_tensor(qq[:, 2 * j:2 * j + 2], e, src, ALU.mult).then_inc(back_done, 1)

            def lo(n, r=0):
                pool.wait_ge(hi_done, r + (n + 1))
                pool.tensor_tensor(w_lo[:, n % 2], raw[:, n % 2], w_hi[:, n % 2].bitcast(F32),
                                   ALU.subtract).then_inc(lo_done, 1)

            steps = Count(pool_step)
            pool.memset(eps, 1.0e-6).then_inc(eps_set, 1)
            for n in range(8):
                lo(n)
            pool.wait_ge(attn_in, 16 * 11)
            pool.wait_ge(evac[1], 3)
            pool.wait_ge(blocks_ready, 8)
            pool.wait_ge(s5_tabs, 1)
            make_blocks(pool, 1, z[:, T_VC])
            e_make(0)
            e_make(1)
            for t in range(16):
                s5_back(t)
                if t + 2 < 16:
                    e_make(t + 2)
            lo(8)
            with pool.Fori(0, (N_ALL - 9) // 2) as i:
                for j in range(2):
                    lo(9 + j, 2 * i)

        @block.vector
        def _(dve):
            steps = Count(dve_step)

            def step(ins):
                steps.inc(ins)
                steps.wait(dve)

            def tt(o, a, b, op):
                step(dve.tensor_tensor(o, a, b, op))

            def rstd(m):
                dve.wait_ge(std_ready, m + 1)
                dve.reciprocal(std[:, :], std[:, :]).then_inc(rstd_ready, 1)
                dve.wait_ge(rstd_ready, m + 1)

            def normed(g, src, gain):
                if g >= 2:
                    dve.wait_ge(hl_ready, g - 1)
                o = hf[:, g % 2]
                dve.scalar_tensor_tensor(o, src, gain, std[:, :], ALU.mult, ALU.mult).then_inc(hf_ready, 1)

            def low_h(g, k, shift=None):
                dve.wait_ge(hh_ready, g + 1)
                if shift is None:
                    ins = dve.tensor_tensor(h_lo[:, k], hf[:, g % 2], h_hi[:, k].bitcast(F32), ALU.subtract)
                else:
                    ins = dve.scalar_tensor_tensor(h_lo[:, k], hf[:, g % 2], shift[:, k:k + 1],
                                                   h_hi[:, k].bitcast(F32), ALU.add, ALU.subtract)
                ins.then_inc(hl_ready, 1)

            def mult(o, a, b): tt(o, a, b, ALU.mult)
            def add(o, a, b): tt(o, a, b, ALU.add)
            def sub(o, a, b): tt(o, a, b, ALU.subtract)

            def renorm(name, gain, shift=None):
                q, m, g0 = NORMS[name]
                if m:
                    rstd(m)
                normed(g0, x[:, 0], gain[:, 0:1])
                for k in range(KD):
                    if k > 1:
                        low_h(g0 + k - 1, k - 1, shift)
                    if k + 1 < KD:
                        normed(g0 + k + 1, x[:, k + 1], gain[:, k + 1:k + 2])
                    if k == 0:
                        low_h(g0, 0, shift)
                low_h(g0 + KD - 1, KD - 1, shift)

            dve.wait_ge(vec_in, 48)
            dve.wait_ge(vec_done, 1)
            dve.tensor_tensor(vec[:, 0:384], bank[4][0:16, 0:384], vmask[:, 0:384], ALU.add).then_inc(vec_ready, 1)
            dve.tensor_tensor(vec[:, 384:704], bank[5][0:16, 0:320], vmask[:, 384:704], ALU.add).then_inc(vec_ready, 1)
            def ada(j, w):
                dve.tensor_tensor_reduce(w, w, c_sil[j >= 16], 1.0, 0.0, ALU.mult, ALU.add, mod[:, j:j + 1])\
                   .then_inc(mod_done, 1)

            dve.wait_ge(cs_ready, 1)
            for j in range(16):
                if j % 4 == 0:
                    dve.wait_ge(ada_in[j // 4 % 2], 16 * (j // 8 + 1))
                ada(j, w_ada[:, j // 4 % 2, j % 4])
                if j == 11:
                    rstd(0)
            dve.wait_ge(gains_in, 32)
            dve.wait_ge(mod_done, 16)
            step(dve.tensor_tensor(mod[:, 0:16], mod[:, 0:16], b_ada[:, 0:16], ALU.add))
            step(dve.scalar_tensor_tensor(GS1, SC1, 1.0, G["n1"], ALU.add, ALU.mult))
            renorm("n1", GS1, SH1)
            dve.memset(s5t[:, 0], 0.0)
            dve.memset(c_s5[:, :, :, :], 0.0)
            dve.wait_ge(s5_act, 1)
            dve.wait_ge(s5_in, 48)
            dve.tensor_tensor(T0, LR, STEP, ALU.mult).then_inc(s5_need, 1)
            mult(TH, LI, STEP)
            step(dve.tensor_scalar(TK, TH, 1.0 / (2 * PI), 12582912.0, ALU.mult, ALU.add))
            step(dve.tensor_scalar(TK, TK, 12582912.0, None, ALU.subtract))
            step(dve.scalar_tensor_tensor(TH, TK, -6.28125, TH, ALU.mult, ALU.add))
            step(dve.scalar_tensor_tensor(TH, TK, -(2 * PI - 6.28125), TH, ALU.mult, ALU.add))
            step(dve.tensor_scalar(TH, TH, 3.1415925, -3.1415925, ALU.min, ALU.max))
            step(dve.tensor_scalar(TC, TH, PI / 2, None, ALU.is_gt))
            step(dve.scalar_tensor_tensor(TC, TC, -2 * PI, TH, ALU.mult, ALU.add))
            step(dve.tensor_scalar(TC, TC, PI / 2, None, ALU.add))
            dve.tensor_scalar(TC, TC, 3.1415925, -3.1415925, ALU.min, ALU.max).then_inc(s5_need, 1)
            dve.wait_ge(s5_act, 4)
            mult(ARE, MAG, COS)
            mult(AIM, MAG, SIN)
            mult(T0, LR, LR)
            mult(T1, LI, LI)
            add(DEN, T0, T1)
            step(dve.reciprocal(DEN, DEN))
            step(dve.tensor_scalar(NRE, ARE, -1.0, None, ALU.add))
            mult(T0, NRE, LR)
            mult(T1, AIM, LI)
            add(T0, T0, T1)
            mult(FRE, T0, DEN)
            mult(T0, AIM, LR)
            mult(T1, NRE, LI)
            sub(T0, T0, T1)
            mult(FIM, T0, DEN)
            fre, fim = (f.unsqueeze(2).broadcast_to([P, 16, 16]) for f in (FRE, FIM))
            mult(s5t[:, 0], c_in[:, 0], fre)
            mult(s5t[:, 1], c_in[:, 1], fim)
            sub(s5t[:, 0], s5t[:, 0], s5t[:, 1])
            mult(s5t[:, 1], c_in[:, 0], fim)
            mult(s5t[:, 2], c_in[:, 1], fre)
            add(s5t[:, 1], s5t[:, 1], s5t[:, 2])
            for g in range(2):
                r = slice(64 * g, 64 * g + 64)
                cc = slice(16 * g, 16 * g + 16)
                dve.tensor_copy(c_s5[r, 0, :, cc], s5t[r, 0])
                dve.tensor_scalar(c_s5[r, 1, :, cc], s5t[r, 0], -1.0, None, ALU.mult)
                step(dve.tensor_scalar(c_s5[r, 2, :, cc], s5t[r, 1], -1.0, None, ALU.mult))

            def square_power():
                mult(PC2, PC, PC)
                mult(T0, PS, PS)
                mult(PS2, PC, PS)
                sub(PC, PC2, T0)
                step(dve.tensor_scalar(PS, PS2, 2.0, None, ALU.mult))

            def grow(tab, count):
                dve.memset(tab[:, 0, :, 0:1], 1.0)
                step(dve.memset(tab[:, 1, :, 0:1], 0.0))
                m = 1
                while m < count:
                    pc, ps = (f.unsqueeze(2).broadcast_to([P, 16, m]) for f in (PC, PS))
                    oc, os_ = tab[:, 0, :, 0:m], tab[:, 1, :, 0:m]
                    nc_, ns = tab[:, 0, :, m:2 * m], tab[:, 1, :, m:2 * m]
                    tmp = s5t[:, 0, :, 0:m]
                    mult(nc_, oc, pc)
                    mult(tmp, os_, ps)
                    sub(nc_, nc_, tmp)
                    mult(ns, oc, ps)
                    mult(tmp, os_, pc)
                    add(ns, ns, tmp)
                    square_power()
                    m *= 2

            step(dve.tensor_copy(PC, COS))
            step(dve.tensor_copy(PS, SIN))
            grow(b_tab, 32)
            grow(a_tab, 16)
            dve.sem_inc(s5_tabs, 1)

            def rope(s_rot, s_dup, src, dst):
                dve.wait_ge(prep_done, max(s_rot, s_dup) + 1)
                ins = dve.tensor_tensor(hf[:, 0], bank[B_PREP[s_rot % 2]][:, :], sinT, ALU.mult)
                ins.then_inc(prep_taken[s_rot % 2], 1)
                if s_dup:
                    dve.tensor_tensor(dst, bank[B_PREP[1]][:, :], cosT, ALU.mult).then_inc(prep_taken[1], 1)
                    dve.wait_ge(prep_taken[1], s_dup // 2 + 1)
                else:
                    step(dve.tensor_tensor(dst, src, cosT, ALU.mult))
                dve.wait_ge(prep_taken[s_rot % 2], s_rot // 2 + 1)
                dve.tensor_tensor(dst, dst, hf[:, 0], ALU.add).then_inc(roped, 1)

            dve.wait_ge(attn_in, 16 * 11)
            dve.wait_ge(hh_ready, 8)
            dve.wait_ge(hl_ready, 8)
            dve.wait_ge(evac[0], 3)
            rope(0, 0, z[:, T_KC], z[:, T_KC])
            dve.wait_ge(roped, 1)
            dve.wait_ge(evac[1], 3)
            make_blocks(dve, 0, z[:, T_KC])
            for j in range(4):
                dve.wait_ge(roped, j + 1)
                rope(4 + j, 0, z[:, T_Q + j], z[:, T_Q + j])
            for j, dst in enumerate((T_VS, T_VW, T_KC, T_VC)):
                dve.wait_ge(roped, 5 + j)
                dve.wait_ge(blocks_ready, 16)
                rope(8 + 2 * j, 9 + 2 * j, None, z[:, dst])
            dve.wait_ge(prep_done, 17)
            dve.tensor_copy(kc_t[:, :], bank[2][:, 0:62]).then_inc(prep_taken[0], 1)
            dve.wait_ge(prep_done, 18)
            dve.tensor_copy(vc_t[0:NCMP, :, :], bank[7][0:NCMP, 0:128].rearrange("p (h f) -> p h f", h=2))\
               .then_inc(prep_taken[1], 1)

            def s5_turn(t):
                e = e_tab[:, t % 2]
                dve.wait_ge(e_ready, t + 1)
                dve.wait_ge(bu_done, t + 1)
                if t:
                    dve.wait_ge(back_done, 2 * t)
                for j in range(2):
                    src = bank[B_BU[j]][:, :].unsqueeze(1).broadcast_to([P, 2, L])
                    dve.tensor_tensor(fw[:, 2 * j:2 * j + 2], e, src, ALU.mult).then_inc(bu_taken, 1)

            def s5_scan(t):
                dve.wait_ge(bu_taken, 2 * t + 2)
                steps.inc(dve.tensor_tensor(fw[:, 0], fw[:, 0], fw[:, 3], ALU.add))
                step(dve.tensor_tensor(fw[:, 2], fw[:, 2], fw[:, 1], ALU.subtract))
                mag = MAG[:, t:t + 1].broadcast_to([P, L])
                for j in (0, 2):
                    dve.tensor_tensor_scan(fw[:, j + 1], mag, fw[:, j], 0.0, ALU.mult, ALU.add).then_inc(states, 1)

            def y_make(zt):
                dve.wait_ge(cmul_done, 4 * zt + 4)
                dve.scalar_tensor_tensor(z[:, zt], z[:, zt], DSKIP[:, zt:zt + 1], bank[B_Y][:, :],
                                         ALU.mult, ALU.add).then_inc(y_ready, 1)

            coef = small[:, 32:35]
            dve.wait_ge(cs_ready, 2)
            for u in range(33):
                if u:
                    h, i = (u - 1) % 8, (u - 1) // 8
                    kw = P * (i + 1)
                    den = small[:, 8 * ((u - 1) % 2):8 * ((u - 1) % 2) + 3]
                    dve.wait_ge(turned, u)
                    if u >= 2:
                        dve.wait_ge(pv_done, u - 1)
                    dve.tensor_copy(pt_s[:, 0:kw], bank[2][:, 0:kw]).then_inc(pt_dve, 1)
                if u < 32:
                    i = u // 8
                    kw = P * (i + 1)
                    nmx = small[:, 8 * (u % 2) + 4:8 * (u % 2) + 7]
                    dve.wait_ge(scores_done, u + 1)
                    for b, (src, m, c0, w) in enumerate((
                            (SC, cmask[:, i], 1024 + 32 * (u % 2), NCMP),
                            (bank[0][:, 0:kw], mask[:, 384 - P * i:512], 0, kw),
                            (bank[1][:, 0:kw], mask[:, 384 - P * i:512], 512, kw))):
                        dve.tensor_tensor_reduce(s_sb[:, c0:c0 + w], src, m, -HD ** -0.5, 1.0e28,
                                                 ALU.add, ALU.min, nmx[:, b:b + 1]).then_inc(max_ready, 1)
                if u:
                    h, i = (u - 1) % 8, (u - 1) // 8
                    dve.wait_ge(exp_done, 3 * u)
                    step(dve.tensor_scalar(den, den, 1.0e-30, None, ALU.max))
                    step(dve.reciprocal(den, den))
                    step(dve.tensor_tensor(coef, den, gates[:, i, 3 * h:3 * h + 3], ALU.mult))
                    o = o_tok[:, i, HD * h:HD * h + HD]
                    dve.wait_ge(r32_in[(u + 3) % 2], 16 * ((u + 3) // 2 + 1))
                    ada(15 + u, r32[:, (u + 3) % 2])
                    dve.wait_ge(pv_done, u)
                    step(dve.tensor_scalar(o, PV[:, 0:64], coef[:, 0:1], None, ALU.mult))
                    step(dve.scalar_tensor_tensor(o, PV[:, 64:128], coef[:, 1:2], o, ALU.mult, ALU.add))
                    dve.scalar_tensor_tensor(o, PV[:, 128:192], coef[:, 2:3], o, ALU.mult, ALU.add)\
                       .then_inc(combined, 1)
                if u in (10, 18, 26, 32):
                    y_make((u - 1) // 8 if u == 32 else u // 8 - 1)
                if u < 32:
                    if u % 2 == 0:
                        s5_turn(u // 2)
                    else:
                        s5_scan(u // 2)
            dve.wait_ge(mod_done, 48)
            step(dve.tensor_tensor(mod[:, 16:48], mod[:, 16:48], b_ada[:, 16:48], ALU.add))
            step(dve.scalar_tensor_tensor(GS2, SC2, 1.0, G["n2"], ALU.add, ALU.mult))
            dve.wait_ge(ostd, 1)
            step(dve.reciprocal(small[:, 24:28], small[:, 20:24]))
            dve.wait_ge(combined, 32)
            for i in range(TT):
                dve.tensor_scalar(o_tok[:, i], o_tok[:, i], small[:, 24 + i:25 + i], None, ALU.mult)\
                   .then_inc(onorm, 1)
            for m in range(4):
                dve.wait_ge(yh_ready, m + 1)
                dve.tensor_tensor(y_lo[:, m], z[:, m], y_hi[:, m].bitcast(F32), ALU.subtract).then_inc(yl_ready, 1)
            for m in range(4):
                g = 8 + m
                dve.wait_ge(oturned, m + 1)
                dve.wait_ge(hl_ready, g - 1)
                dve.tensor_scalar(hf[:, g % 2], bank[4 + m][:, :], G["mix"][:, m:m + 1], None, ALU.mult)\
                   .then_inc(hf_ready, 1)
                if m:
                    low_h(g - 1, m - 1)
            low_h(11, 3)
            for m in range(4):
                t = O_GLU + m
                dve.wait_ge(evac[t % 2], t // 2 + (0 if t % 2 else 1))
                dve.tensor_tensor(z[:, m], z[:, m], pool_t[:, :] if m % 2 else e_tab[:, 0, 0], ALU.mult)\
                   .then_inc(mixed, 1)
            dve.wait_ge(mixed, 4)
            rstd(1)
            for m in range(4):
                normed(12 + m, z[:, m], G["mix"][:, 4 + m:5 + m])
                if m:
                    low_h(11 + m, 3 + m)
            low_h(15, 7)
            for m in range(KD):
                t = O_O + m
                dve.wait_ge(proj_done, t)
                dve.scalar_tensor_tensor(x[:, m], bank[t % 2][:, :], GT1[:, m:m + 1], x[:, m], ALU.mult,
                                         ALU.add).then_inc(evac[t % 2], 1)

            renorm("n2", GS2, SH2)
            with dve.Fori(0, FT // 2) as i:
                steps.loop(i, 8)
                for j in range(2):
                    for m in range(2):
                        c = 2 * i + (j + FT * m)

                        def wb(k):
                            return conv_wb[:, k, bass.ds(c, 1)]

                        u, o = up_av[:, m], cv_av[:, m]
                        dve.wait_ge(evac[m], 2 * i + (emptied(O_UP + 2 * j + m) + 1))
                        step(dve.tensor_scalar(o, u, wb(2), wb(3), ALU.mult, ALU.add))
                        step(dve.scalar_tensor_tensor(o[:, 1:], u[:, 0:L - 1], wb(1), o[:, 1:], ALU.mult, ALU.add))
                        dve.scalar_tensor_tensor(o[:, 2:], u[:, 0:L - 2], wb(0), o[:, 2:], ALU.mult, ALU.add)\
                           .then_inc(conv_done, 1)
                    dve.wait_ge(silu_done, 2 * i + (j + 1))
                    dve.wait_ge(conv_done, 4 * i + (2 * j + 2))
                    dve.tensor_tensor(cv_av[:, 0], cv_av[:, 0], cv_av[:, 1], ALU.mult).then_inc(af_ready, 1)
                    dve.wait_ge(ah_ready, 2 * i + (j + 1))
                    at = bass.ds(2 * i + j, 1)
                    dve.tensor_tensor(act_lo[:, at].rearrange("p a l -> p (a l)"), cv_av[:, 0],
                                      act_hi[:, at].rearrange("p a l -> p (a l)").bitcast(F32),
                                      ALU.subtract).then_inc(al_ready, 1)
                    dve.wait_ge(al_ready, 2 * i + (j + 1))
            steps.leave(FT // 2)
            with dve.Fori(0, 4) as i:
                for j in range(2):
                    at = x[:, bass.ds(2 * i + j, 1)].rearrange("p a l -> p (a l)")
                    dve.wait_ge(proj_done, 2 * i + (O_DOWN + j))
                    dve.scalar_tensor_tensor(at, bank[j][:, :], mod[:, bass.ds(2 * i + (40 + j), 1)], at, ALU.mult,
                                             ALU.add).then_inc(evac[j], 1)
            for m in range(2):
                dve.wait_ge(evac[m], emptied(O_DOWN + 6 + m) + 1)
            rstd(3)
            for k in range(KD):
                dve.scalar_tensor_tensor(x[:, k], x[:, k], G["nf"][:, k:k + 1], std[:, :], ALU.mult, ALU.mult)\
                   .then_inc(xf_ready, 1)
            step(dve.memset(cu[:, 0:2], 0.0))
            dve.wait_ge(xf_ready, KD)
            renorm("conv", G["conv"])
            with dve.Fori(0, CT) as i:
                steps.loop(i, 4)

                def tap(k):
                    return conv2_w[:, k, bass.ds(i, 1)]

                t = O_CIN
                dve.wait_ge(proj_done, 4 * i + (t + 1))
                dve.wait_ge(evac[0], 2 * i + (emptied(t) + 1))
                dve.tensor_tensor(cu[:, 2:], cg[:, :], bank[1][:, :], ALU.mult).then_inc(evac[1], 1)
                dve.wait_ge(evac[1], 2 * i + (emptied(t + 1) + 1))
                step(dve.tensor_scalar(cacc[:, :], cu[:, 2:], tap(2), None, ALU.mult))
                step(dve.scalar_tensor_tensor(cacc[:, :], cu[:, 1:L + 1], tap(1), cacc[:, :], ALU.mult, ALU.add))
                step(dve.scalar_tensor_tensor(cacc[:, :], cu[:, 0:L], tap(0), cacc[:, :], ALU.mult, ALU.add))
                dve.wait_ge(proj_done, 4 * i + (t + 2))
                dve.tensor_tensor(cacc[:, :], cacc[:, :], bank[0][:, :], ALU.mult).then_inc(evac[0], 1)
                dve.wait_ge(evac[0], 2 * i + (emptied(t + 2) + 1))
                dve.wait_ge(evac[1], 2 * i + (emptied(t + 3) + 1))
                dve.tensor_tensor(cacc[:, :], cacc[:, :], csil[:, :], ALU.mult).then_inc(yc_ready, 1)
                dve.wait_ge(ych_ready, i + 1)
                at = bass.ds(i, 1)
                step(dve.tensor_tensor(yc_lo[:, at].rearrange("p a l -> p (a l)"), cacc[:, :],
                                       yc_hi[:, at].rearrange("p a l -> p (a l)").bitcast(F32), ALU.subtract))
            steps.leave(CT)
            dve.sem_inc(ycl_ready, 1)
            with dve.Fori(0, 4) as i:
                for j in range(2):
                    at = x[:, bass.ds(2 * i + j, 1)].rearrange("p a l -> p (a l)")
                    dve.wait_ge(proj_done, 2 * i + (O_COUT + j))
                    dve.tensor_tensor(at, bank[j][:, :], at, ALU.add).then_inc(evac[j], 1)
            for m in range(2):
                dve.wait_ge(evac[m], emptied(O_COUT + 6 + m) + 1)
            renorm("attn2", G["attn2"])

            for c in range(2):
                dve.memset(vv[:, c, :, 1], 1.0).then_inc(d_ones, 1)
            for g in range(3):
                step(dve.tensor_scalar(qk_gain[:, 2 * g:2 * g + 1], qk_gain[:, 2 * g:2 * g + 1], HD ** -0.5, None,
                                       ALU.mult))
            dve.wait_ge(perm_in, 64)

            def qk_make(c, r, e):
                nth = 6 * c + e
                d = GROUPS[e // 2][1]
                dst, a, b = qk[:, c % 2, e], rawd[:, e % 2], stdd[e % 2]
                dve.wait_ge(d_std, 6 * r + (nth + 1))
                step(dve.reciprocal(b, b))
                if d > 1:
                    dst = dst.rearrange("p (r l) -> p l r", r=d)
                    a = a.rearrange("p (l r) -> p l r", r=d)
                    b = b.rearrange("p (l r) -> p l r", r=d)
                dve.scalar_tensor_tensor(dst, a, qk_gain[:, e:e + 1], b, ALU.mult, ALU.mult).then_inc(d_qk, 1)

            def v_make(c, r, g):
                dve.wait_ge(d_vturned, 3 * r + (3 * c + g + 1))
                dve.tensor_copy(vv[:, c % 2, TT * g:TT * g + TT, 0:3:2],
                                bank[3][:, :].rearrange("p (i h f) -> p i h f", i=TT, h=2)).then_inc(d_vset, 1)

            def scores_in(c, r, u):
                dve.wait_ge(d_scores, 4 * r + (4 * c + u + 1))
                if u == 0:
                    dve.wait_ge(bias_in, 16 * r + 16 * (c + 1))
                dve.sem_inc(dve_held, 1)
                for g, h, i, s0, n in unit_slots(u):
                    src = bank[4 + s0 // 4][:, P * (s0 % 4):P * (s0 % 4 + n)]
                    b1 = (256, 384, 512)[g]
                    ins = dve.tensor_tensor_reduce(sd_sb[:, u, P * s0:P * (s0 + n)], src,
                                                   bias[:, h, b1 - P * n:b1], -1.0, 3.0e38, ALU.add, ALU.min,
                                                   stat[:, g, i, h:h + 1])
                ins.then_inc(d_max, 1)

            def spread_stats(c, r):
                dve.wait_ge(d_max, 4 * r + (4 * c + 4))
                for g in range(2):
                    a = stat[:, g + 1].unsqueeze(2).broadcast_to([P, 4, 4, 2])
                    m = pmask[:, g].unsqueeze(1).unsqueeze(3).broadcast_to([P, 4, 4, 2])
                    dve.tensor_tensor(spread[:, g], a, m, ALU.mult).then_inc(d_spread, 1)

            def least(c, r):
                dve.wait_ge(d_natural, r + (c + 1))
                nat = bank[3][:, 0:16].rearrange("p (g i h) -> p g i h", g=2, i=4)
                step(dve.tensor_tensor(mnat, stat[:, 0], nat[:, 0], ALU.min))
                dve.tensor_tensor(mnat, mnat, nat[:, 1], ALU.min).then_inc(d_min, 1)

            def least_back(c, r):
                dve.wait_ge(d_back, r + (c + 1))
                for g in range(2):
                    a = bank[3][:, 64 + 32 * g:96 + 32 * g].rearrange("p (r i h) -> p r i h", r=4, i=4)
                    m = pmask[:, g].unsqueeze(1).unsqueeze(3).broadcast_to([P, 4, 4, 2])
                    step(dve.tensor_tensor(spread[:, g], a, m, ALU.mult))
                dve.tensor_reduce(cw[:, 96:112].rearrange("p (a h) -> p a h", h=2),
                                  cw[:, 0:64].rearrange("p (a i h) -> p a h i", i=4, h=2),
                                  AX.X, ALU.add).then_inc(d_mperm, 1)

            def pt_copy(c, r, u):
                dve.wait_ge(d_turned, 4 * r + (4 * c + u + 1))
                lo_ = P if u < 2 else 0
                steps.inc(dve.tensor_copy(sd_sb[:, u, lo_:512], bank[4][:, lo_:512]))
                steps.wait(dve)
                dve.tensor_copy(sd_sb[:, u, 512:1024], bank[5][:, :]).then_inc(d_pt, 1)

            def finish(c, r):
                dve.wait_ge(d_pv, 4 * r + (4 * c + 4))
                y = yatt[:, bass.ds(r + c, 1)].rearrange("p a l -> p (a l)")
                rows = [slice(0, 64), slice(64, 128)]
                for h in range(2):
                    steps.inc(dve.tensor_copy(rden[rows[h], :], bank[6 + h][rows[1 - h], :]))
                steps.wait(dve)
                step(dve.reciprocal(rden[:, :], rden[:, :]))
                for h in range(2):
                    steps.inc(dve.tensor_tensor(y[rows[h], :], bank[6 + h][rows[h], :], rden[rows[h], :], ALU.mult))
                steps.wait(dve)
                dve.tensor_tensor(y, y, zg[:, c % 2], ALU.mult).then_inc(d_y, 1)

            def y_low(k):
                dve.wait_ge(hh_ready, 40 + k + 1)
                dve.tensor_tensor(h_lo[:, k], yatt[:, k], h_hi[:, k].bitcast(F32), ALU.subtract)\
                   .then_inc(hl_ready, 1)

            def pair_dve(prev, att, nxt):
                if att:
                    scores_in(*att, 0)
                if prev:
                    finish(*prev)
                for u in range(1, 4):
                    if att:
                        scores_in(*att, u)
                    if att and u == 3:
                        spread_stats(*att)
                    if nxt:
                        qk_make(*nxt, u - 1)
                if att:
                    least(*att)
                if nxt:
                    qk_make(*nxt, 3)
                if att:
                    least_back(*att)
                if not nxt:
                    for k in range(K_EARLY):
                        y_low(k)
                if nxt:
                    qk_make(*nxt, 4)
                    qk_make(*nxt, 5)
                for u in range(4):
                    if att:
                        pt_copy(*att, u)
                    if nxt and u < 3:
                        v_make(*nxt, u)

            pair_dve(None, None, (0, 0))
            pair_dve(None, (0, 0), (1, 0))
            with dve.Fori(0, 3) as i:
                steps.loop(i, 2 * PAIR_STEPS)
                pair_dve((0, 2 * i), (1, 2 * i), (2, 2 * i))
                pair_dve((1, 2 * i), (2, 2 * i), (3, 2 * i))
            steps.leave(3)
            pair_dve((6, 0), (7, 0), None)
            finish(7, 0)
            for k in range(K_EARLY, KD):
                y_low(k)
            for k in range(KD):
                dve.wait_ge(proj_done, O_AOUT + k)
                dve.tensor_tensor(x[:, k], bank[k % 2][:, :], x[:, k], ALU.add).then_inc(evac[k % 2], 1)

        @block.tensor
        def _(pe):
            def sums(name, nk, b=B_SUM):
                q0, m, _ = NORMS[name]
                for k in range(nk):
                    pe.wait_ge(sq_ready, q0 + k + 1)
                    mm = pe.matmul(bank[b][:, :], ones[:, :], sq[:, (q0 + k) % 2], start=k == 0, stop=k == nk - 1)
                    mm.then_inc(sq_used, 1)
                pe.wait_ge(sq_used, q0 + nk)
                pe.sem_inc(sums_done, 1)

            def keep_warm(b, n):
                for _ in range(n):
                    pe.matmul(bank[b][:, 0:P], ones[:, :], ones[:, :],
                              start=True, stop=True)

            def bank_free(t, d=0):
                n = t // 2 - (1 if t > 15 and t % 2 else 0)
                if n > 0:
                    pe.wait_ge(evac[t % 2], n)

            pe.wait_ge(ones_in, 16)
            pe.wait_ge(vec_in, 48)
            pe.matmul(bank[4][0:16, 0:384], tabs[:, 0:16], onehot[:, 0:384], start=True, stop=True)
            pe.matmul(bank[5][0:16, 0:256], tabs[:, 16:32], onehot[:, 384:640], start=True, stop=True)
            pe.matmul(bank[5][0:16, 256:320], tabs[:, 32:48], onehot[:, 640:704], start=True, stop=True)\
              .then_inc(vec_done, 1)
            sums("n1", KD)
            for t in range(15):
                n, m = t // 2, t % 2
                if m == 0:
                    pe.wait_ge(lo_done, n + 1)
                bank_free(t)
                mm = products(pe, t % 2, *hblock(n % 2, KD, m), *hx, KD, ready=None if t else 0)
                mm.then_inc(proj_done, 1)

            def prep(s, body):
                if s >= 2:
                    pe.wait_ge(prep_taken[s % 2], s // 2)
                body(bank[B_PREP[s % 2]]).then_inc(prep_done, 1)

            def turn4(dst, src):
                for i in range(TT):
                    mm = pe.transpose(dst[:, i * P:(i + 1) * P], src[:, i * P:(i + 1) * P], ident[:, :])
                return mm

            def once(m, src):
                return lambda b: pe.matmul(b[:, :], ropem[:, m], src, start=True, stop=True)

            pe.wait_ge(attn_in, 16 * 11)
            pe.wait_ge(std_ready, 1)
            pe.wait_ge(evac[0], 8)
            pe.wait_ge(evac[1], 7)
            def hidden(r):
                v, c, hh = r // 4, r // 2 % 2, r % 2
                if r % 4 == 0:
                    pe.wait_ge(blocks_ready, 8 * v + 8)
                if 2 <= r < 6:
                    pe.wait_ge(cmp_in, 16)
                else:
                    pe.wait_ge(r32_in[r % 2], 16 if r < 2 else 32)
                for k in range(8):
                    mm = pe.matmul(bank[B_BU[v]][:, 62 * hh:62 * hh + 62], w_mlp(r)[:, k * P:(k + 1) * P],
                                   blk[:, v, 8 * c + k], start=c == 0 and hh == 0 and k == 0,
                                   stop=c == 1 and k == 7, skip_group_check=True)
                mm.then_inc(r32_used, 1)
                if r % 4 == 3:
                    pe.wait_ge(r32_used, r + 1)
                    pe.sem_inc(hid_done, 1)

            prep(0, once(0, z[:, T_KC]))
            prep(1, lambda b: turn4(b, z[:, T_VS]))
            prep(2, lambda b: turn4(b, z[:, T_VW]))
            prep(3, lambda b: turn4(b, z[:, T_ZG]))
            for j in range(4):
                prep(4 + j, once(0, z[:, T_Q + j]))
                hidden(j)
            for j in range(4):
                src = z[:, T_KS if j < 2 else T_KW]
                prep(8 + 2 * j, once(3 + j % 2, src))
                prep(9 + 2 * j, once(1 + j % 2, src))
                hidden(4 + j)

            def kc_body(b):
                for k in range(2):
                    mm = pe.matmul(b[:, 0:62], w_c2[:, k], hid[:, 0, k], start=k == 0, stop=k == 1)
                return mm

            def vc_body(b):
                for hh in range(2):
                    for k in range(2):
                        mm = pe.matmul(b[0:NCMP, 64 * hh:64 * hh + 64], hid[:, 1, k, 31 * hh:31 * hh + 31], w_v2[:, k],
                                       start=k == 0, stop=k == 1)
                return mm

            pe.wait_ge(hid_taken, 2)
            prep(16, kc_body)
            prep(17, vc_body)
            pe.wait_ge(prep_taken[0], 9)
            pe.wait_ge(prep_taken[1], 9)
            pe.wait_ge(roped, 9)

            ks_of, kw_of = (T_VS, T_VW), (T_KC, T_VC)

            def scores(u):
                h, i = u % 8, u // 8
                r = slice(64 * (h % 2), 64 * (h % 2) + 64)
                kv, w = h // 4, P * (i + 1)
                q = z[r, T_Q + h // 2, i * P:(i + 1) * P]
                if u:
                    pe.wait_ge(max_ready, 3 * u)
                keep_warm(0, 3)
                pe.matmul(bank[0][:, 0:w], q, z[r, ks_of[kv], 0:w], start=True, stop=True)
                pe.matmul(bank[1][:, 0:w], q, z[r, kw_of[kv], 0:w], start=True, stop=True)
                if u >= 2:
                    pe.wait_ge(combined, u - 1)
                pe.matmul(SC, q, kc_t[r, 31 * kv:31 * kv + 31], start=True, stop=True,
                          skip_group_check=True).then_inc(scores_done, 1)

            def turn(u):
                i = u // 8
                pe.wait_ge(exp_done, 3 * u + 3)
                if u:
                    pe.wait_ge(pt_dve, u)
                    pe.wait_ge(pt_act, 2 * u)
                for j in range(i + 1):
                    pe.transpose(bank[2][:, j * P:(j + 1) * P], s_sb[:, j * P:(j + 1) * P], ident[:, :])
                    mm = pe.transpose(bank[7][:, j * P:(j + 1) * P], s_sb[:, 512 + j * P:640 + j * P], ident[:, :])
                mm.then_inc(turned, 1)

            def turn_c(u):
                if u < 31:
                    pe.wait_ge(max_ready, 3 * u + 4)
                else:
                    pe.wait_ge(combined, u)
                pe.transpose(TC31, s_sb[:, 1024 + 32 * (u % 2):1024 + 32 * (u % 2) + NCMP], ident[:, :])\
                  .then_inc(turned_c, 1)

            def values(u):
                h, i = u % 8, u // 8
                kv = slice(64 * (h // 4), 64 * (h // 4) + 64)
                pe.wait_ge(pt_dve, u + 1)
                pe.wait_ge(pt_act, 2 * u + 2)
                if u:
                    pe.wait_ge(combined, u)
                pe.matmul(PV[:, 0:64], pt_c[0:NCMP, :], vc_t[0:NCMP, h // 4], start=True, stop=True,
                          skip_group_check=True)
                for b, pt in enumerate((pt_s, pt_w)):
                    for j in range(i + 1):
                        mm = pe.matmul(PV[:, 64 + 64 * b:128 + 64 * b], pt[:, j * P:(j + 1) * P], v_tok[:, b, j, kv],
                                       start=j == 0, stop=j == i, skip_group_check=True)
                mm.then_inc(pv_done, 1)

            def s5_b(t):
                zt, j = t // 4, t % 4
                r = slice(32 * j, 32 * j + 32)
                if t:
                    pe.wait_ge(bu_taken, 2 * t)
                for c in range(2):
                    mm = pe.matmul(bank[B_BU[c]][:, :], b_s5[r, c, zt], z[r, zt], start=True, stop=True)
                mm.then_inc(bu_done, 1)

            def s5_c(t):
                zt, j = t // 4, t % 4
                pe.wait_ge(back_done, 2 * t + 2)
                if j == 0 and zt:
                    pe.wait_ge(y_ready, zt)
                for n, (part, p) in enumerate(((0, 0), (2, 1), (2, 2), (1, 3))):
                    mm = pe.matmul(bank[B_Y][32 * j:32 * j + 32, :], c_s5[:, part, t], pq[:, 4 + p],
                                   start=n == 0, stop=n == 3, skip_group_check=True)
                mm.then_inc(cmul_done, 1)

            s5_b(0)
            for u in range(33):
                if u:
                    turn(u - 1)
                if u < 32:
                    scores(u)
                if u:
                    turn_c(u - 1)
                if u % 2 and u >= 3:
                    s5_c((u - 3) // 2)
                if u % 2 == 0 and 0 < u < 32:
                    s5_b(u // 2)
                if u:
                    values(u - 1)
            s5_c(15)

            pe.wait_ge(onorm, 4)
            pe.wait_ge(y_ready, 4)
            for m in range(4):
                for i in range(TT):
                    mm = pe.transpose(bank[4 + m][:, i * P:(i + 1) * P], o_tok[:, i, m * P:(m + 1) * P], ident[:, :])
                mm.then_inc(oturned, 1)
            pe.wait_ge(lo_done, N_GLU + 1)
            pe.wait_ge(yl_ready, 4)
            for m in range(4):
                bank_free(O_GLU + m)
                mm = products(pe, m % 2, *hblock(N_GLU % 2, 4, m), lambda k: y_hi[:, k], lambda k: y_lo[:, k], 4)
                mm.then_inc(proj_done, 1)
            sums("ssm", 4)
            for m in range(KD):
                n = N_O + m // 2
                if m % 2 == 0:
                    pe.wait_ge(lo_done, n + 1)
                bank_free(O_O + m)
                mm = products(pe, m % 2, *hblock(n % 2, KD, m % 2), *hx, KD, ready=None if m else 8)
                mm.then_inc(proj_done, 1)

            sums("n2", KD)
            with pe.Fori(0, FT // 2) as i:
                for j in range(2):
                    pe.wait_ge(lo_done, 2 * i + (N_UP + j + 1))
                    for m in range(2):
                        pe.wait_ge(evac[m], 2 * i + emptied(O_UP + 2 * j + m))
                        products(pe, m, *hblock((N_UP + j) % 2, KD, m), *hx, KD,
                                 ready=None if j or m else 16).then_inc(proj_done, 1)
            pe.wait_ge(al_ready, FT)
            with pe.Fori(0, 4) as i:
                for j in range(2):
                    for half in range(2):
                        n = N_DOWN + 2 * j + half
                        pe.wait_ge(lo_done, 4 * i + (n + 1))
                        if half == 0:
                            pe.wait_ge(evac[j], i + emptied(O_DOWN + j))
                        k0 = NB_DOWN * half
                        mm = products(pe, j, *hblock(n % 2, NB_DOWN, 0), lambda k: act_hi[:, k0 + k],
                                      lambda k: act_lo[:, k0 + k], NB_DOWN, half == 0, half == 1)
                        mm.then_inc(half_used if half == 0 else proj_done, 1)
            sums("nf", KD)
            sums("conv", KD)
            with pe.Fori(0, CT) as i:
                for j in range(2):
                    pe.wait_ge(lo_done, 2 * i + (N_CIN + j + 1))
                    for m in range(2):
                        pe.wait_ge(evac[m], 2 * i + emptied(O_CIN + 2 * j + m))
                        products(pe, m, *hblock((N_CIN + j) % 2, KD, m), *hx, KD,
                                 ready=None if j or m else 24).then_inc(proj_done, 1)
            pe.wait_ge(ycl_ready, 1)
            with pe.Fori(0, 4) as i:
                for j in range(2):
                    n = N_COUT + j
                    pe.wait_ge(lo_done, 2 * i + (n + 1))
                    pe.wait_ge(evac[j], i + emptied(O_COUT + j))
                    products(pe, j, *hblock(n % 2, CT, 0), lambda k: yc_hi[:, k], lambda k: yc_lo[:, k], CT)\
                        .then_inc(proj_done, 1)
            sums("attn2", KD)

            def project(c, r, e, ready=None):
                n, t = N_AIN + 5 * c + e // 2, O_AIN + 10 * c + e
                if e % 2 == 0:
                    pe.wait_ge(lo_done, 5 * r + (n + 1))
                pe.wait_ge(evac[e % 2], 5 * r + emptied(t))
                products(pe, e % 2, *hblock(n % 2, KD, e % 2), *hx, KD, ready=ready).then_inc(proj_done, 1)

            def head_sums(c, r, e):
                nth = 6 * c + e
                pe.wait_ge(d_sq, 6 * r + (nth + 1))
                if nth:
                    pe.wait_ge(d_std, 6 * r + nth)
                pe.matmul(bank[2][:, :], head_ones, sq[:, e % 2], start=True, stop=True).then_inc(d_sum, 1)

            def pair_scores(c, r, u):
                if u:
                    pe.wait_ge(d_max, 4 * r + (4 * c + u))
                for g, h, i, s0, n in unit_slots(u):
                    rows = slice(64 * h, 64 * h + 64)
                    q, k = qk[rows, c % 2, 2 * g], qk[rows, c % 2, 2 * g + 1]
                    k1 = P * (i + 1)
                    mm = pe.matmul(bank[4 + s0 // 4][:, P * (s0 % 4):P * (s0 % 4 + n)], q[:, P * i:P * i + P],
                                   k[:, k1 - P * n:k1], start=True, stop=True)
                mm.then_inc(d_scores, 1)

            def to_natural(c, r):
                pe.wait_ge(d_spread, 2 * r + (2 * c + 2))
                pe.wait_ge(d_vset, 3 * r + (3 * c + 3))
                for g in range(2):
                    for j in range(4):
                        mm = pe.matmul(bank[3][:, 8 * g:8 * g + 8], perm_f[:, g, j],
                                       cw[:, 32 * g + 8 * j:32 * g + 8 * j + 8], start=j == 0, stop=j == 3)
                mm.then_inc(d_natural, 1)

            def to_groups(c, r):
                pe.wait_ge(d_min, r + (c + 1))
                for g in range(2):
                    for j in range(4):
                        mm = pe.matmul(bank[3][:, 64 + 32 * g + 8 * j:72 + 32 * g + 8 * j], perm_b[:, g, j],
                                       cw[:, 88:96], start=True, stop=True)
                mm.then_inc(d_back, 1)

            def pair_turn(c, r, u):
                pe.wait_ge(d_exp, 4 * r + (4 * c + u + 1))
                if u:
                    pe.wait_ge(d_pt, 4 * r + (4 * c + u))
                for g, h, i, s0, n in unit_slots(u):
                    for s_ in range(s0, s0 + n):
                        mm = pe.transpose(bank[4 + s_ // 4][:, P * (s_ % 4):P * (s_ % 4) + P],
                                          sd_sb[:, u, P * s_:P * s_ + P], ident[:, :])
                mm.then_inc(d_turned, 1)

            def pair_values(c, r, u):
                pe.wait_ge(d_pt, 4 * r + (4 * c + u + 1))
                if u == 0:
                    pe.wait_ge(d_vset, 3 * r + (3 * c + 3))
                if u < 2:
                    for j in range(TT):
                        w = min(2 * P, L - P * j)
                        v = vv[:, c % 2, j, u:u + 2].rearrange("p a f -> p (a f)")
                        mm = pe.matmul(bank[6 + u][:, P * j:P * j + w], v,
                                       sd_sb[:, u, P * (2 * j + 1):P * (2 * j + 1) + w], start=j == 0,
                                       stop=False, skip_group_check=True)
                    mm.then_inc(d_pv, 1)
                    return
                for g, h, i, s0, n in unit_slots(u):
                    acc = bank[6 + h][:, :]
                    if g == 1:
                        o = acc.rearrange("p (l r) -> p r l", r=4)[:, i]
                    else:
                        o = acc.rearrange("p (l r) -> p r l", r=16)[:, 4 * i:4 * i + 4]
                    v = vv[:, c % 2, TT * g + i, h:h + 2].rearrange("p a f -> p (a f)")
                    mm = pe.matmul(o, v, sd_sb[:, u, P * s0:P * s0 + P], start=False,
                                   stop=g == 2 and i == 3, skip_group_check=True)
                mm.then_inc(d_pv, 1)

            def turn_v(c, r, g):
                pe.wait_ge(evac[g % 2], 5 * r + (emptied(O_AIN + 10 * c + 6 + g) + 1))
                if 3 * c + g:
                    pe.wait_ge(d_vset, 3 * r + (3 * c + g))
                if g == 0 and c:
                    pe.wait_ge(d_mperm, r + c)
                for i in range(TT):
                    mm = pe.transpose(bank[3][:, P * i:P * i + P], hf[:, 0, P * i:P * i + P], ident[:, :])
                mm.then_inc(d_vturned, 1)

            def pair_pe(att, nxt):
                for e in range(10):
                    if att and e < 4:
                        pair_scores(*att, e)
                    if att and e >= 8:
                        pair_turn(*att, e - 8)
                        turn_v(*nxt, e - 8) if nxt and e == 8 else None
                        if e == 9:
                            pair_values(*att, 0)
                            if nxt:
                                turn_v(*nxt, 1)
                    elif nxt and e >= 8:
                        turn_v(*nxt, e - 8)
                    if nxt:
                        project(*nxt, e, None if att or e else 32)
                        if not att and e == 0:
                            pe.wait_ge(perm_in, 64)
                            pe.wait_ge(d_ones, 2)
                        if 1 <= e <= 6:
                            head_sums(*nxt, e - 1)
                    if att and e == 4:
                        to_natural(*att)
                    if att and e == 5:
                        to_groups(*att)
                    if not nxt and e == 5:
                        pe.wait_ge(lo_done, N_AOUT + 1)
                        for m in range(2):
                            pe.wait_ge(evac[m], emptied(O_AOUT + m))
                            products(pe, m, *hblock(N_AOUT % 2, KD, m), *hx, K_EARLY, last=False,
                                     ready=None if m else 40)
                if att:
                    pair_turn(*att, 2)
                    pair_values(*att, 1)
                if nxt:
                    turn_v(*nxt, 2)
                if att:
                    pair_turn(*att, 3)
                    pair_values(*att, 2)
                    pair_values(*att, 3)

            pair_pe(None, (0, 0))
            with pe.Fori(0, 3) as i:
                pair_pe((0, 2 * i), (1, 2 * i))
                pair_pe((1, 2 * i), (2, 2 * i))
            pair_pe((6, 0), (7, 0))
            pair_pe((7, 0), None)
            for k in range(KD):
                n = N_AOUT + k // 2
                if k % 2 == 0:
                    pe.wait_ge(lo_done, n + 1)
                k0 = K_EARLY if k < 2 else 0
                if k >= 2:
                    pe.wait_ge(evac[k % 2], emptied(O_AOUT + k))
                left = [lambda j, f=f: f(k0 + j) for f in (*hblock(n % 2, KD, k % 2), *hx)]
                products(pe, k % 2, *left, KD - k0, first=k >= 2, ready=None if k else 40 + K_EARLY).then_inc(proj_done, 1)


def row_tiles(w):
    k, n = w.shape
    return w.reshape(k // P, P, n).transpose(1, 0, 2)


def chunks(w, cols_per):
    k, n = w.shape
    c = n // cols_per
    v = w.reshape(k // P, P, c, cols_per // P, P)
    return v.transpose(2, 1, 3, 0, 4).reshape(c, P, -1)


def col(v):
    return v.reshape(-1, P).T


def constants():
    c = {"ones": np.ones((P, P), np.float32), "ident": np.eye(P, dtype=np.float32)}
    rot = np.zeros((P, P), np.float32)
    for h in (0, 64):
        for j in range(32):
            rot[h + j, h + 32 + j] = -1.0
            rot[h + 32 + j, h + j] = 1.0
    dup = [np.zeros((P, P), np.float32) for _ in range(2)]
    for kv in range(2):
        for p in range(P):
            dup[kv][p, 64 * kv + p % 64] = 1.0
    c["ropem"] = np.stack([m.T for m in (rot, dup[0], dup[1], rot @ dup[0], rot @ dup[1])], axis=1)
    inv = np.power(np.float32(10000.0), -np.arange(32, dtype=np.float32) * np.float32(2.0) / np.float32(64))
    ang = np.arange(L, dtype=np.float32)[None, :] * inv.astype(np.float32)[np.arange(P) % 32][:, None]
    c["rope_cs"] = np.stack([np.cos(ang), np.sin(ang)], axis=1).astype(np.float32)
    q = np.arange(P)
    m = np.zeros((P, 512), np.float32)
    m[:, 384:] = np.where(q[None, :] <= q[:, None], 0.0, NEG)
    c["mask"] = m
    t = (np.arange(TT)[None, :] * P + q[:, None])[:, :, None]
    c["cmask"] = np.where(np.arange(NCMP)[None, None, :] * 16 + 31 <= t, 0.0, NEG).astype(np.float32)
    oh, vm = np.zeros((32, VTOT), np.float32), np.full((16, VTOT), NEG, np.float32)
    for g, (window, dil) in enumerate(GROUPS):
        far = 31 if g == 2 else 127 if g == 1 else 128
        zero = (255, 127, 31)[g]
        for s in range(far + 1):
            d = np.int32(s * dil)
            big = 16 + int(np.float32(np.log(np.float32(max(d, 1)) / np.float32(16)))
                           / np.float32(np.log(128.0)) * np.float32(16))
            oh[d if d < 16 else min(big, 31), VOFF[g] + zero - s] = 1.0
            vm[:, VOFF[g] + zero - s] = 0.0
    c["onehot"], c["vmask"] = oh, vm
    c["neg"] = np.full((P, P), NEG, np.float32)
    f = np.zeros((P, 2, 4, P), np.float32)
    pm = np.zeros((P, 2, 4), np.float32)
    for p in range(P):
        for i in range(4):
            for g, token in enumerate((4 * p + i, 16 * (p % 32) + 4 * i + p // 32)):
                f[p, g, i, token % P] = 1.0
                pm[p, g, token // P] = 1.0
    c["perm_f"], c["perm_b"], c["pmask"] = f, f.transpose(3, 1, 2, 0), pm
    c["head_ones"] = np.kron(np.eye(2), np.ones((64, 64))).astype(np.float32)
    return c


def kernel(x, c, norm1_g, norm2_g, normf_g, w_ada, b_ada, w_in, pe_k, pe_v, w_ck1, w_ck2, w_cv1, w_cv2,
           lam_re, lam_im, log_step, b_re, b_im, c_re, c_im, d_skip, w_glu, b_glu, attn_norm_g,
           ssm_norm_g, w_o, w_up, conv_w, conv_b, w_down, conv_norm_2, conv_w_in_2, conv_w_2,
           conv_w_out_2, attn_norm_2, attn_w_in_2, attn_q_gain_2, attn_k_gain_2, attn_w_out_2,
           rel_bias_2):
    import concourse.bacc as bacc
    from concourse.bass_utils import run_bass_kernel_spmd

    a = constants()
    a["x"] = row_tiles(x[0].T)
    a["c"] = c
    a["b_ada"] = col(b_ada[0])
    a["gains"] = np.concatenate([col(v) for v in (
        norm1_g[0], norm2_g[0], normf_g, conv_norm_2[0], attn_norm_2[0],
        np.concatenate([attn_norm_g[0], ssm_norm_g[0]]), b_glu[0], d_skip[0].reshape(-1))], axis=1)
    w = w_in[0]
    at = np.cumsum([0, 512, 128, 128, 128, 128, 128, 128, 24, 512])
    q_, kc, vc, ks, vs, kw, vw, zg, zs = (w[:, at[i]:at[i + 1]] for i in range(9))
    w_in_c = np.concatenate([zs, kc, vc, q_, ks, vs, kw, vw, zg, np.zeros((D, 232), np.float32)], axis=1)
    up = w_up[0].reshape(D, 2, FT, P).transpose(0, 2, 1, 3).reshape(D, 2 * FT * P)
    a["w_a"] = np.concatenate([chunks(w_in_c, 256), chunks(w_glu[0], 512), chunks(w_o[0], 256),
                               chunks(up, 256)])
    a["w_d"] = np.concatenate([chunks(w_down[0][h * 1408:(h + 1) * 1408], P)[:, None] for h in range(2)], axis=1)\
        .reshape(16, P, NB_DOWN * P)
    order4 = conv_w_in_2[0].reshape(D, 4, CT, P)[:, [1, 2, 0, 3]].transpose(0, 2, 1, 3).reshape(D, 4 * CT * P)
    wq = attn_w_in_2[0][:, :9216].reshape(D, 3, 3, NPAIR, P)
    wz = attn_w_in_2[0][:, 9216:].reshape(D, NPAIR, P)
    pairs = np.stack([wq[:, 0, 0], wq[:, 0, 1], wq[:, 1, 0], wq[:, 1, 1], wq[:, 2, 0], wq[:, 2, 1],
                      wq[:, 0, 2], wq[:, 1, 2], wq[:, 2, 2], wz], axis=2).reshape(D, NPAIR * 10 * P)
    a["w_b"] = np.concatenate([chunks(order4, 256), chunks(conv_w_out_2[0], P), chunks(pairs, 256),
                               chunks(attn_w_out_2[0], 256)])
    a["tabs"] = rel_bias_2
    ck = [chunks(m[0][1024 * i:1024 * i + 1024], P) for m in (w_ck1, w_cv1) for i in range(2)]
    a["w32"] = np.concatenate(ck)
    a["w_ada"] = w_ada[0].T.reshape(48, P, D)
    a["pe_t"] = np.stack([np.tile(pe[0].T, (2, 1)) for pe in (pe_k, pe_v)], axis=1)
    a["w_c2"] = row_tiles(np.concatenate([w_ck2[0]] * 2, axis=1))
    a["w_v2"] = row_tiles(w_cv2[0])
    a["s5c"] = np.stack([lam_re[0].reshape(16, P).T, lam_im[0].reshape(16, P).T,
                         np.repeat(log_step[0], 64).reshape(16, P).T], axis=1)
    bs = np.zeros((P, 2, 4, P), np.float32)
    for i, b in enumerate((b_re, b_im)):
        for g in range(32):
            zt, r = g // 8, 16 * (g % 8)
            bs[r:r + 16, i, zt, 64 * (g % 2):64 * (g % 2) + 64] = b[0, g].T
    a["b_s5"] = bs
    a["c_s5"] = np.stack([m[0].transpose(0, 2, 1).reshape(16, P, 16).transpose(1, 0, 2) for m in (c_re, c_im)], axis=1)
    a["conv_wb"] = np.stack([col(conv_w[0, i]) for i in range(3)] + [col(conv_b[0])], axis=1)
    a["conv2_w"] = np.stack([col(conv_w_2[0, i]) for i in range(3)], axis=1)
    a["qk_gain"] = np.stack([np.tile(g[0, i], 2) for i in range(3) for g in (attn_q_gain_2, attn_k_gain_2)], axis=1)

    nc = bacc.Bacc("TRN2", target_bir_lowering=False, num_devices=1)
    arrays, aps = {}, {}
    for name, v in a.items():
        v = np.ascontiguousarray(v)
        arrays["in_" + name] = v
        aps[name] = nc.dram_tensor("in_" + name, v.shape, F32, kind="ExternalInput").ap()
    out = nc.dram_tensor("out_x", (P, KD, L), F32, kind="ExternalOutput").ap()
    build(nc, aps, out)
    r = run_bass_kernel_spmd(nc, [arrays], core_ids=[0]).results[0]["out_x"]
    return np.ascontiguousarray(r.transpose(1, 0, 2).reshape(D, L).T)[None]
```
